# Optimizing a Trainium2 kernel written in Bass

```python
import math
import jax, jax.numpy as jnp
from jax import lax
import numpy as np

D_MODEL = 1024
BATCH = 1
SEQ = 512
DEPTH = 1

D_RWKV = D_MODEL
RWKV_HEAD = 64
RWKV_HEADS = D_RWKV // RWKV_HEAD
LORA_W = 64
LORA_A = 64
LORA_G = 128
DECAY_SCALE = math.exp(-0.5)
GN_EPS = 64e-5
D_CONV = D_MODEL
CONV_WIDTH = 31
N_EXPERTS = 64
TOP_K = 8
N_GROUPS = 8
TOPK_GROUPS = 4
D_EXPERT = 256
D_SHARED = 256
ROUTED_SCALE = 2.5
MOE_BLOCK = 1024
N_BRANCH = 2
LN_EPS = 1e-5
RW_SPLITS = (D_RWKV, D_RWKV, D_RWKV, LORA_W, LORA_W, LORA_A, LORA_A, LORA_G)
RW_COLS = sum(RW_SPLITS)
P_TOTAL = RW_COLS + 2 * D_CONV + N_BRANCH * D_MODEL

kernel_name = "hybrid_rwkv7_conformer_moe_encoder"

def layer_norm(x, w=None, b=None, eps=LN_EPS):
    xf = x.astype(jnp.float32)
    mu = jnp.mean(xf, -1, keepdims=True)
    var = jnp.mean(jnp.square(xf - mu), -1, keepdims=True)
    y = (xf - mu) * lax.rsqrt(var + eps)
    if w is not None:
        y = y * w.astype(jnp.float32) + b.astype(jnp.float32)
    return y.astype(x.dtype)

def centred_shift(p, mu_prev, mu_next):
    p_prev = jnp.pad(p, ((0, 0), (1, 0), (0, 0)))[:, :-1]
    p_next = jnp.pad(p, ((0, 0), (0, 1), (0, 0)))[:, 1:]
    return p + mu_prev * (p_prev - p) + mu_next * (p_next - p)

def wkv7_scan(r, w, k, v, kk, a, reverse):
    B, S, H, N = r.shape
    xs = tuple(jnp.swapaxes(t, 0, 1) for t in (r, w, k, v, kk, a))

    def step(state, inp):
        r_t, w_t, k_t, v_t, kk_t, a_t = inp
        s_kk = jnp.einsum('bhvk,bhk->bhv', state, kk_t)
        new = (state * w_t[:, :, None, :]
               - s_kk[..., None] * (kk_t * a_t)[:, :, None, :]
               + v_t[..., None] * k_t[:, :, None, :])
        read = state if reverse else new
        return new, jnp.einsum('bhvk,bhk->bhv', read, r_t)

    _, ys = lax.scan(step, jnp.zeros((B, H, N, N), jnp.float32), xs, reverse=reverse)
    return jnp.swapaxes(ys, 0, 1)

def rwkv7_branch(p_rw, w0, w_up, a0, a_up, g_up, k_k, k_a, r_k, lnx_w, lnx_b):
    B, S, _ = p_rw.shape
    H, N = RWKV_HEADS, RWKV_HEAD
    f32 = jnp.float32
    idx = np.cumsum(RW_SPLITS)[:-1].tolist()
    r, k, v, wl_f, wl_b, al_f, al_b, gl = jnp.split(p_rw.astype(f32), idx, axis=-1)
    heads = lambda t: t.reshape(B, S, H, N)
    g = jax.nn.sigmoid(gl) @ g_up.astype(f32)
    kk = heads(k * k_k.astype(f32))
    kk = kk / jnp.maximum(jnp.linalg.norm(kk, axis=-1, keepdims=True), 1e-12)
    r_h, v_h = heads(r), heads(v)
    outs = []
    ks = []
    for d, (wl, al) in enumerate(((wl_f, al_f), (wl_b, al_b))):
        decay = jnp.exp(-DECAY_SCALE * jax.nn.sigmoid(w0[d].astype(f32) + jnp.tanh(wl) @ w_up[d].astype(f32)))
        a = jax.nn.sigmoid(a0[d].astype(f32) + al @ a_up[d].astype(f32))
        k_d = k * (1.0 + (a - 1.0) * k_a.astype(f32))
        ks.append(k_d)
        outs.append(wkv7_scan(r_h, heads(decay), heads(k_d), v_h, kk, heads(a), reverse=(d == 1)))
    y = outs[0] + outs[1]
    mu = jnp.mean(y, -1, keepdims=True)
    var = jnp.mean(jnp.square(y - mu), -1, keepdims=True)
    y = ((y - mu) * lax.rsqrt(var + GN_EPS)).reshape(B, S, D_RWKV) * lnx_w.astype(f32) + lnx_b.astype(f32)
    bonus = jnp.sum(r_h * heads(ks[0]) * r_k.astype(f32), -1, keepdims=True) * v_h
    return (y + bonus.reshape(B, S, D_RWKV)) * g

def conformer_conv_branch(p_conv, conv_w, conv_b, cnorm_w, cnorm_b, cpw_w, cpw_b):
    h_a, h_b = jnp.split(p_conv, 2, axis=-1)
    h = h_a * jax.nn.sigmoid(h_b)
    pad = CONV_WIDTH // 2
    h = lax.conv_general_dilated(h, conv_w[:, None, :].astype(h.dtype), window_strides=(1,),
                                 padding=[(pad, pad)], dimension_numbers=('NWC', 'WIO', 'NWC'),
                                 feature_group_count=D_CONV) + conv_b
    h = jax.nn.silu(layer_norm(h, cnorm_w, cnorm_b))
    return h @ cpw_w + cpw_b

def token_mix(u, w_in, shift_mu, w0, w_up, a0, a_up, g_up, k_k, k_a, r_k, lnx_w, lnx_b,
              conv_w, conv_b, cnorm_w, cnorm_b, cpw_w, cpw_b, gate_b, w_o):
    proj = u @ w_in
    p_rw, p_conv, p_gate = jnp.split(proj, [RW_COLS, RW_COLS + 2 * D_CONV], axis=-1)
    p_rw = centred_shift(p_rw, shift_mu[0], shift_mu[1])
    y_a = rwkv7_branch(p_rw, w0, w_up, a0, a_up, g_up, k_k, k_a, r_k, lnx_w, lnx_b).astype(u.dtype)
    y_b = conformer_conv_branch(p_conv, conv_w, conv_b, cnorm_w, cnorm_b, cpw_w, cpw_b)
    g_a, g_b = jnp.split(jax.nn.sigmoid(p_gate + gate_b.reshape(-1)), N_BRANCH, axis=-1)
    return (g_a * y_a + g_b * y_b) @ w_o

def moe_ffn(u, router_w, router_b, exp_gate, exp_up, exp_down, sh_gate, sh_up, sh_down):
    B, S, D = u.shape
    T = B * S
    f32 = jnp.float32
    ut = u.reshape(T, D)
    scores = jax.nn.sigmoid(ut.astype(f32) @ router_w.astype(f32))
    sel = scores + router_b.astype(f32)
    grp = sel.reshape(T, N_GROUPS, N_EXPERTS // N_GROUPS)
    grp_score = jnp.sum(lax.top_k(grp, 2)[0], -1)
    _, gidx = lax.top_k(grp_score, TOPK_GROUPS)
    rows = jnp.arange(T)[:, None]
    gmask = jnp.zeros((T, N_GROUPS), bool).at[rows, gidx].set(True)
    emask = jnp.repeat(gmask, N_EXPERTS // N_GROUPS, axis=1)
    _, eidx = lax.top_k(jnp.where(emask, sel, -jnp.inf), TOP_K)
    w_sel = jnp.take_along_axis(scores, eidx, axis=1)
    w_sel = w_sel / jnp.sum(w_sel, -1, keepdims=True) * ROUTED_SCALE
    gate = jnp.zeros((T, N_EXPERTS), f32).at[rows, eidx].set(w_sel)
    blk = math.gcd(T, MOE_BLOCK)

    def expert_block(args):
        ub, gb = args
        h = jax.nn.silu(jnp.einsum('td,edf->tef', ub, exp_gate)) * jnp.einsum('td,edf->tef', ub, exp_up)
        h = h * gb[..., None].astype(h.dtype)
        return jnp.einsum('tef,efd->td', h, exp_down)

    routed = lax.map(expert_block, (ut.reshape(T // blk, blk, D), gate.reshape(T // blk, blk, N_EXPERTS)))
    shared = (jax.nn.silu(ut @ sh_gate) * (ut @ sh_up)) @ sh_down
    return (routed.reshape(T, D).astype(u.dtype) + shared).reshape(B, S, D)

def setup_inputs(seed: int = 0) -> dict:
    key = jax.random.key(seed)
    ks = iter(jax.random.split(key, 48))
    L, D, E, F, Fs = DEPTH, D_MODEL, N_EXPERTS, D_EXPERT, D_SHARED
    beta = (8.0 * DEPTH) ** -0.25
    nrm = lambda shape, s: jax.random.normal(next(ks), shape, jnp.float32) * s
    uni = lambda shape, lo, hi: jax.random.uniform(next(ks), shape, jnp.float32, lo, hi)
    gain = lambda shape: 1.0 + nrm(shape, 0.05)
    return {
        "x": nrm((BATCH, SEQ, D), 1.0),
        "c": nrm((BATCH, D), 1.0),
        "ada_w": nrm((L, D, 6 * D), 0.5 * D ** -0.5),
        "ada_b": nrm((L, 6 * D), 0.02),
        "w_in": nrm((L, D, P_TOTAL), D ** -0.5),
        "shift_mu": uni((L, 2, RW_COLS), 0.0, 0.5),
        "w0": uni((L, 2, D_RWKV), -5.0, 1.0),
        "w_up": nrm((L, 2, LORA_W, D_RWKV), 0.1),
        "a0": nrm((L, 2, D_RWKV), 0.2),
        "a_up": nrm((L, 2, LORA_A, D_RWKV), 0.5 * LORA_A ** -0.5),
        "g_up": nrm((L, LORA_G, D_RWKV), LORA_G ** -0.5),
        "k_k": 0.85 + nrm((L, D_RWKV), 0.05),
        "k_a": gain((L, D_RWKV)),
        "r_k": nrm((L, RWKV_HEADS, RWKV_HEAD), 0.1),
        "lnx_w": gain((L, D_RWKV)),
        "lnx_b": nrm((L, D_RWKV), 0.02),
        "conv_w": nrm((L, CONV_WIDTH, D_CONV), CONV_WIDTH ** -0.5),
        "conv_b": nrm((L, D_CONV), 0.02),
        "cnorm_w": gain((L, D_CONV)),
        "cnorm_b": nrm((L, D_CONV), 0.02),
        "cpw_w": nrm((L, D_CONV, D), beta * D_CONV ** -0.5),
        "cpw_b": nrm((L, D), 0.02),
        "gate_b": nrm((L, N_BRANCH, D), 0.1),
        "w_o": nrm((L, D, D), beta * D ** -0.5),
        "ln1_w": gain((L, D)),
        "ln1_b": nrm((L, D), 0.02),
        "router_w": nrm((L, D, E), D ** -0.5),
        "router_b": nrm((L, E), 0.01),
        "exp_gate": nrm((L, E, D, F), D ** -0.5),
        "exp_up": nrm((L, E, D, F), D ** -0.5),
        "exp_down": nrm((L, E, F, D), beta * F ** -0.5),
        "sh_gate": nrm((L, D, Fs), D ** -0.5),
        "sh_up": nrm((L, D, Fs), D ** -0.5),
        "sh_down": nrm((L, Fs, D), beta * Fs ** -0.5),
        "ln2_w": gain((L, D)),
        "ln2_b": nrm((L, D), 0.02),
    }

def reference(x, c, ada_w, ada_b, w_in, shift_mu, w0, w_up, a0, a_up, g_up, k_k, k_a, r_k,
              lnx_w, lnx_b, conv_w, conv_b, cnorm_w, cnorm_b, cpw_w, cpw_b, gate_b, w_o,
              ln1_w, ln1_b, router_w, router_b, exp_gate, exp_up, exp_down,
              sh_gate, sh_up, sh_down, ln2_w, ln2_b):
    alpha = (2.0 * DEPTH) ** 0.25
    for l in range(DEPTH):
        mod = jax.nn.silu(c) @ ada_w[l] + ada_b[l]
        sh1, sc1, gt1, sh2, sc2, gt2 = jnp.split(mod[:, None, :], 6, axis=-1)
        u1 = layer_norm(x) * (1.0 + sc1) + sh1
        mix = token_mix(u1, w_in[l], shift_mu[l], w0[l], w_up[l], a0[l], a_up[l], g_up[l],
                        k_k[l], k_a[l], r_k[l], lnx_w[l], lnx_b[l], conv_w[l], conv_b[l],
                        cnorm_w[l], cnorm_b[l], cpw_w[l], cpw_b[l], gate_b[l], w_o[l])
        x = layer_norm(alpha * x + (1.0 + gt1) * mix, ln1_w[l], ln1_b[l])
        u2 = layer_norm(x) * (1.0 + sc2) + sh2
        ffn = moe_ffn(u2, router_w[l], router_b[l], exp_gate[l], exp_up[l], exp_down[l],
                      sh_gate[l], sh_up[l], sh_down[l])
        x = layer_norm(alpha * x + (1.0 + gt2) * ffn, ln2_w[l], ln2_b[l])
    return x


_drawn_inputs = setup_inputs


def setup_inputs(seed=0):
    import zlib

    import numpy as np

    out = dict(_drawn_inputs(seed))
    spreads = {}
    factors = {'lnx_b': 2.804, 'conv_b': 2.867, 'cnorm_b': 3.016, 'ln2_b': 2.943, 'cnorm_w': 2.823}
    for name, (base, spread) in spreads.items():
        noise = np.random.default_rng([zlib.crc32(name.encode()), seed]).standard_normal(out[name].shape)
        drawn = base * np.exp(spread * noise) if base else spread * noise
        out[name] = __import__('jax').numpy.asarray(drawn.astype(out[name].dtype))
    for name, factor in factors.items():
        out[name] = (out[name] * factor).astype(out[name].dtype)
    return out
```

```python
from contextlib import ExitStack
import math
import concourse.bass as bass
from concourse import mybir

F32 = mybir.dt.float32
I32 = mybir.dt.int32
ALU = mybir.AluOpType
ACT = mybir.ActivationFunctionType
AX_X = mybir.AxisListType.X

P = 128
T = 512
D = 1024
KC = D // P
TT = T // P
HALF = 3 * D
CW = 31
PAD = CW // 2
LN_EPS = 1e-5
RW_COLS = 3 * D + 4 * 64 + 128
MODS = 6


def hold(pool, sem, value, held):
    pool.wait_ge(sem, value)
    pool.sem_inc(held, 1)


class Chain:

    def __init__(self, eng, sem, held=None):
        self.eng, self.sem, self.n, self.trip, self.held = eng, sem, 0, 0, held

    def enter(self, trip, length):
        self.trip, self.length, self.start = trip * length, length, self.n

    def leave(self, trips):
        assert self.n - self.start == self.length, (self.n - self.start, self.length)
        self.n, self.trip = self.start + self.length * trips, 0

    def mark(self, ins):
        ins.then_inc(self.sem, 1)
        self.n += 1

    def wait(self):
        if self.held is None:
            self.eng.wait_ge(self.sem, self.trip + self.n)
        else:
            hold(self.eng, self.sem, self.trip + self.n, self.held)

    def __call__(self, ins):
        self.mark(ins)
        self.wait()


class Scope:

    def __init__(self, nc, ctx, stage):
        self.nc, self.ctx, self.stage, self.sems = nc, ctx, stage, []
        ctx.callback(self.close)

    def close(self):
        self.nc.clear_and_free_semaphores(self.sems)
        self.nc.all_engine_barrier()

    def sb(self, name, shape, dt=F32):
        return self.ctx.enter_context(self.nc.sbuf_tensor(f"{self.stage}_{name}", list(shape), dt))

    def ps(self, name, shape=(P, 512)):
        return self.ctx.enter_context(self.nc.psum_tensor(f"{self.stage}_{name}", list(shape), F32))

    def sem(self, name):
        self.sems.append(self.nc.alloc_semaphore(f"{self.stage}_{name}"))
        return self.sems[-1]


def columns(vec, n=KC):
    return vec.rearrange("(k p) -> p k", p=P)


def modulation_and_norm(nc, g, x, c, ada_w, ada_b):
    with ExitStack() as ctx:
        s = Scope(nc, ctx, "mod")
        NB = 4
        aw = s.sb("aw", [P, NB, HALF])
        xs = s.sb("x", [P, TT, D])
        xn = s.sb("xn", [P, TT, D])
        ccol = s.sb("ccol", [P, KC])
        csil = s.sb("csil", [P, KC])
        abrow = s.sb("abrow", [1, MODS * D])
        modrow = s.sb("modrow", [1, MODS * D])
        sh = s.sb("sh", [P, KC])
        sc = s.sb("sc", [P, KC])
        stats = s.sb("stats", [P, TT, 2, 6])
        mv = s.sb("mv", [P, TT, 2])
        std = s.sb("std", [P, TT])
        rstd = s.sb("rstd", [P, TT])
        acc = [s.ps(f"acc{i}") for i in range(6)]
        tp = [s.ps(f"tp{i}") for i in range(2)]
        x_in, c_in, b_in = s.sem("x_in"), s.sem("c_in"), s.sem("b_in")
        aw_in = [s.sem(f"aw_in{i}") for i in range(NB)]
        aw_used, silu_done, half_done, row_half, row_out, cols_in = (s.sem(n) for n in (
            "aw_used", "silu_done", "half_done", "row_half", "row_out", "cols_in"))
        var_done, std_done, xn_done, tp_done, tp_used, dve = (s.sem(n) for n in (
            "var_done", "std_done", "xn_done", "tp_done", "tp_used", "dve"))
        block = ctx.enter_context(nc.Block())

        @block.sync
        def _(sp):
            sp.dma_start(ccol[:], columns(c[0])).then_inc(c_in, 16)
            sp.dma_start(xs[:], x[0].rearrange("(n p) d -> p n d", p=P)).then_inc(x_in, 16)
            sp.dma_start(abrow[:], ada_b).then_inc(b_in, 16)
            for n in range(2 * KC):
                h, k = n // KC, n % KC
                if n >= NB:
                    sp.wait_ge(aw_used, n - NB + 1)
                sp.dma_start(aw[:, n % NB], ada_w[0, k * P:(k + 1) * P, h * HALF:(h + 1) * HALF]) \
                  .then_inc(aw_in[n % NB], 16)
            sp.wait_ge(row_half, 12)
            sp.dma_start(g["mod"], modrow[0:1, :]).then_inc(row_out, 16)
            sp.wait_ge(row_out, 16)
            sp.dma_start(sh[:], columns(g["mod"][0, 0:D])).then_inc(cols_in, 16)
            sp.dma_start(sc[:], columns(g["mod"][0, D:2 * D])).then_inc(cols_in, 16)

        @block.gpsimd
        def _(pool):
            pass

        @block.scalar
        def _(act):
            act.wait_ge(c_in, 16)
            nc.scalar.activation(csil[:], ccol[:], ACT.Silu).then_inc(silu_done, 1)
            act.wait_ge(var_done, TT)
            nc.scalar.activation(std[:], mv[:, :, 1], ACT.Sqrt, bias=g["eps"][:, 0:1]).then_inc(std_done, 1)

        @block.tensor
        def _(pe):
            pe.wait_ge(silu_done, 1)
            for n in range(2 * KC):
                h, k = n // KC, n % KC
                pe.wait_ge(aw_in[n % NB], 16 * (n // NB + 1))
                if n == KC:
                    pe.wait_ge(row_half, 6)
                for j in range(6):
                    ins = nc.tensor.matmul(acc[j][0:1, :], csil[:, k:k + 1], aw[:, n % NB, j * 512:(j + 1) * 512],
                                           start=(k == 0), stop=(k == KC - 1))
                ins.then_inc(aw_used, 1)
            pe.wait_ge(xn_done, TT)
            for k in range(KC):
                if k >= 2:
                    pe.wait_ge(tp_used, k - 1)
                for t in range(TT):
                    ins = nc.tensor.transpose(tp[k % 2][:, t * P:(t + 1) * P], xn[:, t, k * P:(k + 1) * P], g["ident"][:])
                ins.then_inc(tp_done, 1)

        @block.vector
        def _(v):
            ch = Chain(v, dve)
            v.wait_ge(x_in, 16)
            for t in range(TT):
                for h in range(2):
                    ch.mark(nc.vector.bn_stats(stats[:, t, h, :], xs[:, t, h * 512:(h + 1) * 512]))
            ch.wait()
            for t in range(TT):
                nc.vector.bn_aggr(mv[:, t, :], stats[:, t, :, :]).then_inc(var_done, 1)
            v.wait_ge(std_done, 1)
            ch(nc.vector.reciprocal(rstd[:], std[:]))
            for t in range(TT):
                nc.vector.tensor_scalar(xn[:, t, :], xs[:, t, :], mv[:, t, 0:1], rstd[:, t:t + 1],
                                        ALU.subtract, ALU.mult).then_inc(xn_done, 1)
            v.wait_ge(b_in, 16)
            for h in range(2):
                v.wait_ge(aw_used, (h + 1) * KC)
                for j in range(6):
                    o = h * HALF + j * 512
                    nc.vector.tensor_tensor(modrow[0:1, o:o + 512], acc[j][0:1, :], abrow[0:1, o:o + 512],
                                            ALU.add).then_inc(row_half, 1)
            v.wait_ge(cols_in, 32)
            ch(nc.vector.tensor_scalar(sc[:], sc[:], 1.0, None, ALU.add))
            for k in range(KC):
                v.wait_ge(tp_done, k + 1)
                nc.vector.tensor_scalar(g["u1T"][:, k, :], tp[k % 2][:], sc[:, k:k + 1], sh[:, k:k + 1],
                                        ALU.mult, ALU.add).then_inc(tp_used, 1)


RW_TILES = RW_COLS // P
TILE0 = {"ha": RW_TILES, "hb": RW_TILES + KC, "r": 0, "k": KC, "v": 2 * KC,
         "ga": RW_TILES + 2 * KC, "gb": RW_TILES + 3 * KC}
KINDS = list(TILE0)


def projections_and_conv(nc, g, w_in, shift_mu, conv_w, conv_b, cnorm_w, cnorm_b, cpw_w, cpw_b, gate_b):
    with ExitStack() as ctx:
        s = Scope(nc, ctx, "proj")
        NK = len(KINDS)
        w = s.sb("w", [P, NK, KC, P])
        mu = s.sb("mu", [P, 3, RW_TILES])
        cwT = s.sb("cwT", [P, KC, CW])
        cols = s.sb("cols", [P, 6, KC])
        sg = s.sb("sg", [P, T])
        hp = s.sb("hp", [P, T + 2 * PAD])
        hc = s.sb("hc", [P, KC, T])
        st = s.sb("st", [P, 5, T])
        sq = s.sb("sq", [P, 2, T])
        rs = s.sb("rs", [P, T])
        gb = s.sb("gb", [P, 2, T])
        yo = s.sb("yo", [P, 2, T])
        bank = [s.ps(f"bank{i}") for i in range(NK)]
        pstat = s.ps("pstat")
        w_in_sem = [s.sem(f"w{k}") for k in KINDS]
        params, dve, sg_done, h_used, base_done, out_ready, dv = (s.sem(n) for n in (
            "params", "dve", "sg_done", "h_used", "base_done", "out_ready", "dv"))
        held = s.sem("held")
        left = [s.sem(f"left{j}") for j in range(5)]
        tile_done = s.sem("tile_done")
        read = [s.sem(f"read_{k}") for k in KINDS]
        shifted = [s.sem(f"shifted{j}") for j in range(3)]
        gated = [s.sem(f"gated{j}") for j in range(2)]
        stored = [s.sem(f"stored{j}") for j in range(5)]
        mean_done, cent, sq_done, sq_used, var_done, std_done, nrm, silu, cpw_done, cpw_read, yb_done, gb_in, yb_out = (
            s.sem(n) for n in ("mean_done", "cent", "sq_done", "sq_used", "var_done", "std_done", "nrm", "silu",
                               "cpw_done", "cpw_read", "yb_done", "gb_in", "yb_out"))
        wc_in = [s.sem(f"wc_in{j}") for j in range(2)]
        yb_slot = [s.sem(f"yb_slot{j}") for j in range(2)]
        gb_slot = [s.sem(f"gb_slot{j}") for j in range(2)]
        w_v = w_in[0].rearrange("(k p) n -> p k n", p=P)
        cpw_v = cpw_w[0].rearrange("(k p) n -> p k n", p=P)
        block = ctx.enter_context(nc.Block())

        @block.sync
        def _(sp):
            if True:
                for j in range(2):
                    sp.dma_start(mu[:, j], shift_mu[0, j].rearrange("(k p) -> p k", p=P)).then_inc(params, 16)
                for n, vec in enumerate((conv_b[0], cnorm_w[0], cnorm_b[0], cpw_b[0], gate_b[0, 0], gate_b[0, 1])):
                    sp.dma_start(cols[:, n], columns(vec)).then_inc(params, 16)
                for k in range(KC):
                    sp.dma_start(cwT[:, k], conv_w[0, :, k * P:(k + 1) * P].rearrange("j p -> p j")).then_inc(params, 16)
            for j in range(NK):
                sp.dma_start(w[:, j], w_v[:, :, TILE0[KINDS[j]] * P:(TILE0[KINDS[j]] + 1) * P]).then_inc(w_in_sem[j], 16)
            with sp.Fori(1, KC) as i:
                for j in range(NK):
                    sp.wait_ge(tile_done, (i - 1) * NK + j + 1)
                    sp.dma_start(w[:, j], w_v[:, :, bass.ds((TILE0[KINDS[j]] + i) * P, P)]).then_inc(w_in_sem[j], 16)
            for j in range(3):
                sp.wait_ge(tile_done, (KC - 1) * NK + j + 1)
                sp.dma_start(w[:, j], w_v[:, :, (3 * KC + j) * P:(3 * KC + j + 1) * P]).then_inc(w_in_sem[j], 16)
            for n in range(KC):
                if n < 2:
                    sp.wait_ge(tile_done, KC * NK)
                else:
                    sp.wait_ge(cpw_done, n - 1)
                sp.dma_start(w[:, 3 + n % 2], cpw_v[:, :, n * P:(n + 1) * P]).then_inc(wc_in[n % 2], 16)

        @block.gpsimd
        def _(pool):
            with pool.Fori(0, KC) as i:
                for j in range(3):
                    hold(pool, shifted[j], i + 1, held)
                    pool.dma_start(g["rkv"][j, bass.ds(i, 1)].rearrange("a p t -> (a p) t"), st[:, j]).then_inc(stored[j], 16)
                for j in range(2):
                    hold(pool, gated[j], i + 1, held)
                    pool.dma_start(g["gate"][j, bass.ds(i, 1)].rearrange("a p t -> (a p) t"), st[:, 3 + j]).then_inc(stored[3 + j], 16)
                for j in range(5):
                    hold(pool, stored[j], 16 * (i + 1), held)
                    pool.sem_inc(left[j], 1)
            for j in range(3):
                pool.wait_ge(shifted[j], KC + 1)
                pool.dma_start(g["lora"][j], st[:, j]).then_inc(stored[j], 16)
            pool.wait_ge(stored[4], 16 * KC)
            for n in range(KC):
                if n >= 2:
                    pool.wait_ge(yb_done, n - 1)
                pool.dma_start(gb[:, n % 2], g["gate"][1, n]).then_inc(gb_slot[n % 2], 16)
                pool.wait_ge(yb_done, n + 1)
                pool.dma_start(g["yb"][n], yo[:, n % 2]).then_inc(yb_slot[n % 2], 16)
            for j in range(3):
                pool.wait_ge(stored[j], 16 * (KC + 1))
            pool.wait_ge(stored[3], 16 * KC)
            for j in range(2):
                pool.wait_ge(yb_slot[j], 16 * KC // 2)

        @block.tensor
        def _(pe):
            def project(j, w_trip, free):
                pe.wait_ge(w_in_sem[j], 16 * (w_trip + 1))
                if free is not None:
                    pe.wait_ge(read[j], free)
                for k in range(KC):
                    ins = nc.tensor.matmul(bank[j][:], w[:, j, k], g["u1T"][:, k], start=(k == 0), stop=(k == KC - 1))
                ins.then_inc(tile_done, 1)
            for j in range(NK):
                project(j, 0, None)
            with pe.Fori(1, KC) as i:
                for j in range(NK):
                    project(j, i, i)
            for j in range(3):
                project(j, KC, KC)
            pe.wait_ge(h_used, KC + 1)
            for k in range(KC):
                ins = nc.tensor.matmul(pstat[:], g["mean1024"][:], hc[:, k], start=(k == 0), stop=(k == KC - 1))
            ins.then_inc(mean_done, 1)
            pe.wait_ge(cent, KC)
            for k in range(KC):
                pe.wait_ge(sq_done, k + 1)
                nc.tensor.matmul(pstat[:], g["mean1024"][:], sq[:, k % 2], start=(k == 0), stop=(k == KC - 1)) \
                  .then_inc(sq_used, 1)
            pe.wait_ge(silu, KC)
            for n in range(KC):
                pe.wait_ge(wc_in[n % 2], 16 * (n // 2 + 1))
                if n < 2:
                    pe.wait_ge(read[3 + n], KC)
                if n >= 2:
                    pe.wait_ge(cpw_read, n - 1)
                for k in range(KC):
                    ins = nc.tensor.matmul(bank[3 + n % 2][:], w[:, 3 + n % 2, k], hc[:, k], start=(k == 0), stop=(k == KC - 1))
                ins.then_inc(cpw_done, 1)

        @block.scalar
        def _(act):
            for sem in (dv, *left):
                act.sem_inc(sem, 1)
            act.wait_ge(params, 16 * (2 + 6 + KC))
            act.wait_ge(dve, 2)
            with act.Fori(0, KC) as i:
                act.wait_ge(tile_done, i * NK + 2)
                act.wait_ge(dv, i + 1)
                nc.scalar.activation(sg[:], bank[1][:], ACT.Sigmoid).then_inc(read[1], 1)
                for j in range(3):
                    act.wait_ge(tile_done, i * NK + 3 + j)
                    act.wait_ge(left[j], i + 1)
                    nc.scalar.activation(st[:, j], bank[2 + j][:], ACT.Copy, scale=mu[:, 2, bass.ds(j * KC + i, 1)]) \
                      .then_inc(base_done, 1)
                for j in range(2):
                    act.wait_ge(tile_done, i * NK + 6 + j)
                    act.wait_ge(left[3 + j], i + 1)
                    nc.scalar.activation(st[:, 3 + j], bank[5 + j][:], ACT.Sigmoid, bias=cols[:, 4 + j, bass.ds(i, 1)]) \
                      .then_inc(gated[j], 1)
                    act.wait_ge(gated[j], i + 1)
                    nc.scalar.sem_inc(read[5 + j], 1)
            for j in range(3):
                act.wait_ge(tile_done, KC * NK + j + 1)
                act.wait_ge(left[j], KC + 1)
                nc.scalar.activation(st[:, j], bank[j][:], ACT.Copy, scale=mu[:, 2, 3 * KC + j:3 * KC + j + 1]) \
                  .then_inc(base_done, 1)
            for k in range(KC):
                act.wait_ge(cent, k + 1)
                if k >= 2:
                    act.wait_ge(sq_used, k - 1)
                nc.scalar.activation(sq[:, k % 2], hc[:, k], ACT.Square).then_inc(sq_done, 1)
            act.wait_ge(sq_used, KC)
            nc.scalar.activation(rs[:], pstat[:], ACT.Sqrt, bias=g["eps"][:, 0:1]).then_inc(std_done, 1)
            for k in range(KC):
                act.wait_ge(nrm, k + 2)
                nc.scalar.activation(hc[:, k], hc[:, k], ACT.Silu, scale=cols[:, 1, k:k + 1], bias=cols[:, 2, k:k + 1]) \
                  .then_inc(silu, 1)

        @block.vector
        def _(v):
            v.sem_inc(h_used, 1)
            nc.vector.memset(hp[:, 0:PAD], 0.0)
            nc.vector.memset(hp[:, PAD + T:], 0.0)
            v.wait_ge(params, 16 * (2 + 6 + KC))
            nc.vector.tensor_tensor(mu[:, 2], mu[:, 0], mu[:, 1], ALU.add).then_inc(dve, 1)
            v.wait_ge(dve, 1)
            nc.vector.tensor_scalar(mu[:, 2], mu[:, 2], -1.0, 1.0, ALU.mult, ALU.add).then_inc(dve, 1)

            conv = s.sem("conv")
            ch = Chain(v, conv)

            def shift(j, tile, b, done, n_base):
                v.wait_ge(base_done, n_base)
                ch(nc.vector.scalar_tensor_tensor(st[:, j, 1:T], bank[b][:, 0:T - 1], mu[:, 0, tile], st[:, j, 1:T],
                                                  ALU.mult, ALU.add))
                nc.vector.scalar_tensor_tensor(st[:, j, 0:T - 1], bank[b][:, 1:T], mu[:, 1, tile], st[:, j, 0:T - 1],
                                               ALU.mult, ALU.add).then_inc(shifted[j], 1)
                v.wait_ge(shifted[j], done)
                v.sem_inc(read[b], 1)

            with v.Fori(0, KC) as i:
                ch.enter(i, CW - 1 + 3)
                v.wait_ge(tile_done, i * NK + 1)
                v.wait_ge(read[1], i + 1)
                v.wait_ge(h_used, i + 1)
                nc.vector.tensor_tensor(hp[:, PAD:PAD + T], bank[0][:], sg[:], ALU.mult).then_inc(dv, 1)
                v.wait_ge(dv, i + 2)
                v.sem_inc(read[0], 1)
                o = hc[:, bass.ds(i, 1), :].rearrange("p a t -> p (a t)")
                ch(nc.vector.tensor_scalar(o, hp[:, 0:T], cwT[:, bass.ds(i, 1), 0], cols[:, 0, bass.ds(i, 1)],
                                           ALU.mult, ALU.add))
                for j in range(1, CW):
                    ins = nc.vector.scalar_tensor_tensor(o, hp[:, j:j + T], cwT[:, bass.ds(i, 1), j], o, ALU.mult, ALU.add)
                    if j < CW - 1:
                        ch(ins)
                    else:
                        ins.then_inc(h_used, 1)
                for j in range(3):
                    shift(j, bass.ds(j * KC + i, 1), 2 + j, i + 1, i * 3 + j + 1)
            ch.leave(KC)
            for j in range(3):
                shift(j, slice(3 * KC + j, 3 * KC + j + 1), j, KC + 1, 3 * KC + j + 1)
            v.wait_ge(mean_done, 1)
            for k in range(KC):
                nc.vector.tensor_tensor(hc[:, k], hc[:, k], pstat[:], ALU.subtract).then_inc(cent, 1)
            v.wait_ge(std_done, 1)
            nc.vector.reciprocal(rs[:], rs[:]).then_inc(nrm, 1)
            v.wait_ge(nrm, 1)
            v.wait_ge(sq_done, KC)
            for k in range(KC):
                nc.vector.tensor_tensor(hc[:, k], hc[:, k], rs[:], ALU.mult).then_inc(nrm, 1)
            for n in range(KC):
                v.wait_ge(cpw_done, n + 1)
                v.wait_ge(gb_slot[n % 2], 16 * (n // 2 + 1))
                if n >= 2:
                    v.wait_ge(yb_slot[n % 2], 16 * (n // 2))
                nc.vector.scalar_tensor_tensor(yo[:, n % 2], bank[3 + n % 2][:], cols[:, 3, n:n + 1], gb[:, n % 2],
                                               ALU.add, ALU.mult).then_inc(cpw_read, 1)
                v.wait_ge(cpw_read, n + 1)
                v.sem_inc(yb_done, 1)


def constants(nc, g):
    with ExitStack() as ctx:
        s = Scope(nc, ctx, "const")
        ms, done = s.sem("ms"), s.sem("done")
        block = ctx.enter_context(nc.Block())

        @block.gpsimd
        def _(pool):
            nc.gpsimd.memset(g["ident"][:], 0.0).then_inc(ms, 1)
            nc.gpsimd.memset(g["mean1024"][:], 1.0 / D).then_inc(done, 1)
            nc.gpsimd.memset(g["eps"][:, 0:1], LN_EPS).then_inc(done, 1)
            nc.gpsimd.memset(g["eps"][:, 1:2], 64e-5).then_inc(done, 1)
            pool.wait_ge(ms, 1)
            nc.gpsimd.affine_select(out=g["ident"][:], in_=g["ident"][:], compare_op=ALU.not_equal, fill=1.0, base=0,
                                    pattern=[[-1, P]], channel_multiplier=1).then_inc(done, 1)


HD = 64
C = 64
NCH = T // C
PAIRS = D // P
DS = math.exp(-0.5)
GN_EPS = 64e-5
LEVELS = 6
NU = 4


def job_steps(d):
    steps = []
    for X in range(2):
        steps += [("GB", d, X, 0), ("GB", d, X, 1), ("GK", d, X, 0), ("GK", d, X, 1)]
    for X in range(2):
        steps += [("TQ", d, X), ("TK", d, X), ("TB", d, X)] + ([("TV", d, X)] if d == 0 else [])
    steps += [("T", d, X, 0) for X in range(2)]
    for j in range(1, LEVELS):
        steps += [("U", d, X, j) for X in range(2)] + [("V", d, X, j) for X in range(2)]
        if j < LEVELS - 1:
            steps += [("T", d, X, j) for X in range(2)]
    steps += [("MV", d, X) for X in range(2)]
    steps += [("AC", d, X, n) for X in range(2) for n in range(2)]
    steps += [("PR", d, X, n) for X in range(2) for n in range(2)]
    for n in range(NCH):
        if n % NU == 0:
            steps.append(("Y", d, n // NU))
        if n < NCH - 1:
            steps.append(("S", d, n))
    return steps


JOB_BANKS = 6


class BankUses:

    def __init__(self):
        self.place, self.per_pair, self.before = {}, [0] * 8, [0] * 8
        n = 0
        for d in range(2):
            for step in job_steps(d):
                self._add(step, n % JOB_BANKS)
                n += 1
            for step in ([("ZW", 1), ("ZA", 1), ("BO", 1), ("G", 1)] if d == 0 else [("SS", 0), ("ZW", 0), ("ZA", 0)]):
                self._add(step, 7 if step[0] in ("ZA", "G") else 6)
        for step in (("MEAN",), ("VAR",)):
            self._add(step, 6)
        for step, b in ((("SS", 0), 6), (("ZW", 0), 6), (("ZA", 0), 7)):
            self.place["first", *step] = (b, self.before[b])
            self.before[b] += 1

    def _add(self, step, bank):
        self.place[step] = (bank, self.per_pair[bank])
        self.per_pair[bank] += 1

    def __call__(self, step, pair):
        if pair is None:
            return self.place["first", *step]
        b, n = self.place[step]
        if isinstance(pair, int) and pair == PAIRS - 1 and step[0] in ("MEAN", "VAR"):
            n -= 2
        return b, self.before[b] + n + pair * self.per_pair[b]


def rwkv(nc, g, w0, w_up, a0, a_up, g_up, k_k, k_a, r_k, lnx_w, lnx_b):
    uses = BankUses()
    with ExitStack() as ctx:
        s = Scope(nc, ctx, "rwkv")
        inb = s.sb("inb", [P, 3, T])
        lo = s.sb("lo", [P, 3, T])
        wst = s.sb("wst", [P, 2, 2, P])
        gst = s.sb("gst", [P, P])
        NPAR = 8
        par = s.sb("par", [P, PAIRS, NPAR])
        pc = s.sb("pc", [P, NPAR])
        lnx = s.sb("lnx", [P, 2, PAIRS])
        kkr, nrm, kk = s.sb("kkr", [P, T]), s.sb("nrm", [P, T]), s.sb("kk", [P, T])
        sq = s.sb("sq", [P, T])
        tw, ta, lw, Ls, Es = (s.sb(n, [P, T]) for n in ("tw", "ta", "lw", "Ls", "Es"))
        eE, eN, eL = (s.sb(n, [P, T]) for n in ("eE", "eN", "eL"))
        kd = s.sb("kd", [P, 2, T])
        bb = s.sb("bb", [P, T])
        bon, gbuf = s.sb("bon", [P, T]), s.sb("gbuf", [P, T])
        GC = s.sb("GC", [P, 2, NCH])
        QR = [s.sb(f"QR{d}", [P, NCH, 2, P]) for d in range(2)]
        KB = [s.sb(f"KB{d}", [P, NCH, 2, P]) for d in range(2)]
        Vbd = s.sb("Vbd", [P, NCH, P])
        Vtm = s.sb("Vtm", [P, NCH, P])
        RB = s.sb("RB", [P, NCH, 3, P])
        MK = s.sb("MK", [P, NCH, 2, P])
        Kt = s.sb("Kt", [P, NCH, P])
        W = s.sb("W", [P, NCH, 2, P])
        AC = s.sb("AC", [P, NCH, 2, P])
        PR = s.sb("PR", [P, NCH, 2, P])
        Tn, Tt, U = (s.sb(n, [P, NCH, P]) for n in ("Tn", "Tt", "U"))
        Sb = s.sb("Sb", [P, 2, P])
        yt = s.sb("yt", [P, T])
        fin = s.sb("fin", [P, 2, T])
        mlow = s.sb("mlow", [P, LEVELS, P])
        mup = s.sb("mup", [P, LEVELS, P])
        mg = s.sb("mg", [P, 2, 2, P])
        sum64 = s.sb("sum64", [P, P])
        mean64 = s.sb("mean64", [P, P])
        cmask = s.sb("cmask", [P, T])
        sq2 = s.sb("sq2", [P, T])
        fsqb, frsb = s.sb("fsqb", [P, T]), s.sb("frsb", [P, T])
        bank = [s.ps(f"bank{i}") for i in range(8)]
        full = [s.sem(f"full{i}") for i in range(8)]
        free = [s.sem(f"free{i}") for i in range(8)]
        names = """masks params lora_in lora_ready in_ready pc_ready wst_ready gst_ready fin_ready kk_sq kk_norm kk_rn
            kk_done in_used logw scanned edone th ta_done exps bd_ready rb_ready mk_ready tt_ready t_ready u_ready
            tm_ready v_ready w_ready ac_ready pr_ready s_ready job_done rkk bo_copied g_copied bon_done cent fsq
            fstd frs fnorm faff fin_done vchain pchain achain wst_used held""".split()
        S = {n: s.sem(n) for n in names}
        block = ctx.enter_context(nc.Block())

        def rep(ap, n):
            a = ap.unsqueeze(1)
            return a.broadcast_to([P, n] + list(ap.shape[1:]))

        def wait_full(eng, step, pair):
            b, n = uses(step, pair)
            eng.wait_ge(full[b], n + 1)
            return bank[b]

        def now_read(ins, step, pair):
            ins.then_inc(free[uses(step, pair)[0]], 1)

        def order(d):
            return list(range(NCH)) if d == 0 else list(range(NCH - 1, -1, -1))

        @block.sync
        def _(sp):
            for n, vec in enumerate((w0[0, 0], w0[0, 1], a0[0, 0], a0[0, 1], k_k[0], k_a[0], k_a[0],
                                     r_k[0].rearrange("h n -> (h n)"))):
                sp.dma_start(par[:, :, n], columns(vec)).then_inc(S["params"], 16)
            for n, vec in enumerate((lnx_w[0], lnx_b[0])):
                sp.dma_start(lnx[:, n], columns(vec)).then_inc(S["params"], 16)
            for j in range(3):
                sp.dma_start(lo[:, j], g["lora"][j]).then_inc(S["lora_in"], 16)

            def load_pair(i):
                one = bass.ds(i, 1)
                for j in range(3):
                    sp.dma_start(inb[:, j], g["rkv"][j, one].rearrange("a p t -> (a p) t")).then_inc(S["in_ready"], 16)
                for d in range(2):
                    rows = slice(d * HD, (d + 1) * HD)
                    sp.dma_start(wst[rows, d, 0], w_up[0, d, :, bass.ds(i * P, P)]).then_inc(S["wst_ready"], 16)
                    sp.dma_start(wst[rows, d, 1], a_up[0, d, :, bass.ds(i * P, P)]).then_inc(S["wst_ready"], 16)
                sp.dma_start(gst[:], g_up[0, :, bass.ds(i * P, P)]).then_inc(S["gst_ready"], 16)

            def load_fin(i):
                one = bass.ds(i, 1)
                sp.dma_start(fin[:, 0], g["gate"][0, one].rearrange("a p t -> (a p) t")).then_inc(S["fin_ready"], 16)
                sp.dma_start(fin[:, 1], g["yb"][one].rearrange("a p t -> (a p) t")).then_inc(S["fin_ready"], 16)

            sp.wait_ge(S["masks"], 5)
            load_pair(0)
            load_fin(0)

            def trip(i):
                sp.wait_ge(S["in_used"], i + 1)
                sp.wait_ge(S["bon_done"], i + 1)
                sp.wait_ge(S["wst_used"], i + 1)
                load_pair(i + 1)
                sp.wait_ge(S["fin_done"], i + 2)
                load_fin(i + 1)
            with sp.Fori(0, PAIRS - 1) as i:
                trip(i)

        @block.gpsimd
        def _(pool):
            ch = Chain(pool, S["pchain"], S["held"])

            def keep(ap, base, pattern, mult, op=ALU.is_ge):
                ch(nc.gpsimd.affine_select(out=ap, in_=ap, compare_op=op, fill=0.0, base=base, pattern=pattern,
                                           channel_multiplier=mult))

            def same_block(ap, b, lo_half=0, half=None):
                size = 2 * b if half is None else b
                keep(ap, -lo_half, [[-2 * b, P // (2 * b)], [0, 2 * b]], 1)
                keep(ap, lo_half + size - 1, [[2 * b, P // (2 * b)], [0, 2 * b]], -1)

            def blocks(ap, b):
                return ap.rearrange("p (n c) -> p n c", c=2 * b)

            pool.sem_inc(S["job_done"], 1)
            ch(nc.gpsimd.memset(mlow[:], 0.0))
            ch(nc.gpsimd.memset(mup[:], 0.0))
            for j in range(LEVELS):
                b = 1 << j
                lowv, upv = blocks(mlow[:, j], b), blocks(mup[:, j], b)
                ch(nc.gpsimd.memset(lowv[:, :, 0:b], 1.0))
                ch(nc.gpsimd.memset(upv[:, :, b:2 * b], 1.0))
                same_block(lowv, b, b, 1)
                same_block(upv, b, 0, 1)
            for d in range(2):
                for n in range(2):
                    ch(nc.gpsimd.memset(mg[:, d, n], 1.0))
                    same_block(blocks(mg[:, d, n], HD // 2), HD // 2)
                    sign = 1 if d == 0 else -1
                    op = ALU.is_ge if (d == 0 and n == 1) else ALU.is_gt
                    keep(mg[:, d, n], 0, [[sign, P]], -sign, op)
            ch(nc.gpsimd.memset(sum64[:], 1.0))
            same_block(blocks(sum64[:], HD // 2), HD // 2)
            ch(nc.gpsimd.memset(mean64[:], 1.0 / HD))
            same_block(blocks(mean64[:], HD // 2), HD // 2)
            ch(nc.gpsimd.memset(cmask[:], 1.0))
            nc.gpsimd.memset(cmask[:].rearrange("p (n c) -> p n c", c=C)[:, :, 0:1], 0.0).then_inc(S["masks"], 1)
            nc.gpsimd.memset(wst[:], 0.0).then_inc(S["masks"], 1)
            for t in (QR[0], QR[1], KB[0], KB[1], Vbd):
                ins = nc.gpsimd.memset(t[:], 0.0)
                ch.mark(ins)
            ch.wait()
            pool.sem_inc(S["masks"], 3)

            def prep(i, d, q, first=False):
                v3 = lambda ap: ap.rearrange("p (n c) -> p n c", c=C)
                hold(pool, S["th"], q + 1, S["held"])
                if not first:
                    hold(pool, S["exps"], q, S["held"])
                    hold(pool, S["scanned"], q, S["held"])
                nc.gpsimd.tensor_scalar(lw[:], tw[:], -DS / 2, -DS / 2, ALU.mult, ALU.add).then_inc(S["logw"], 1)
                ch.mark(nc.gpsimd.tensor_scalar(kd[:, d], ta[:], pc[:, 5:6], pc[:, 6:7], ALU.mult, ALU.add))
                ch(nc.gpsimd.tensor_scalar(bb[:], ta[:], 0.5, 0.5, ALU.mult, ALU.add))
                if d == 0:
                    hold(pool, S["kk_rn"], i + 1, S["held"])
                    ch(nc.gpsimd.tensor_tensor(kk[:], kkr[:], nrm[:], ALU.mult))
                    pool.sem_inc(S["kk_done"], 1)
                ch.mark(nc.gpsimd.tensor_tensor(kd[:, d], kd[:, d], inb[:, 1], ALU.mult))
                ch(nc.gpsimd.tensor_tensor(bb[:], bb[:], kk[:], ALU.mult))
                hold(pool, S["scanned"], q + 1, S["held"])
                nc.gpsimd.tensor_tensor(Es[:], Ls[:], lw[:], ALU.subtract).then_inc(S["edone"], 1)
                if not first:
                    hold(pool, S["job_done"], q, S["held"])
                hold(pool, S["exps"], q + 1, S["held"])
                for h in range(2):
                    rows, cs = slice(h * HD, (h + 1) * HD), slice(h * C, (h + 1) * C)
                    eR = eL if d == 0 else eE
                    for dst, a, b in ((QR[d][rows, :, 0, cs], kk, eE), (KB[d][rows, :, 0, cs], None, eN),
                                      (KB[d][rows, :, 1, cs], bb, eN)):
                        src = kd[rows, d] if a is None else a[rows]
                        ch.mark(nc.gpsimd.tensor_tensor(dst, v3(src), v3(b[rows]), ALU.mult))
                    ch.mark(nc.gpsimd.tensor_tensor(QR[d][rows, :, 1, cs], v3(inb[rows, 0]), v3(eR[rows]), ALU.mult))
                    if d == 0:
                        ch.mark(nc.gpsimd.tensor_copy(Vbd[rows, :, cs], v3(inb[rows, 2])))
                ch.wait()
                if d == 1:
                    ch(nc.gpsimd.tensor_tensor(sq[:], inb[:, 0], kd[:, 0], ALU.mult))
                    ch(nc.gpsimd.tensor_scalar(sq[:], sq[:], pc[:, 7:8], None, ALU.mult))
                    pool.sem_inc(S["rkk"], 1)
                pool.sem_inc(S["bd_ready"], 1)
                if d == 1:
                    pool.sem_inc(S["in_used"], 1)
                    hold(pool, S["bo_copied"], i + 1, S["held"])
                    ch(nc.gpsimd.tensor_tensor(bon[:], bon[:], inb[:, 2], ALU.mult))
                    pool.sem_inc(S["bon_done"], 1)

            prep(0, 0, 0, first=True)
            with pool.Fori(0, PAIRS - 1) as i:
                ch.enter(i, 30)
                prep(i, 1, 2 * i + 1)
                prep(i + 1, 0, 2 * i + 2)
                ch.leave(PAIRS - 1)
            prep(PAIRS - 1, 1, 2 * PAIRS - 1)

        @block.tensor
        def _(pe):
            def begin(step, pair):
                b, n = uses(step, pair)
                pe.wait_ge(free[b], n + 1)
                return bank[b]

            def end(ins, step, pair):
                ins.then_inc(full[uses(step, pair)[0]], 1)

            def mm(out, lhsT, rhs, start=True, stop=True):
                return nc.tensor.matmul(out, lhsT, rhs, start=start, stop=stop)

            def low_rank(pair, d, q):
                pe.wait_ge(S["wst_ready"], 64 * (q // 2 + 1) if isinstance(q, int) else 64 * (pair + 1 + (1 if d == 0 else 0)))
                o = begin(("ZW", d), pair)
                end(mm(o[:], wst[:, d, 0], lo[:, 0]), ("ZW", d), pair)
                o = begin(("ZA", d), pair)
                end(mm(o[:], wst[:, d, 1], lo[:, 1]), ("ZA", d), pair)

            def norm_kk(pair, n):
                pe.wait_ge(S["kk_sq"], n)
                o = begin(("SS", 0), pair)
                end(mm(o[:], sum64[:], sq2[:]), ("SS", 0), pair)

            for sem in free:
                pe.sem_inc(sem, 1)
            pe.wait_ge(S["masks"], 5)
            pe.wait_ge(S["lora_ready"], 2)
            norm_kk(None, 1)
            low_rank(None, 0, 0)

            def job(i, d, last):
                J = 2 * i + d
                pe.wait_ge(S["bd_ready"], J + 1)
                for X in range(2):
                    for which, rhs_of in (("GB", 1), ("GK", 0)):
                        for n in range(2):
                            o = begin((which, d, X, n), i)
                            for m in range(2):
                                c = NU * X + 2 * n + m
                                ins = mm(o[:, m * 256:(m + 1) * 256], KB[d][:, c, rhs_of],
                                         QR[d][:, c].rearrange("p a t -> p (a t)"))
                            end(ins, (which, d, X, n), i)
                for X in range(2):
                    for key, src in (("TQ", lambda c: QR[d][:, c, 0]), ("TK", lambda c: KB[d][:, c, 0]),
                                     ("TB", lambda c: KB[d][:, c, 1])) + ((("TV", lambda c: Vbd[:, c]),) if d == 0 else ()):
                        o = begin((key, d, X), i)
                        for u in range(NU):
                            ins = nc.tensor.transpose(o[:, u * P:(u + 1) * P], src(NU * X + u), g["ident"][:])
                        end(ins, (key, d, X), i)
                for j in range(LEVELS):
                    if j > 0:
                        for X in range(2):
                            pe.wait_ge(S["t_ready"], 10 * J + 2 * (j - 1) + X + 1)
                            o = begin(("U", d, X, j), i)
                            for u in range(NU):
                                c = NU * X + u
                                ins = mm(o[:, u * P:(u + 1) * P], RB[:, c, 0], Tn[:, c])
                            end(ins, ("U", d, X, j), i)
                        for X in range(2):
                            pe.wait_ge(S["u_ready"], 10 * J + 2 * (j - 1) + X + 1)
                            o = begin(("V", d, X, j), i)
                            for u in range(NU):
                                c = NU * X + u
                                ins = mm(o[:, u * P:(u + 1) * P], U[:, c], Tt[:, c])
                            end(ins, ("V", d, X, j), i)
                    if j < LEVELS - 1:
                        for X in range(2):
                            pe.wait_ge(S["tt_ready"], 12 * J + 2 * j + X + 1)
                            o = begin(("T", d, X, j), i)
                            for u in range(NU):
                                ins = nc.tensor.transpose(o[:, u * P:(u + 1) * P], Tt[:, NU * X + u], g["ident"][:])
                            end(ins, ("T", d, X, j), i)
                    if j == 0 and d == 0:
                        low_rank(i, 1, None)
                    if j == 3 and d == 0:
                        pe.wait_ge(S["rkk"], i + 1)
                        o = begin(("BO", 1), i)
                        end(mm(o[:], sum64[:], sq[:]), ("BO", 1), i)
                        o = begin(("G", 1), i)
                        pe.wait_ge(S["gst_ready"], 16 * (i + 1))
                        ins = mm(o[:], gst[:], lo[:, 2])
                        end(ins, ("G", 1), i)
                        pe.wait_ge(full[7], uses(("G", 1), i)[1] + 1)
                        pe.sem_inc(S["wst_used"], 1)
                    if j == 1 and d == 1 and not last:
                        norm_kk(i, i + 2)
                        low_rank(i, 0, None)
                pe.wait_ge(S["v_ready"], 2 * (i + 1))
                for X in range(2):
                    pe.wait_ge(S["mk_ready"], 4 * J + 2 * X + 2)
                    o = begin(("MV", d, X), i)
                    for u in range(NU):
                        c = NU * X + u
                        ins = mm(o[:, u * P:(u + 1) * P], MK[:, c, 0], Vtm[:, c])
                    end(ins, ("MV", d, X), i)
                for X in range(2):
                    pe.wait_ge(S["w_ready"], 2 * J + X + 1)
                    pe.wait_ge(S["tt_ready"], 12 * J + 2 * (LEVELS - 1) + X + 1)
                    for n in range(2):
                        o = begin(("AC", d, X, n), i)
                        for m in range(2):
                            c = NU * X + 2 * n + m
                            ins = mm(o[:, m * 256:(m + 1) * 256], Tt[:, c], W[:, c].rearrange("p a t -> p (a t)"))
                        end(ins, ("AC", d, X, n), i)
                for X in range(2):
                    for n in range(2):
                        pe.wait_ge(S["ac_ready"], 4 * J + 2 * X + n + 1)
                        o = begin(("PR", d, X, n), i)
                        for m in range(2):
                            c = NU * X + 2 * n + m
                            ins = mm(o[:, m * 256:(m + 1) * 256], AC[:, c, 0], RB[:, c, 1:3].rearrange("p a t -> p (a t)"))
                        end(ins, ("PR", d, X, n), i)
                pe.wait_ge(S["pr_ready"], 4 * J + 4)
                for n, c in enumerate(order(d)):
                    u = n % NU
                    if u == 0:
                        oy = begin(("Y", d, n // NU), i)
                    y = oy[:, u * P:(u + 1) * P]
                    if n < NCH - 1:
                        os_ = begin(("S", d, n), i)[:, 0:P]
                        mm(os_, Kt[:, c], Vtm[:, c], True, False)
                        ins = mm(os_, RB[:, c, 1], AC[:, c, 1], False, n == 0)
                        if n == 0:
                            end(ins, ("S", d, n), i)
                    mm(y, Vtm[:, c], MK[:, c, 1], True, False)
                    ins = mm(y, AC[:, c, 1], RB[:, c, 2], False, n == 0)
                    if n > 0:
                        pe.wait_ge(S["s_ready"], 7 * J + n)
                        if n < NCH - 1:
                            end(mm(os_, PR[:, c, 0], Sb[:, n % 2], False, True), ("S", d, n), i)
                        ins = mm(y, Sb[:, n % 2], PR[:, c, 1], False, True)
                    if u == NU - 1:
                        end(ins, ("Y", d, n // NU), i)

            def finish(i):
                pe.wait_ge(S["job_done"], 2 * i + 3)
                o = begin(("MEAN",), i)
                end(mm(o[:], mean64[:], yt[:]), ("MEAN",), i)
                pe.wait_ge(S["fsq"], i + 1)
                o = begin(("VAR",), i)
                end(mm(o[:], mean64[:], fsqb[:]), ("VAR",), i)

            with pe.Fori(0, PAIRS - 1) as i:
                job(i, 0, False)
                job(i, 1, False)
                finish(i)
            job(PAIRS - 1, 0, True)
            job(PAIRS - 1, 1, True)
            finish(PAIRS - 1)

        @block.scalar
        def _(act):
            ch = Chain(act, S["achain"])
            act.sem_inc(S["fin_done"], 1)
            act.wait_ge(S["lora_in"], 48)
            nc.scalar.activation(lo[:, 2], lo[:, 2], ACT.Sigmoid).then_inc(S["lora_ready"], 1)
            nc.scalar.activation(lo[:, 0], lo[:, 0], ACT.Tanh).then_inc(S["lora_ready"], 1)

            def squares(q2):
                act.wait_ge(S["in_ready"], 48 * q2)
                act.wait_ge(S["pc_ready"], q2)
                ch.mark(nc.scalar.activation(kkr[:], inb[:, 1], ACT.Copy, scale=pc[:, 4:5]))
                nc.scalar.activation(sq2[:], inb[:, 1], ACT.Square, scale=pc[:, 4:5]).then_inc(S["kk_sq"], 1)

            def tanhs(pair, d):
                if d == 0:
                    o = wait_full(act, ("SS", 0), pair)
                    ins = nc.scalar.activation(nrm[:], o[:], ACT.Sqrt)
                    now_read(ins, ("SS", 0), pair)
                    act.wait_ge(free[6], uses(("SS", 0), pair)[1] + 2)
                    act.wait_ge(S["achain"], ch.trip + ch.n)
                    act.sem_inc(S["kk_norm"], 1)
                o = wait_full(act, ("ZW", d), pair)
                ins = nc.scalar.activation(tw[:], o[:], ACT.Tanh, scale=0.5, bias=pc[:, d:d + 1])
                now_read(ins, ("ZW", d), pair)
                o = wait_full(act, ("ZA", d), pair)
                ins = nc.scalar.activation(ta[:], o[:], ACT.Tanh, scale=0.5, bias=pc[:, 2 + d:3 + d])
                now_read(ins, ("ZA", d), pair)
                b, n = uses(("ZW", d), pair)
                act.wait_ge(free[b], n + 2)
                b, n = uses(("ZA", d), pair)
                act.wait_ge(free[b], n + 2)
                act.sem_inc(S["th"], 1)

            def exps(d, q):
                act.wait_ge(S["edone"], q + 1)
                ch.mark(nc.scalar.activation(eE[:], Es[:], ACT.Exp))
                ch.mark(nc.scalar.activation(eN[:], Ls[:], ACT.Exp, scale=-1.0))
                if d == 0:
                    ch(nc.scalar.activation(eL[:], Ls[:], ACT.Exp))
                v = Ls[:].rearrange("p (n c) -> p n c", c=C)
                end_ = C - 1 if d == 0 else 0
                ch(nc.scalar.activation(GC[:, d], v[:, :, end_], ACT.Exp))
                act.sem_inc(S["exps"], 1)

            squares(1)
            tanhs(None, 0)
            exps(0, 0)

            def job(i, d, last):
                J = 2 * i + d
                for X in range(2):
                    cs = slice(NU * X, NU * X + NU)
                    for key, dst in (("TQ", W[:, cs, 0]), ("TK", Kt[:, cs]), ("TB", RB[:, cs, 1])) + \
                            ((("TV", Vtm[:, cs]),) if d == 0 else ()):
                        o = wait_full(act, (key, d, X), i)
                        ins = nc.scalar.activation(dst, o[:].rearrange("p (u t) -> p u t", u=NU), ACT.Copy)
                        now_read(ins, (key, d, X), i)
                    b, n = uses(("TB", d, X), i)
                    act.wait_ge(free[b], n + 2)
                    if d == 0:
                        b, n = uses(("TV", d, X), i)
                        act.wait_ge(free[b], n + 2)
                        act.sem_inc(S["v_ready"], 1)
                if d == 1 and not last:
                    squares(i + 2)
                for j in range(LEVELS - 1):
                    for X in range(2):
                        cs = slice(NU * X, NU * X + NU)
                        o = wait_full(act, ("T", d, X, j), i)
                        ins = nc.scalar.activation(Tn[:, cs], o[:].rearrange("p (u t) -> p u t", u=NU), ACT.Copy)
                        now_read(ins, ("T", d, X, j), i)
                        b, n = uses(("T", d, X, j), i)
                        act.wait_ge(free[b], n + 2)
                        act.sem_inc(S["t_ready"], 1)
                    if j == 1:
                        if d == 0:
                            tanhs(i, 1)
                        elif not last:
                            tanhs(i, 0)
                    if j == 3:
                        if d == 0:
                            exps(1, 2 * i + 1)
                        elif not last:
                            exps(0, 2 * i + 2)
                    if j == 4 and d == 0:
                        act.wait_ge(S["fin_done"], i + 1)
                        o = wait_full(act, ("BO", 1), i)
                        now_read(nc.scalar.activation(bon[:], o[:], ACT.Copy), ("BO", 1), i)
                        o = wait_full(act, ("G", 1), i)
                        now_read(nc.scalar.activation(gbuf[:], o[:], ACT.Copy), ("G", 1), i)
                        for key in ("BO", "G"):
                            b, n = uses((key, 1), i)
                            act.wait_ge(free[b], n + 2)
                        act.sem_inc(S["bo_copied"], 1)
                for X in range(2):
                    cs = slice(NU * X, NU * X + NU)
                    o = wait_full(act, ("MV", d, X), i)
                    ins = nc.scalar.activation(W[:, cs, 1], o[:].rearrange("p (u t) -> p u t", u=NU), ACT.Copy)
                    now_read(ins, ("MV", d, X), i)
                    b, n = uses(("MV", d, X), i)
                    act.wait_ge(free[b], n + 2)
                    act.sem_inc(S["w_ready"], 1)
                for n, c in enumerate(order(d)[:-1]):
                    o = wait_full(act, ("S", d, n), i)
                    ins = nc.scalar.activation(Sb[:, (n + 1) % 2], o[:, 0:P], ACT.Copy, scale=GC[:, d, c:c + 1])
                    now_read(ins, ("S", d, n), i)
                    b, m = uses(("S", d, n), i)
                    act.wait_ge(free[b], m + 2)
                    act.sem_inc(S["s_ready"], 1)

            def finish(i):
                act.wait_ge(S["cent"], i + 1)
                nc.scalar.activation(fsqb[:], yt[:], ACT.Square).then_inc(S["fsq"], 1)
                o = wait_full(act, ("VAR",), i)
                ins = nc.scalar.activation(frsb[:], o[:], ACT.Sqrt, bias=g["eps"][:, 1:2])
                now_read(ins, ("VAR",), i)
                b, n = uses(("VAR",), i)
                act.wait_ge(free[b], n + 2)
                act.sem_inc(S["fstd"], 1)
                act.wait_ge(S["fnorm"], i + 1)
                one = bass.ds(i, 1)
                nc.scalar.activation(yt[:], yt[:], ACT.Identity, scale=lnx[:, 0, one], bias=lnx[:, 1, one]) \
                  .then_inc(S["faff"], 1)

            with act.Fori(0, PAIRS - 1) as i:
                ch.enter(i, 8)
                job(i, 0, False)
                job(i, 1, False)
                finish(i)
                ch.leave(PAIRS - 1)
            job(PAIRS - 1, 0, True)
            job(PAIRS - 1, 1, True)
            finish(PAIRS - 1)

        @block.vector
        def _(v):
            ch = Chain(v, S["vchain"])
            v.wait_ge(S["params"], 160)
            ch(nc.vector.tensor_scalar(par[:, :, 0:4], par[:, :, 0:4], 0.5, None, ALU.mult))
            ch(nc.vector.tensor_scalar(par[:, :, 5], par[:, :, 5], 0.5, None, ALU.mult))
            ch(nc.vector.tensor_scalar(par[:, :, 6], par[:, :, 5], -1.0, 1.0, ALU.mult, ALU.add))

            def pick(i):
                nc.vector.tensor_copy(pc[:], par[:, bass.ds(i, 1), :].rearrange("p a n -> p (a n)")).then_inc(S["pc_ready"], 1)

            def scan(d, q, n_kk, first=False):
                if d == 0:
                    v.wait_ge(S["kk_norm"], n_kk)
                    ch(nc.vector.tensor_scalar(nrm[:], nrm[:], 1e-12, None, ALU.max))
                    nc.vector.reciprocal(nrm[:], nrm[:]).then_inc(S["kk_rn"], 1)
                v.wait_ge(S["logw"], q + 1)
                if not first:
                    v.wait_ge(S["exps"], q)
                r = slice(None) if d == 0 else slice(None, None, -1)
                nc.vector.tensor_tensor_scan(Ls[:, r], cmask[:], lw[:, r], 0.0, ALU.mult, ALU.add).then_inc(S["scanned"], 1)

            pick(0)
            v.wait_ge(S["masks"], 5)
            scan(0, 0, 1, first=True)

            def job(i, d, last):
                J = 2 * i + d
                for X in range(2):
                    for n in range(2):
                        cs = slice(NU * X + 2 * n, NU * X + 2 * n + 2)
                        o = wait_full(v, ("GB", d, X, n), i)
                        for h in range(2):
                            ins = nc.vector.tensor_tensor(RB[:, cs, 2 * h],
                                                          o[:].rearrange("p (u a t) -> p u a t", u=2, a=2)[:, :, h],
                                                          rep(mg[:, d, h], 2), ALU.mult)
                            if h == 0:
                                ch.mark(ins)
                        now_read(ins, ("GB", d, X, n), i)
                    for n in range(2):
                        cs = slice(NU * X + 2 * n, NU * X + 2 * n + 2)
                        o = wait_full(v, ("GK", d, X, n), i)
                        ins = nc.vector.tensor_tensor(MK[:, cs].rearrange("p u a t -> p u (a t)"),
                                                      o[:].rearrange("p (u a) -> p u a", u=2),
                                                      rep(mg[:, d].rearrange("p a t -> p (a t)"), 2), ALU.mult)
                        now_read(ins, ("GK", d, X, n), i)
                        b, m = uses(("GK", d, X, n), i)
                        v.wait_ge(free[b], m + 2)
                        v.sem_inc(S["mk_ready"], 1)
                m1t = mup if d == 0 else mlow
                mj = mlow if d == 0 else mup
                ch.wait()
                for X in range(2):
                    cs = slice(NU * X, NU * X + NU)
                    ch.mark(nc.vector.tensor_tensor(Tt[:, cs], RB[:, cs, 0], rep(m1t[:, 0], NU), ALU.mult))
                ch.wait()
                for X in range(2):
                    cs = slice(NU * X, NU * X + NU)
                    nc.vector.tensor_tensor(Tt[:, cs], rep(g["ident"][:], NU), Tt[:, cs], ALU.subtract) \
                      .then_inc(S["tt_ready"], 1)
                if d == 1 and not last:
                    v.wait_ge(S["bon_done"], i + 1)
                    pick(i + 1)
                for j in range(1, LEVELS):
                    for X in range(2):
                        cs = slice(NU * X, NU * X + NU)
                        o = wait_full(v, ("U", d, X, j), i)
                        ins = nc.vector.tensor_tensor(U[:, cs], o[:].rearrange("p (u t) -> p u t", u=NU),
                                                      rep(mj[:, j], NU), ALU.mult)
                        now_read(ins, ("U", d, X, j), i)
                        b, m = uses(("U", d, X, j), i)
                        v.wait_ge(free[b], m + 2)
                        v.sem_inc(S["u_ready"], 1)
                    for X in range(2):
                        cs = slice(NU * X, NU * X + NU)
                        o = wait_full(v, ("V", d, X, j), i)
                        ins = nc.vector.tensor_tensor(Tt[:, cs], Tt[:, cs], o[:].rearrange("p (u t) -> p u t", u=NU),
                                                      ALU.subtract)
                        now_read(ins, ("V", d, X, j), i)
                        b, m = uses(("V", d, X, j), i)
                        v.wait_ge(free[b], m + 2)
                        v.sem_inc(S["tt_ready"], 1)
                    if j == 3:
                        if d == 0:
                            scan(1, 2 * i + 1, None)
                        elif not last:
                            scan(0, 2 * i + 2, i + 2)
                for X in range(2):
                    for n in range(2):
                        cs = slice(NU * X + 2 * n, NU * X + 2 * n + 2)
                        o = wait_full(v, ("AC", d, X, n), i)
                        o4 = o[:].rearrange("p (u a t) -> p u a t", u=2, a=2)
                        ch.mark(nc.vector.tensor_copy(AC[:, cs, 0], o4[:, :, 0]))
                        ins = nc.vector.tensor_scalar(AC[:, cs, 1], o4[:, :, 1], -1.0, None, ALU.mult)
                        now_read(ins, ("AC", d, X, n), i)
                        b, m = uses(("AC", d, X, n), i)
                        v.wait_ge(free[b], m + 2)
                        ch.wait()
                        v.sem_inc(S["ac_ready"], 1)
                for X in range(2):
                    for n in range(2):
                        cs = slice(NU * X + 2 * n, NU * X + 2 * n + 2)
                        o = wait_full(v, ("PR", d, X, n), i)
                        o4 = o[:].rearrange("p (u a t) -> p u a t", u=2, a=2)
                        ch.mark(nc.vector.tensor_tensor(PR[:, cs, 0], rep(g["ident"][:], 2), o4[:, :, 0], ALU.subtract))
                        ins = nc.vector.tensor_tensor(PR[:, cs, 1], QR[d][:, cs, 1], o4[:, :, 1], ALU.subtract)
                        now_read(ins, ("PR", d, X, n), i)
                        b, m = uses(("PR", d, X, n), i)
                        v.wait_ge(free[b], m + 2)
                        ch.wait()
                        v.sem_inc(S["pr_ready"], 1)
                for half in range(2):
                    o = wait_full(v, ("Y", d, half), i)
                    o4 = o[:].rearrange("p (u a) -> p u a", u=NU)
                    cs = order(d)[NU * half:NU * half + NU]
                    for h in range(2):
                        rows, fs = slice(h * HD, (h + 1) * HD), slice(h * C, (h + 1) * C)
                        y3 = yt[rows].rearrange("p (n c) -> p n c", c=C)
                        y3 = y3[:, cs[0]:cs[-1] + 1] if d == 0 else y3[:, cs[-1]:cs[0] + 1][:, ::-1]
                        src = o4[rows, :, fs]
                        ins = (nc.vector.tensor_copy(y3, src) if d == 0 else
                               nc.vector.tensor_tensor(y3, y3, src, ALU.add))
                        if h == 0:
                            ch.mark(ins)
                    now_read(ins, ("Y", d, half), i)
                    b, m = uses(("Y", d, half), i)
                    v.wait_ge(free[b], m + 2)
                ch.wait()
                v.sem_inc(S["job_done"], 1)

            def finish(i):
                o = wait_full(v, ("MEAN",), i)
                ins = nc.vector.tensor_tensor(yt[:], yt[:], o[:], ALU.subtract)
                now_read(ins, ("MEAN",), i)
                b, m = uses(("MEAN",), i)
                v.wait_ge(free[b], m + 2)
                v.sem_inc(S["cent"], 1)
                v.wait_ge(S["fstd"], i + 1)
                ch(nc.vector.reciprocal(frsb[:], frsb[:]))
                nc.vector.tensor_tensor(yt[:], yt[:], frsb[:], ALU.mult).then_inc(S["fnorm"], 1)
                v.wait_ge(S["faff"], i + 1)
                v.wait_ge(S["bon_done"], i + 1)
                ch(nc.vector.tensor_tensor(yt[:], yt[:], bon[:], ALU.add))
                ch(nc.vector.tensor_tensor(yt[:], yt[:], gbuf[:], ALU.mult))
                v.wait_ge(S["fin_ready"], 32 * (i + 1))
                ch(nc.vector.tensor_tensor(yt[:], yt[:], fin[:, 0], ALU.mult))
                nc.vector.tensor_tensor(g["u1T"][:, bass.ds(i, 1), :].rearrange("p a t -> p (a t)"), yt[:], fin[:, 1],
                                        ALU.add).then_inc(S["fin_done"], 1)
                v.wait_ge(S["fin_done"], i + 2)

            with v.Fori(0, PAIRS - 1) as i:
                ch.enter(i, 37)
                job(i, 0, False)
                job(i, 1, False)
                finish(i)
                ch.leave(PAIRS - 1)
            job(PAIRS - 1, 0, True)
            job(PAIRS - 1, 1, True)
            finish(PAIRS - 1)


E = 64
F_EXP = 256
GROUPS, PER_GROUP = 8, 8
TOP_GROUPS, TOP_K = 4, 8
ROUTED_SCALE = 2.5
ALPHA = 2.0 ** 0.25
ROWS = T + P
MAX_BLOCKS = (T * TOP_K - E) // P + E
SLOTS = 3
AHEAD = 2
TRIPS = -(-MAX_BLOCKS // SLOTS)
NBT = SLOTS * TRIPS + AHEAD
BIG = 1e30
N_CONSTS = 6 + SLOTS
NO_ROW = 65536


def row_of(vec):
    return vec.partition_broadcast(P)


def mix_and_route(nc, g, x, w_o, ln1_w, ln1_b, router_w, router_b, sh_gate, sh_up, sh_down):
    with ExitStack() as ctx:
        s = Scope(nc, ctx, "mix")
        wo = s.sb("wo", [P, KC, D])
        rows = s.sb("rows", [P, 5, D])
        xs = s.sb("x", [P, TT, D])
        u2T = s.sb("u2T", [P, KC, T])
        tmp = s.sb("tmp", [P, D])
        st = s.sb("st", [P, 2, 6])
        mv = s.sb("mv", [P, 2])
        rstd = s.sb("rstd", [P, 2 * TT])
        zrow = s.sb("zrow", [P, D])
        rw = s.sb("rw", [P, KC, E])
        rb = s.sb("rb", [P, E])
        shw = s.sb("shw", [P, KC, 2, F_EXP])
        shd = s.sb("shd", [P, 2, D])
        hT = s.sb("hT", [P, 2, T])
        hs = s.sb("hs", [P, 2, T])
        yo = s.sb("yo", [P, TT, D])
        sc = s.sb("sc", [P, TT, E])
        sel = s.sb("sel", [P, TT, E])
        m8 = s.sb("m8", [P, TT, GROUPS, 8])
        gsx = s.sb("gsx", [P, TT, 12])
        t8 = s.sb("t8", [P, TT, 8])
        gr = s.sb("gr", [P, TT, 12])
        er = s.sb("er", [P, TT, E])
        A = s.sb("A", [P, TT, E])
        wgt = s.sb("wgt", [P, TT, E])
        ws = s.sb("ws", [P, TT])
        ones = s.sb("ones", [P, P])
        before = s.sb("before", [P, P])
        upto = s.sb("upto", [P, P])
        iob = s.sb("iob", [E, NBT])
        cnt = s.sb("cnt", [E, 4])
        nb = s.sb("nb", [E, 1])
        nbr = s.sb("nbr", [E, P])
        M = s.sb("M", [E, NBT])
        ci = s.sb("ci", [E, 1])
        bank = [s.ps(f"bank{i}") for i in range(8)]
        (wo_in, x_in, rows_in, sh_in, mixed, mix_read, var1, std1, u2_ready, tp_done, tp_read, u2_out, z_ready, z_out,
         rt_in, h_done, gate_read, up_read, y_done, y_read, y_out, sh_silu, logit, score, sel_done, dve, consts, a_ready,
         pos_done, pos_read, cnt_done, nb_ready, ci_done, m_ready, eb_done, x1_out, pc, acc_sem, row1) = (s.sem(n) for n in (
             """wo_in x_in rows_in sh_in mixed mix_read var1 std1 u2_ready tp_done tp_read u2_out z_ready z_out
         rt_in h_done gate_read up_read y_done y_read y_out sh_silu logit score sel_done dve consts a_ready
         pos_done pos_read cnt_done nb_ready ci_done m_ready eb_done x1_out pc acc_sem row1""").split())
        block = ctx.enter_context(nc.Block())

        @block.sync
        def _(sp):
            sp.dma_start(wo[:], w_o[0].rearrange("(k p) n -> p k n", p=P)).then_inc(wo_in, 16)
            sp.dma_start(xs[:], x[0].rearrange("(n p) d -> p n d", p=P)).then_inc(x_in, 16)
            mod = g["mod"][0]
            for n, vec in enumerate((mod[2 * D:3 * D], ln1_w[0], ln1_b[0], mod[4 * D:5 * D], mod[3 * D:4 * D])):
                sp.dma_start(rows[:, n], row_of(vec)).then_inc(rows_in, 16)
            sp.dma_start(rw[:], router_w[0].rearrange("(k p) n -> p k n", p=P)).then_inc(rt_in, 16)
            sp.dma_start(rb[:], row_of(router_b[0])).then_inc(rt_in, 16)
            sp.dma_start(shw[:, :, 0], sh_gate[0].rearrange("(k p) n -> p k n", p=P)).then_inc(sh_in, 16)
            sp.dma_start(shw[:, :, 1], sh_up[0].rearrange("(k p) n -> p k n", p=P)).then_inc(sh_in, 16)
            sp.dma_start(shd[:], sh_down[0].rearrange("(c p) n -> p c n", p=P)).then_inc(sh_in, 16)
            sp.wait_ge(z_ready, 1)
            sp.dma_start(g["u2d"][T:ROWS], zrow[:]).then_inc(z_out, 16)
            sp.dma_start(g["acc"][T:ROWS], zrow[:]).then_inc(z_out, 16)
            for t in range(TT):
                sp.wait_ge(u2_ready, t + 1)
                sp.dma_start(g["u2d"][t * P:(t + 1) * P], xs[:, t]).then_inc(u2_out, 16)
            for t in range(TT):
                sp.wait_ge(y_read, 2 * t + 2)
                sp.dma_start(g["acc"][t * P:(t + 1) * P], yo[:, t]).then_inc(y_out, 16)
            sp.wait_ge(z_out, 32)
            sp.wait_ge(u2_out, 16 * TT)
            sp.wait_ge(y_out, 16 * TT)

        @block.gpsimd
        def _(pool):
            nc.gpsimd.memset(zrow[:], 0.0).then_inc(z_ready, 1)
            nc.gpsimd.memset(ones[:], 1.0).then_inc(pc, 1)
            nc.gpsimd.memset(before[:], 1.0).then_inc(pc, 1)
            nc.gpsimd.memset(upto[:], 1.0).then_inc(pc, 1)
            nc.gpsimd.memset(gsx[:], BIG).then_inc(pc, 1)
            pool.wait_ge(pc, 4)
            nc.gpsimd.affine_select(out=before[:], in_=before[:], compare_op=ALU.is_gt, fill=0.0, base=0,
                                    pattern=[[1, P]], channel_multiplier=-1).then_inc(consts, 1)
            nc.gpsimd.affine_select(out=upto[:], in_=upto[:], compare_op=ALU.is_ge, fill=0.0, base=0,
                                    pattern=[[1, P]], channel_multiplier=-1).then_inc(consts, 1)
            nc.gpsimd.iota(iob[:], pattern=[[1, NBT]], base=0, channel_multiplier=0,
                           allow_small_or_imprecise_dtypes=True).then_inc(consts, 1)
            nc.gpsimd.iota(g["place"][:], pattern=[[0, TT], [1, P]], base=1, channel_multiplier=0,
                           allow_small_or_imprecise_dtypes=True).then_inc(consts, 1)
            for b in range(SLOTS):
                nc.gpsimd.iota(g["rhs"][:, b, :, 0], pattern=[[P, TT]], base=1, channel_multiplier=1,
                               allow_small_or_imprecise_dtypes=True).then_inc(consts, 1)
            nc.gpsimd.iota(g["spare"][:, 0:1], pattern=[[0, 1]], base=T, channel_multiplier=1,
                           allow_small_or_imprecise_dtypes=True).then_inc(consts, 1)
            nc.gpsimd.iota(g["spare"][:, 1:2], pattern=[[0, 1]], base=-(T + 1), channel_multiplier=-1,
                           allow_small_or_imprecise_dtypes=True).then_inc(consts, 1)

        @block.tensor
        def _(pe):
            pe.wait_ge(wo_in, 16)
            for t in range(TT):
                for h in range(2):
                    for k in range(KC):
                        ins = nc.tensor.matmul(bank[2 * t + h][:], g["u1T"][:, k, t * P:(t + 1) * P],
                                               wo[:, k, h * 512:(h + 1) * 512], start=(k == 0), stop=(k == KC - 1))
                ins.then_inc(mixed, 1)
            pe.wait_ge(mix_read, 2 * TT)
            for t in range(TT):
                pe.wait_ge(u2_ready, t + 1)
                for h in range(2):
                    n = 2 * t + h
                    if n >= 2:
                        pe.wait_ge(tp_read, n - 1)
                    for k in range(4):
                        ins = nc.tensor.transpose(bank[n % 2][:, k * P:(k + 1) * P], xs[:, t, (4 * h + k) * P:(4 * h + k + 1) * P],
                                                  g["ident"][:])
                    ins.then_inc(tp_done, 1)
            pe.wait_ge(tp_read, 2 * TT)
            pe.wait_ge(rt_in, 32)
            for t in range(TT):
                for k in range(KC):
                    ins = nc.tensor.matmul(bank[2][:, t * E:(t + 1) * E], u2T[:, k, t * P:(t + 1) * P], rw[:, k],
                                           start=(k == 0), stop=(k == KC - 1))
                ins.then_inc(logit, 1)
            pe.wait_ge(sh_in, 48)
            for f in range(2):
                for w in range(2):
                    for k in range(KC):
                        ins = nc.tensor.matmul(bank[4 + 2 * f + w][:], shw[:, k, w, f * P:(f + 1) * P], u2T[:, k],
                                               start=(k == 0), stop=(k == KC - 1))
                    ins.then_inc(h_done, 1)
            pe.wait_ge(up_read, 2)
            for t in range(TT):
                for h in range(2):
                    n = 2 * t + h
                    if n >= 2:
                        pe.wait_ge(y_read, n - 1)
                    for f in range(2):
                        ins = nc.tensor.matmul(bank[n % 2][:], hT[:, f, t * P:(t + 1) * P], shd[:, f, h * 512:(h + 1) * 512],
                                               start=(f == 0), stop=(f == 1))
                    ins.then_inc(y_done, 1)
            pe.wait_ge(consts, N_CONSTS)
            pe.wait_ge(a_ready, TT)
            for t in range(TT):
                o = bank[3][:, t * E:(t + 1) * E]
                for i in range(t):
                    nc.tensor.matmul(o, ones[:], A[:, i], start=(i == 0), stop=False)
                nc.tensor.matmul(o, before[:], A[:, t], start=(t == 0), stop=True).then_inc(pos_done, 1)
            for t in range(TT):
                ins = nc.tensor.matmul(bank[2][0:E, 0:1], A[:, t], ones[:, 0:1], start=(t == 0), stop=(t == TT - 1))
            ins.then_inc(cnt_done, 1)
            pe.wait_ge(nb_ready, 1)
            nc.tensor.matmul(bank[4][0:E, 0:1], upto[0:E, 0:E], nb[:], start=True, stop=True).then_inc(ci_done, 1)
            pe.wait_ge(m_ready, 1)
            nc.tensor.matmul(bank[5][:, 0:NBT], ones[0:E], M[:], start=True, stop=True)
            nc.tensor.matmul(bank[6][:, 0:NBT], nbr[:], M[:], start=True, stop=True)
            nc.tensor.matmul(bank[7][:, 0:1], nbr[:], ones[0:E, 0:1], start=True, stop=True).then_inc(eb_done, 1)

        @block.scalar
        def _(act):
            for n in range(2 * TT):
                act.wait_ge(var1, n + 1)
                nc.scalar.activation(rstd[:, n:n + 1], mv[:, 1:2], ACT.Sqrt, bias=g["eps"][:, 0:1]).then_inc(std1, 1)
            for t in range(TT):
                act.wait_ge(logit, TT)
                nc.scalar.activation(sc[:, t], bank[2][:, t * E:(t + 1) * E], ACT.Sigmoid).then_inc(score, 1)
            for f in range(2):
                act.wait_ge(h_done, 2 * f + 1)
                nc.scalar.activation(hs[:, f], bank[4 + 2 * f][:], ACT.Silu).then_inc(sh_silu, 1)
            for n in range(2 * TT):
                act.wait_ge(y_done, n + 1)
                nc.scalar.activation(yo[:, n // 2, (n % 2) * 512:(n % 2 + 1) * 512], bank[n % 2][:], ACT.Copy) \
                   .then_inc(y_read, 1)

        @block.vector
        def _(v):
            ch = Chain(v, dve)
            v.wait_ge(rows_in, 80)
            ch.mark(nc.vector.tensor_scalar(rows[:, 0], rows[:, 0], 1.0, None, ALU.add))
            ch(nc.vector.tensor_scalar(rows[:, 3], rows[:, 3], 1.0, None, ALU.add))
            v.wait_ge(x_in, 16)

            def norm(t, src, dst, w, b, n, done):
                for h in range(2):
                    ch.mark(nc.vector.bn_stats(st[:, h], src[:, h * 512:(h + 1) * 512]))
                ch.wait()
                nc.vector.bn_aggr(mv[:], st[:]).then_inc(var1, 1)
                v.wait_ge(std1, n + 1)
                ch(nc.vector.reciprocal(rstd[:, n:n + 1], rstd[:, n:n + 1]))
                ch(nc.vector.tensor_scalar(tmp[:], src, mv[:, 0:1], rstd[:, n:n + 1], ALU.subtract, ALU.mult))
                ch(nc.vector.tensor_tensor(tmp[:], tmp[:], rows[:, w], ALU.mult))
                ins = nc.vector.tensor_tensor(dst, tmp[:], rows[:, b], ALU.add)
                if done is None:
                    ch(ins)
                else:
                    ins.then_inc(done, 1)

            for t in range(TT):
                v.wait_ge(mixed, t + 1)
                for h in range(2):
                    hs_ = slice(h * 512, (h + 1) * 512)
                    nc.vector.tensor_tensor(tmp[:, hs_], bank[2 * t + h][:], rows[:, 0, hs_], ALU.mult).then_inc(mix_read, 1)
                v.wait_ge(mix_read, 2 * t + 2)
                ch(nc.vector.scalar_tensor_tensor(tmp[:], xs[:, t], ALPHA, tmp[:], ALU.mult, ALU.add))
                ch(nc.vector.tensor_copy(xs[:, t], tmp[:]))
                norm(t, xs[:, t], g["x1"][:, t], 1, 2, 2 * t, None)
                norm(t, g["x1"][:, t], xs[:, t], 3, 4, 2 * t + 1, u2_ready)
                v.wait_ge(u2_ready, t + 1)
            for n in range(2 * TT):
                t, h = n // 2, n % 2
                v.wait_ge(tp_done, n + 1)
                nc.vector.tensor_copy(u2T[:, 4 * h:4 * h + 4, t * P:(t + 1) * P],
                                      bank[n % 2][:].rearrange("p (k t) -> p k t", k=4)).then_inc(tp_read, 1)
            v.wait_ge(rt_in, 32)
            v.wait_ge(consts, N_CONSTS)
            for t in range(TT):
                v.wait_ge(score, t + 1)
                ch(nc.vector.tensor_tensor(sel[:, t], sc[:, t], rb[:], ALU.add))
                for q in range(GROUPS):
                    ch.mark(nc.vector.max(m8[:, t, q], sel[:, t, q * PER_GROUP:(q + 1) * PER_GROUP]))
                ch.wait()
                ch(nc.vector.tensor_tensor(gsx[:, t, 4:12], m8[:, t, :, 0], m8[:, t, :, 1], ALU.add))
                ch(nc.vector.max(t8[:, t], gsx[:, t]))
                ch(nc.vector.match_replace(gr[:, t], t8[:, t], gsx[:, t], -BIG))
                ch(nc.vector.tensor_scalar(gr[:, t], gr[:, t], -BIG / 2, -BIG, ALU.is_gt, ALU.mult))
                gv = gr[:, t, 4:12].unsqueeze(2).broadcast_to([P, GROUPS, PER_GROUP])
                ch(nc.vector.tensor_tensor(sel[:, t].rearrange("p (q n) -> p q n", q=GROUPS),
                                           sel[:, t].rearrange("p (q n) -> p q n", q=GROUPS), gv, ALU.add))
                ch(nc.vector.max(t8[:, t], sel[:, t]))
                ch(nc.vector.match_replace(er[:, t], t8[:, t], sel[:, t], -3e38))
                ch(nc.vector.tensor_scalar(A[:, t], er[:, t], -2e38, None, ALU.is_lt))
                v.sem_inc(a_ready, 1)
                ch(nc.vector.tensor_tensor(wgt[:, t], sc[:, t], A[:, t], ALU.mult))
                ch(nc.vector.tensor_reduce(ws[:, t:t + 1], wgt[:, t], AX_X, ALU.add))
                ch(nc.vector.reciprocal(ws[:, t:t + 1], ws[:, t:t + 1]))
                ch(nc.vector.tensor_scalar(g["pg"][:, :, t, 1], wgt[:, t], ws[:, t:t + 1], ROUTED_SCALE, ALU.mult, ALU.mult))
                if t < 2:
                    v.wait_ge(h_done, 2 * t + 2)
                    v.wait_ge(sh_silu, t + 1)
                    nc.vector.tensor_tensor(hT[:, t], hs[:, t], bank[5 + 2 * t][:], ALU.mult).then_inc(up_read, 1)
            for t in range(TT):
                v.wait_ge(pos_done, TT)
                nc.vector.scalar_tensor_tensor(g["pg"][:, :, t, 0], bank[3][:, t * E:(t + 1) * E], 1.0, A[:, t],
                                               ALU.add, ALU.mult).then_inc(pos_read, 1)
            v.wait_ge(cnt_done, 1)
            for j in range(4):
                ch.mark(nc.vector.tensor_scalar(cnt[:, j:j + 1], bank[2][0:E, 0:1], float(P * j), None, ALU.is_gt))
            ch.wait()
            ch(nc.vector.tensor_reduce(nb[:], cnt[:], AX_X, ALU.add))
            v.sem_inc(nb_ready, 1)
            v.wait_ge(ci_done, 1)
            ch(nc.vector.tensor_copy(ci[:], bank[4][0:E, 0:1]))
            ch.mark(nc.vector.tensor_scalar(M[:], iob[:], ci[:], None, ALU.is_ge))
            ch(nc.vector.tensor_scalar(nbr[:], ones[0:E], nb[:], None, ALU.mult))
            v.sem_inc(m_ready, 1)
            v.wait_ge(eb_done, 1)
            ch.mark(nc.vector.tensor_scalar(g["table"][0:1, 0:NBT], bank[5][0:1, 0:NBT], float(E - 1), None, ALU.min))
            ch.mark(nc.vector.tensor_copy(g["table"][0:1, NBT:NBT + 1], bank[7][0:1, 0:1]))
            ch(nc.vector.tensor_copy(g["c0"][:], bank[6][:, 0:NBT]))
            ch(nc.vector.tensor_tensor(g["c0"][:], g["place"][:, 0, 0:NBT], g["c0"][:], ALU.subtract))
            ch(nc.vector.tensor_scalar(g["c0"][:], g["c0"][:], float(P), -float(P), ALU.mult, ALU.add))


def moe(nc, g, exp_gate, exp_up, exp_down):
    with ExitStack() as ctx:
        s = Scope(nc, ctx, "moe")
        wg = [s.sb(f"wg{p}", [P, KC, 2, F_EXP]) for p in range(SLOTS)]
        wd = [s.sb(f"wd{p}", [P, 2, D]) for p in range(SLOTS)]
        xg = [s.sb(f"xg{p}", [P, D]) for p in range(SLOTS)]
        xT = s.sb("xT", [P, KC, P])
        S_ = s.sb("S", [P, TT, P])
        pos = s.sb("pos", [P, TT])
        hs, hm = s.sb("hs", [P, F_EXP]), s.sb("hm", [P, F_EXP])
        hT = s.sb("hT", [P, 2, P])
        y = [s.sb(f"y{p}", [P, D]) for p in range(SLOTS)]
        val = s.sb("val", [P, 2])
        occ = s.sb("occ", [P, 1])
        row = s.sb("row", [P, 1])
        idx = [s.sb(f"idx{p}", [P, 1], I32) for p in range(SLOTS)]
        sidx = [s.sb(f"sidx{p}", [P, 1], I32) for p in range(SLOTS)]
        gcol = [s.sb(f"gcol{p}", [P, 1]) for p in range(SLOTS)]
        fetch = s.sb("fetch", [P, 1])
        pH = s.ps("pH")
        pX = [s.ps(f"pX{h}") for h in range(2)]
        pY = [s.ps(f"pY{h}") for h in range(2)]
        pT, pI = s.ps("pT"), s.ps("pI")
        wg_in = [s.sem(f"wg_in{p}") for p in range(SLOTS)]
        wu_in = [s.sem(f"wu_in{p}") for p in range(SLOTS)]
        wd_in = [s.sem(f"wd_in{p}") for p in range(SLOTS)]
        gathered = [s.sem(f"gathered{p}") for p in range(SLOTS)]
        h_done = [s.sem(f"h_done{p}") for p in range(SLOTS)]
        d_done = [s.sem(f"d_done{p}") for p in range(SLOTS)]
        (s_built, i_done, i_ready, x_zero, x_turned, x_read, silu_done, hm_done, h_turned, h_read,
         y0_read, y1_read, dch, held) = (s.sem(n) for n in (
             "s_built i_done i_ready x_zero x_turned x_read silu_done hm_done h_turned h_read "
             "y0_read y1_read dch held").split())
        y_free = [s.sem(f"y_free{p}") for p in range(SLOTS)]
        added = s.sem("added")
        block = ctx.enter_context(nc.Block())

        def blocks(eng, body):
            n_blocks = eng.value_load(g["table"][0:1, NBT:NBT + 1], min_val=1, max_val=MAX_BLOCKS)
            with eng.Fori(0, TRIPS) as i:
                with eng.If(SLOTS * i < n_blocks):
                    body(SLOTS * i, 0, i)
                    for p in range(1, SLOTS):
                        with eng.If(SLOTS * i + p < n_blocks):
                            body(SLOTS * i + p, p, i)
            return n_blocks

        def expert(eng, b):
            return bass.ds(eng.value_load(g["table"][0:1, bass.ds(b, 1)], min_val=0, max_val=E - 1), 1)

        @block.sync
        def _(sp):
            def body(b, p, i):
                e = expert(sp, b)
                sp.wait_ge(h_done[p], i + 1)
                sp.dma_start(wg[p][:, :, 0], exp_gate[0, e].rearrange("a (p k) f -> p (a k) f", p=P)).then_inc(wg_in[p], 16)
                sp.dma_start(wg[p][:, :, 1], exp_up[0, e].rearrange("a (p k) f -> p (a k) f", p=P)).then_inc(wu_in[p], 16)
                sp.wait_ge(d_done[p], 2 * i + 1)
                sp.dma_start(wd[p][:], exp_down[0, e].rearrange("a (p c) d -> p (a c) d", p=P)).then_inc(wd_in[p], 16)
            blocks(sp, body)

        @block.gpsimd
        def _(pool):
            def gather(b, q):
                hold(pool, i_ready, b + 1, held)
                pool.indirect_dma_start(out=xg[q][:], out_offset=None, in_=g["u2d"][:],
                                        in_offset=bass.IndirectOffsetOnAxis(ap=idx[q][:, 0:1], axis=0),
                                        bounds_check=ROWS - 1, oob_is_err=False).then_inc(gathered[q], 16)

            for q in range(SLOTS):
                nc.gpsimd.memset(xg[q][:], 0.0).then_inc(x_zero, 1)
            pool.wait_ge(x_zero, SLOTS)
            for q in range(AHEAD):
                gather(q, q)

            def body(b, p, i):
                hold(pool, x_turned, 2 * b + 2, held)
                gather(b + AHEAD, (p + AHEAD) % SLOTS)
                hold(pool, y0_read, b + 2, held)
                hold(pool, y1_read, b + 2, held)
                pool.indirect_dma_start(out=g["acc"][:], out_offset=bass.IndirectOffsetOnAxis(ap=sidx[p][:, 0:1], axis=0),
                                        in_=y[p][:], in_offset=None, bounds_check=ROWS - 1, compute_op=ALU.add) \
                    .then_inc(added, 16)
                hold(pool, added, 16 * (b + 1), held)
                pool.sem_inc(y_free[p], 1)
            n = blocks(pool, body)
            for q in range(SLOTS):
                pool.wait_ge(gathered[q], 16 * ((n + AHEAD + SLOTS - 1 - q) // SLOTS))

        @block.tensor
        def _(pe):
            def indices(b, q):
                pe.wait_ge(s_built, b + 1)
                for t in range(TT):
                    ins = nc.tensor.matmul(pI[:, 2 * q:2 * q + 2], S_[:, t], g["rhs"][:, q, t], start=(t == 0), stop=(t == TT - 1))
                ins.then_inc(i_done, 1)

            def turn_x(b, q, n, h, first=False):
                pe.wait_ge(gathered[q], 16 * (n + 1))
                if not first:
                    pe.wait_ge(x_read, 2 * b + h - 1)
                x3 = xg[q][:].rearrange("t (p k) -> t k p", k=KC)
                for k in range(4):
                    ins = nc.tensor.transpose(pX[h][:, k * P:(k + 1) * P], x3[:, 4 * h + k], g["ident"][:])
                ins.then_inc(x_turned, 1)

            for sem in (*h_done, *d_done, *y_free, y0_read, y1_read):
                pe.sem_inc(sem, 1)
            for q in range(AHEAD):
                indices(q, q)
            for h in range(2):
                turn_x(0, 0, 0, h, first=True)
            hm3 = hm[:].rearrange("t (p c) -> t c p", c=2)

            def body(b, p, i):
                pe.wait_ge(x_read, 2 * b + 2)
                pe.wait_ge(wg_in[p], 16 * (i + 1))
                pe.wait_ge(wu_in[p], 16 * (i + 1))
                for k in range(KC):
                    ins = nc.tensor.matmul(pH[:], xT[:, k], wg[p][:, k].rearrange("p w f -> p (w f)"),
                                           start=(k == 0), stop=(k == KC - 1))
                ins.then_inc(h_done[p], 1)
                after = (p + 1) % SLOTS, i + (p + 1) // SLOTS
                turn_x(b + 1, *after, 0)
                pe.wait_ge(hm_done, b + 1)
                for f in range(2):
                    ins = nc.tensor.transpose(pT[:, f * P:(f + 1) * P], hm3[:, f], g["ident"][:])
                ins.then_inc(h_turned, 1)
                indices(b + AHEAD, (p + AHEAD) % SLOTS)
                turn_x(b + 1, *after, 1)
                pe.wait_ge(h_read, b + 1)
                pe.wait_ge(wd_in[p], 16 * (i + 1))
                for h, used in ((0, y0_read), (1, y1_read)):
                    pe.wait_ge(used, b + 1)
                    for f in range(2):
                        ins = nc.tensor.matmul(pY[h][:], hT[:, f], wd[p][:, f, h * 512:(h + 1) * 512], start=(f == 0), stop=(f == 1))
                    ins.then_inc(d_done[p], 1)
            blocks(pe, body)

        @block.scalar
        def _(act):
            def read_x(b, h):
                act.wait_ge(x_turned, 2 * b + h + 1)
                nc.scalar.activation(xT[:, 4 * h:4 * h + 4], pX[h][:].rearrange("p (k t) -> p k t", k=4), ACT.Copy) \
                   .then_inc(x_read, 1)
            for h in range(2):
                read_x(0, h)

            def body(b, p, i):
                act.wait_ge(h_done[p], i + 2)
                nc.scalar.activation(hs[:], pH[:, 0:F_EXP], ACT.Silu).then_inc(silu_done, 1)
                read_x(b + 1, 0)
                act.wait_ge(h_turned, b + 1)
                nc.scalar.activation(hT[:], pT[:, 0:2 * P].rearrange("p (f t) -> p f t", f=2), ACT.Copy).then_inc(h_read, 1)
                read_x(b + 1, 1)
                act.wait_ge(d_done[p], 2 * i + 2)
                act.wait_ge(i_ready, b + 1)
                act.wait_ge(y_free[p], i + 1)
                nc.scalar.activation(y[p][:, 0:512], pY[0][:], ACT.Copy, scale=gcol[p][:, 0:1]).then_inc(y0_read, 1)
            blocks(act, body)

        @block.vector
        def _(v):
            ch = Chain(v, dch)

            def match(b, q):
                e = expert(v, b)
                ch.mark(nc.vector.tensor_copy(g["rhs"][:, q, :, 1], g["pg"][:, e, :, 1].rearrange("p a t -> p (a t)")))
                ch(nc.vector.tensor_scalar(pos[:], g["pg"][:, e, :, 0].rearrange("p a t -> p (a t)"),
                                           g["c0"][:, bass.ds(b, 1)], None, ALU.subtract))
                nc.vector.tensor_tensor(S_[:], g["place"][:], pos[:].unsqueeze(2).broadcast_to([P, TT, P]),
                                        ALU.is_equal).then_inc(s_built, 1)

            def rows(b, q):
                v.wait_ge(i_done, b + 1)
                ch(nc.vector.tensor_copy(val[:], pI[:, 2 * q:2 * q + 2]))
                ch.mark(nc.vector.tensor_copy(gcol[q][:], val[:, 1:2]))
                ch.mark(nc.vector.tensor_scalar(fetch[:], val[:, 0:1], 0.5, float(NO_ROW), ALU.is_lt, ALU.mult))
                ch(nc.vector.tensor_scalar(occ[:], val[:, 0:1], 1.0, None, ALU.min))
                ch.mark(nc.vector.scalar_tensor_tensor(row[:], occ[:], g["spare"][:, 1:2], val[:, 0:1], ALU.mult, ALU.add))
                nc.vector.scalar_tensor_tensor(idx[q][:], val[:, 0:1], -1.0, fetch[:], ALU.add, ALU.add).then_inc(i_ready, 1)
                ch.wait()
                ch(nc.vector.tensor_tensor(sidx[q][:], row[:], g["spare"][:, 0:1], ALU.add))

            for b in range(AHEAD):
                match(b, b)
                rows(b, b)

            def body(b, p, i):
                ch.enter(b, 8)
                q = (p + AHEAD) % SLOTS
                match(b + AHEAD, q)
                v.wait_ge(silu_done, b + 1)
                nc.vector.tensor_tensor(hm[:], hs[:], pH[:, F_EXP:2 * F_EXP], ALU.mult).then_inc(hm_done, 1)
                v.wait_ge(y_free[q], i + 1 + (p + AHEAD) // SLOTS)
                rows(b + AHEAD, q)
                v.wait_ge(d_done[p], 2 * i + 3)
                nc.vector.tensor_scalar(y[p][:, 512:D], pY[1][:], gcol[p][:, 0:1], None, ALU.mult).then_inc(y1_read, 1)
                assert ch.n - ch.start == ch.length, ch.n - ch.start
                ch.n = ch.start
            blocks(v, body)


def last_norm(nc, g, ln2_w, ln2_b, out):
    with ExitStack() as ctx:
        s = Scope(nc, ctx, "last")
        rows = s.sb("rows", [P, 3, D])
        acc = s.sb("acc", [P, TT, D])
        st = s.sb("st", [P, TT, 2, 6])
        mv = s.sb("mv", [P, TT, 2])
        rstd = s.sb("rstd", [P, TT])
        rows_in, acc_in, var_done, std_done, out_ready, stored, dve = (s.sem(n) for n in (
            "rows_in acc_in var_done std_done out_ready stored dve").split())
        acc_in = [s.sem(f"acc_in{t}") for t in range(TT)]
        block = ctx.enter_context(nc.Block())

        @block.sync
        def _(sp):
            for n, vec in enumerate((g["mod"][0][5 * D:6 * D], ln2_w[0], ln2_b[0])):
                sp.dma_start(rows[:, n], row_of(vec)).then_inc(rows_in, 16)
            for t in range(TT):
                sp.dma_start(acc[:, t], g["acc"][t * P:(t + 1) * P]).then_inc(acc_in[t], 16)
            for t in range(TT):
                sp.wait_ge(out_ready, t + 1)
                sp.dma_start(out[0, t * P:(t + 1) * P], acc[:, t]).then_inc(stored, 16)
            sp.wait_ge(stored, 16 * TT)

        @block.scalar
        def _(act):
            for t in range(TT):
                act.wait_ge(var_done, t + 1)
                nc.scalar.activation(rstd[:, t:t + 1], mv[:, t, 1:2], ACT.Sqrt, bias=g["eps"][:, 0:1]).then_inc(std_done, 1)

        @block.vector
        def _(v):
            ch = Chain(v, dve)
            v.wait_ge(rows_in, 48)
            ch(nc.vector.tensor_scalar(rows[:, 0], rows[:, 0], 1.0, None, ALU.add))
            for t in range(TT):
                v.wait_ge(acc_in[t], 16)
                ch(nc.vector.tensor_tensor(acc[:, t], acc[:, t], rows[:, 0], ALU.mult))
                ch(nc.vector.scalar_tensor_tensor(acc[:, t], g["x1"][:, t], ALPHA, acc[:, t], ALU.mult, ALU.add))
                for h in range(2):
                    ch.mark(nc.vector.bn_stats(st[:, t, h], acc[:, t, h * 512:(h + 1) * 512]))
                ch.wait()
                nc.vector.bn_aggr(mv[:, t], st[:, t]).then_inc(var_done, 1)
                v.wait_ge(std_done, t + 1)
                ch(nc.vector.reciprocal(rstd[:, t:t + 1], rstd[:, t:t + 1]))
                ch(nc.vector.tensor_scalar(acc[:, t], acc[:, t], mv[:, t, 0:1], rstd[:, t:t + 1], ALU.subtract, ALU.mult))
                ch(nc.vector.tensor_tensor(acc[:, t], acc[:, t], rows[:, 1], ALU.mult))
                nc.vector.tensor_tensor(acc[:, t], acc[:, t], rows[:, 2], ALU.add).then_inc(out_ready, 1)


_INS = """x c ada_w ada_b w_in shift_mu w0 w_up a0 a_up g_up k_k k_a r_k lnx_w lnx_b conv_w conv_b cnorm_w
cnorm_b cpw_w cpw_b gate_b w_o ln1_w ln1_b router_w router_b exp_gate exp_up exp_down sh_gate sh_up sh_down
ln2_w ln2_b""".split()


def hybrid_encoder_layer(nc, a, out):
    with ExitStack() as ctx:
        ctx.enter_context(nc.allow_non_contiguous_dma("columns of parameters"))

        def sb(name, shape, dt=F32):
            return ctx.enter_context(nc.sbuf_tensor(name, shape, dt))

        g = {
            "u1T": sb("u1T", [P, KC, T]),
            "ident": sb("ident", [P, P]),
            "mean1024": sb("mean1024", [P, P]),
            "eps": sb("eps", [P, 2]),
        }
        for name, shape in (("mod", (1, MODS * D)), ("rkv", (3, KC, P, T)), ("lora", (3, P, T)), ("gate", (2, KC, P, T)),
                            ("yb", (KC, P, T)), ("u2d", (ROWS, D)), ("acc", (ROWS, D))):
            g[name] = nc.dram_tensor(f"scratch_{name}", shape, F32, kind="Internal").ap()
        constants(nc, g)
        modulation_and_norm(nc, g, a["x"], a["c"], a["ada_w"], a["ada_b"])
        projections_and_conv(nc, g, *[a[n] for n in (
            "w_in", "shift_mu", "conv_w", "conv_b", "cnorm_w", "cnorm_b", "cpw_w", "cpw_b", "gate_b")])
        rwkv(nc, g, *[a[n] for n in ("w0", "w_up", "a0", "a_up", "g_up", "k_k", "k_a", "r_k", "lnx_w", "lnx_b")])
        g["x1"] = sb("x1", [P, TT, D])
        g["pg"] = sb("pg", [P, E, TT, 2])
        g["place"] = sb("place", [P, TT, P])
        g["rhs"] = sb("rhs", [P, SLOTS, TT, 2])
        g["spare"] = sb("spare", [P, 2])
        g["table"] = sb("table", [1, NBT + 2], I32)
        g["c0"] = sb("c0", [P, NBT])
        mix_and_route(nc, g, *[a[n] for n in ("x", "w_o", "ln1_w", "ln1_b", "router_w", "router_b",
                                              "sh_gate", "sh_up", "sh_down")])
        moe(nc, g, a["exp_gate"], a["exp_up"], a["exp_down"])
        last_norm(nc, g, a["ln2_w"], a["ln2_b"], out)


def kernel(**inputs):
    import numpy as _np
    import concourse.bacc as _bacc
    from concourse.bass_utils import run_bass_kernel_spmd as _run

    nc = _bacc.Bacc("TRN2", target_bir_lowering=False, num_devices=1)
    arrays, args = {}, {}
    for name in _INS:
        arr = _np.ascontiguousarray(inputs[name])
        arrays[f"in_{name}"] = arr
        args[name] = nc.dram_tensor(f"in_{name}", arr.shape, mybir.dt.from_np(arr.dtype), kind="ExternalInput").ap()
    out = nc.dram_tensor("out", (1, T, D), F32, kind="ExternalOutput").ap()
    hybrid_encoder_layer(nc, args, out)
    r = _run(nc, [arrays], core_ids=[0])
    return r.results[0]["out"]
```

```python
from contextlib import ExitStack
import math
import concourse.bass as bass
from concourse import mybir

F32 = mybir.dt.float32
I32 = mybir.dt.int32
ALU = mybir.AluOpType
ACT = mybir.ActivationFunctionType
AX_X = mybir.AxisListType.X

P = 128
T = 512
D = 1024
KC = D // P
TT = T // P
HALF = 3 * D
CW = 31
PAD = CW // 2
LN_EPS = 1e-5
RW_COLS = 3 * D + 4 * 64 + 128
MODS = 6


def hold(pool, sem, value, held):
    pool.wait_ge(sem, value)
    pool.sem_inc(held, 1)


class Chain:

    def __init__(self, eng, sem, held=None):
        self.eng, self.sem, self.n, self.trip, self.held = eng, sem, 0, 0, held

    def enter(self, trip, length):
        self.trip, self.length, self.start = trip * length, length, self.n

    def leave(self, trips):
        assert self.n - self.start == self.length, (self.n - self.start, self.length)
        self.n, self.trip = self.start + self.length * trips, 0

    def mark(self, ins):
        ins.then_inc(self.sem, 1)
        self.n += 1

    def wait(self):
        if self.held is None:
            self.eng.wait_ge(self.sem, self.trip + self.n)
        else:
            hold(self.eng, self.sem, self.trip + self.n, self.held)

    def __call__(self, ins):
        self.mark(ins)
        self.wait()


class Scope:

    def __init__(self, nc, ctx, stage):
        self.nc, self.ctx, self.stage, self.sems = nc, ctx, stage, []
        ctx.callback(self.close)

    def close(self):
        self.nc.clear_and_free_semaphores(self.sems)
        self.nc.all_engine_barrier()

    def sb(self, name, shape, dt=F32):
        return self.ctx.enter_context(self.nc.sbuf_tensor(f"{self.stage}_{name}", list(shape), dt))

    def ps(self, name, shape=(P, 512)):
        return self.ctx.enter_context(self.nc.psum_tensor(f"{self.stage}_{name}", list(shape), F32))

    def sem(self, name):
        self.sems.append(self.nc.alloc_semaphore(f"{self.stage}_{name}"))
        return self.sems[-1]


def columns(vec, n=KC):
    return vec.rearrange("(k p) -> p k", p=P)


def modulation_and_norm(nc, g, x, c, ada_w, ada_b):
    with ExitStack() as ctx:
        s = Scope(nc, ctx, "mod")
        NB = 4
        aw = s.sb("aw", [P, NB, HALF])
        xs = s.sb("x", [P, TT, D])
        xn = s.sb("xn", [P, TT, D])
        ccol = s.sb("ccol", [P, KC])
        csil = s.sb("csil", [P, KC])
        abrow = s.sb("abrow", [1, MODS * D])
        modrow = s.sb("modrow", [1, MODS * D])
        sh = s.sb("sh", [P, KC])
        sc = s.sb("sc", [P, KC])
        stats = s.sb("stats", [P, TT, 2, 6])
        mv = s.sb("mv", [P, TT, 2])
        std = s.sb("std", [P, TT])
        rstd = s.sb("rstd", [P, TT])
        acc = [s.ps(f"acc{i}") for i in range(6)]
        tp = [s.ps(f"tp{i}") for i in range(2)]
        x_in, c_in, b_in = s.sem("x_in"), s.sem("c_in"), s.sem("b_in")
        aw_in = [s.sem(f"aw_in{i}") for i in range(NB)]
        aw_used, silu_done, half_done, row_half, row_out, cols_in = (s.sem(n) for n in (
            "aw_used", "silu_done", "half_done", "row_half", "row_out", "cols_in"))
        var_done, std_done, xn_done, tp_done, tp_used, dve = (s.sem(n) for n in (
            "var_done", "std_done", "xn_done", "tp_done", "tp_used", "dve"))
        block = ctx.enter_context(nc.Block())

        @block.sync
        def _(sp):
            sp.dma_start(ccol[:], columns(c[0])).then_inc(c_in, 16)
            sp.dma_start(xs[:], x[0].rearrange("(n p) d -> p n d", p=P)).then_inc(x_in, 16)
            sp.dma_start(abrow[:], ada_b).then_inc(b_in, 16)
            for n in range(2 * KC):
                h, k = n // KC, n % KC
                if n >= NB:
                    sp.wait_ge(aw_used, n - NB + 1)
                sp.dma_start(aw[:, n % NB], ada_w[0, k * P:(k + 1) * P, h * HALF:(h + 1) * HALF]) \
                  .then_inc(aw_in[n % NB], 16)
            sp.wait_ge(row_half, 12)
            sp.dma_start(g["mod"], modrow[0:1, :]).then_inc(row_out, 16)
            sp.wait_ge(row_out, 16)
            sp.dma_start(sh[:], columns(g["mod"][0, 0:D])).then_inc(cols_in, 16)
            sp.dma_start(sc[:], columns(g["mod"][0, D:2 * D])).then_inc(cols_in, 16)

        @block.gpsimd
        def _(pool):
            pass

        @block.scalar
        def _(act):
            act.wait_ge(c_in, 16)
            nc.scalar.activation(csil[:], ccol[:], ACT.Silu).then_inc(silu_done, 1)
            act.wait_ge(var_done, TT)
            nc.scalar.activation(std[:], mv[:, :, 1], ACT.Sqrt, bias=g["eps"][:, 0:1]).then_inc(std_done, 1)

        @block.tensor
        def _(pe):
            pe.wait_ge(silu_done, 1)
            for n in range(2 * KC):
                h, k = n // KC, n % KC
                pe.wait_ge(aw_in[n % NB], 16 * (n // NB + 1))
                if n == KC:
                    pe.wait_ge(row_half, 6)
                for j in range(6):
                    ins = nc.tensor.matmul(acc[j][0:1, :], csil[:, k:k + 1], aw[:, n % NB, j * 512:(j + 1) * 512],
                                           start=(k == 0), stop=(k == KC - 1))
                ins.then_inc(aw_used, 1)
            pe.wait_ge(xn_done, TT)
            for k in range(KC):
                if k >= 2:
                    pe.wait_ge(tp_used, k - 1)
                for t in range(TT):
                    ins = nc.tensor.transpose(tp[k % 2][:, t * P:(t + 1) * P], xn[:, t, k * P:(k + 1) * P], g["ident"][:])
                ins.then_inc(tp_done, 1)

        @block.vector
        def _(v):
            ch = Chain(v, dve)
            v.wait_ge(x_in, 16)
            for t in range(TT):
                for h in range(2):
                    ch.mark(nc.vector.bn_stats(stats[:, t, h, :], xs[:, t, h * 512:(h + 1) * 512]))
            ch.wait()
            for t in range(TT):
                nc.vector.bn_aggr(mv[:, t, :], stats[:, t, :, :]).then_inc(var_done, 1)
            v.wait_ge(std_done, 1)
            ch(nc.vector.reciprocal(rstd[:], std[:]))
            for t in range(TT):
                nc.vector.tensor_scalar(xn[:, t, :], xs[:, t, :], mv[:, t, 0:1], rstd[:, t:t + 1],
                                        ALU.subtract, ALU.mult).then_inc(xn_done, 1)
            v.wait_ge(b_in, 16)
            for h in range(2):
                v.wait_ge(aw_used, (h + 1) * KC)
                for j in range(6):
                    o = h * HALF + j * 512
                    nc.vector.tensor_tensor(modrow[0:1, o:o + 512], acc[j][0:1, :], abrow[0:1, o:o + 512],
                                            ALU.add).then_inc(row_half, 1)
            v.wait_ge(cols_in, 32)
            ch(nc.vector.tensor_scalar(sc[:], sc[:], 1.0, None, ALU.add))
            for k in range(KC):
                v.wait_ge(tp_done, k + 1)
                nc.vector.tensor_scalar(g["u1T"][:, k, :], tp[k % 2][:], sc[:, k:k + 1], sh[:, k:k + 1],
                                        ALU.mult, ALU.add).then_inc(tp_used, 1)


RW_TILES = RW_COLS // P
TILE0 = {"ha": RW_TILES, "hb": RW_TILES + KC, "r": 0, "k": KC, "v": 2 * KC,
         "ga": RW_TILES + 2 * KC, "gb": RW_TILES + 3 * KC}
KINDS = list(TILE0)


def projections_and_conv(nc, g, w_in, shift_mu, conv_w, conv_b, cnorm_w, cnorm_b, cpw_w, cpw_b, gate_b):
    with ExitStack() as ctx:
        s = Scope(nc, ctx, "proj")
        NK = len(KINDS)
        w = s.sb("w", [P, NK, KC, P])
        mu = s.sb("mu", [P, 3, RW_TILES])
        cwT = s.sb("cwT", [P, KC, CW])
        cols = s.sb("cols", [P, 6, KC])
        sg = s.sb("sg", [P, T])
        hp = s.sb("hp", [P, T + 2 * PAD])
        hc = s.sb("hc", [P, KC, T])
        st = s.sb("st", [P, 5, T])
        sq = s.sb("sq", [P, 2, T])
        rs = s.sb("rs", [P, T])
        gb = s.sb("gb", [P, 2, T])
        yo = s.sb("yo", [P, 2, T])
        bank = [s.ps(f"bank{i}") for i in range(NK)]
        pstat = s.ps("pstat")
        w_in_sem = [s.sem(f"w{k}") for k in KINDS]
        params, dve, sg_done, h_used, base_done, out_ready, dv = (s.sem(n) for n in (
            "params", "dve", "sg_done", "h_used", "base_done", "out_ready", "dv"))
        held = s.sem("held")
        left = [s.sem(f"left{j}") for j in range(5)]
        tile_done = s.sem("tile_done")
        read = [s.sem(f"read_{k}") for k in KINDS]
        shifted = [s.sem(f"shifted{j}") for j in range(3)]
        gated = [s.sem(f"gated{j}") for j in range(2)]
        stored = [s.sem(f"stored{j}") for j in range(5)]
        mean_done, cent, sq_done, sq_used, var_done, std_done, nrm, silu, cpw_done, cpw_read, yb_done, gb_in, yb_out = (
            s.sem(n) for n in ("mean_done", "cent", "sq_done", "sq_used", "var_done", "std_done", "nrm", "silu",
                               "cpw_done", "cpw_read", "yb_done", "gb_in", "yb_out"))
        wc_in = [s.sem(f"wc_in{j}") for j in range(2)]
        yb_slot = [s.sem(f"yb_slot{j}") for j in range(2)]
        gb_slot = [s.sem(f"gb_slot{j}") for j in range(2)]
        w_v = w_in[0].rearrange("(k p) n -> p k n", p=P)
        cpw_v = cpw_w[0].rearrange("(k p) n -> p k n", p=P)
        block = ctx.enter_context(nc.Block())

        @block.sync
        def _(sp):
            if True:
                for j in range(2):
                    sp.dma_start(mu[:, j], shift_mu[0, j].rearrange("(k p) -> p k", p=P)).then_inc(params, 16)
                for n, vec in enumerate((conv_b[0], cnorm_w[0], cnorm_b[0], cpw_b[0], gate_b[0, 0], gate_b[0, 1])):
                    sp.dma_start(cols[:, n], columns(vec)).then_inc(params, 16)
                for k in range(KC):
                    sp.dma_start(cwT[:, k], conv_w[0, :, k * P:(k + 1) * P].rearrange("j p -> p j")).then_inc(params, 16)
            for j in range(NK):
                sp.dma_start(w[:, j], w_v[:, :, TILE0[KINDS[j]] * P:(TILE0[KINDS[j]] + 1) * P]).then_inc(w_in_sem[j], 16)
            with sp.Fori(1, KC) as i:
                for j in range(NK):
                    sp.wait_ge(tile_done, (i - 1) * NK + j + 1)
                    sp.dma_start(w[:, j], w_v[:, :, bass.ds((TILE0[KINDS[j]] + i) * P, P)]).then_inc(w_in_sem[j], 16)
            for j in range(3):
                sp.wait_ge(tile_done, (KC - 1) * NK + j + 1)
                sp.dma_start(w[:, j], w_v[:, :, (3 * KC + j) * P:(3 * KC + j + 1) * P]).then_inc(w_in_sem[j], 16)
            for n in range(KC):
                if n < 2:
                    sp.wait_ge(tile_done, KC * NK)
                else:
                    sp.wait_ge(cpw_done, n - 1)
                sp.dma_start(w[:, 3 + n % 2], cpw_v[:, :, n * P:(n + 1) * P]).then_inc(wc_in[n % 2], 16)

        @block.gpsimd
        def _(pool):
            with pool.Fori(0, KC) as i:
                for j in range(3):
                    hold(pool, shifted[j], i + 1, held)
                    pool.dma_start(g["rkv"][j, bass.ds(i, 1)].rearrange("a p t -> (a p) t"), st[:, j]).then_inc(stored[j], 16)
                for j in range(2):
                    hold(pool, gated[j], i + 1, held)
                    pool.dma_start(g["gate"][j, bass.ds(i, 1)].rearrange("a p t -> (a p) t"), st[:, 3 + j]).then_inc(stored[3 + j], 16)
                for j in range(5):
                    hold(pool, stored[j], 16 * (i + 1), held)
                    pool.sem_inc(left[j], 1)
            for j in range(3):
                pool.wait_ge(shifted[j], KC + 1)
                pool.dma_start(g["lora"][j], st[:, j]).then_inc(stored[j], 16)
            pool.wait_ge(stored[4], 16 * KC)
            for n in range(KC):
                if n >= 2:
                    pool.wait_ge(yb_done, n - 1)
                pool.dma_start(gb[:, n % 2], g["gate"][1, n]).then_inc(gb_slot[n % 2], 16)
                pool.wait_ge(yb_done, n + 1)
                pool.dma_start(g["yb"][n], yo[:, n % 2]).then_inc(yb_slot[n % 2], 16)
            for j in range(3):
                pool.wait_ge(stored[j], 16 * (KC + 1))
            pool.wait_ge(stored[3], 16 * KC)
            for j in range(2):
                pool.wait_ge(yb_slot[j], 16 * KC // 2)

        @block.tensor
        def _(pe):
            def project(j, w_trip, free):
                pe.wait_ge(w_in_sem[j], 16 * (w_trip + 1))
                if free is not None:
                    pe.wait_ge(read[j], free)
                for k in range(KC):
                    ins = nc.tensor.matmul(bank[j][:], w[:, j, k], g["u1T"][:, k], start=(k == 0), stop=(k == KC - 1))
                ins.then_inc(tile_done, 1)
            for j in range(NK):
                project(j, 0, None)
            with pe.Fori(1, KC) as i:
                for j in range(NK):
                    project(j, i, i)
            for j in range(3):
                project(j, KC, KC)
            pe.wait_ge(h_used, KC + 1)
            for k in range(KC):
                ins = nc.tensor.matmul(pstat[:], g["mean1024"][:], hc[:, k], start=(k == 0), stop=(k == KC - 1))
            ins.then_inc(mean_done, 1)
            pe.wait_ge(cent, KC)
            for k in range(KC):
                pe.wait_ge(sq_done, k + 1)
                nc.tensor.matmul(pstat[:], g["mean1024"][:], sq[:, k % 2], start=(k == 0), stop=(k == KC - 1)) \
                  .then_inc(sq_used, 1)
            pe.wait_ge(silu, KC)
            for n in range(KC):
                pe.wait_ge(wc_in[n % 2], 16 * (n // 2 + 1))
                if n < 2:
                    pe.wait_ge(read[3 + n], KC)
                if n >= 2:
                    pe.wait_ge(cpw_read, n - 1)
                for k in range(KC):
                    ins = nc.tensor.matmul(bank[3 + n % 2][:], w[:, 3 + n % 2, k], hc[:, k], start=(k == 0), stop=(k == KC - 1))
                ins.then_inc(cpw_done, 1)

        @block.scalar
        def _(act):
            for sem in (dv, *left):
                act.sem_inc(sem, 1)
            act.wait_ge(params, 16 * (2 + 6 + KC))
            act.wait_ge(dve, 2)
            with act.Fori(0, KC) as i:
                act.wait_ge(tile_done, i * NK + 2)
                act.wait_ge(dv, i + 1)
                nc.scalar.activation(sg[:], bank[1][:], ACT.Sigmoid).then_inc(read[1], 1)
                for j in range(3):
                    act.wait_ge(tile_done, i * NK + 3 + j)
                    act.wait_ge(left[j], i + 1)
                    nc.scalar.activation(st[:, j], bank[2 + j][:], ACT.Copy, scale=mu[:, 2, bass.ds(j * KC + i, 1)]) \
                      .then_inc(base_done, 1)
                for j in range(2):
                    act.wait_ge(tile_done, i * NK + 6 + j)
                    act.wait_ge(left[3 + j], i + 1)
                    nc.scalar.activation(st[:, 3 + j], bank[5 + j][:], ACT.Sigmoid, bias=cols[:, 4 + j, bass.ds(i, 1)]) \
                      .then_inc(gated[j], 1)
                    act.wait_ge(gated[j], i + 1)
                    nc.scalar.sem_inc(read[5 + j], 1)
            for j in range(3):
                act.wait_ge(tile_done, KC * NK + j + 1)
                act.wait_ge(left[j], KC + 1)
                nc.scalar.activation(st[:, j], bank[j][:], ACT.Copy, scale=mu[:, 2, 3 * KC + j:3 * KC + j + 1]) \
                  .then_inc(base_done, 1)
            for k in range(KC):
                act.wait_ge(cent, k + 1)
                if k >= 2:
                    act.wait_ge(sq_used, k - 1)
                nc.scalar.activation(sq[:, k % 2], hc[:, k], ACT.Square).then_inc(sq_done, 1)
            act.wait_ge(sq_used, KC)
            nc.scalar.activation(rs[:], pstat[:], ACT.Sqrt, bias=g["eps"][:, 0:1]).then_inc(std_done, 1)
            for k in range(KC):
                act.wait_ge(nrm, k + 2)
                nc.scalar.activation(hc[:, k], hc[:, k], ACT.Silu, scale=cols[:, 1, k:k + 1], bias=cols[:, 2, k:k + 1]) \
                  .then_inc(silu, 1)

        @block.vector
        def _(v):
            v.sem_inc(h_used, 1)
            nc.vector.memset(hp[:, 0:PAD], 0.0)
            nc.vector.memset(hp[:, PAD + T:], 0.0)
            v.wait_ge(params, 16 * (2 + 6 + KC))
            nc.vector.tensor_tensor(mu[:, 2], mu[:, 0], mu[:, 1], ALU.add).then_inc(dve, 1)
            v.wait_ge(dve, 1)
            nc.vector.tensor_scalar(mu[:, 2], mu[:, 2], -1.0, 1.0, ALU.mult, ALU.add).then_inc(dve, 1)

            conv = s.sem("conv")
            ch = Chain(v, conv)

            def shift(j, tile, b, done, n_base):
                v.wait_ge(base_done, n_base)
                ch(nc.vector.scalar_tensor_tensor(st[:, j, 1:T], bank[b][:, 0:T - 1], mu[:, 0, tile], st[:, j, 1:T],
                                                  ALU.mult, ALU.add))
                nc.vector.scalar_tensor_tensor(st[:, j, 0:T - 1], bank[b][:, 1:T], mu[:, 1, tile], st[:, j, 0:T - 1],
                                               ALU.mult, ALU.add).then_inc(shifted[j], 1)
                v.wait_ge(shifted[j], done)
                v.sem_inc(read[b], 1)

            with v.Fori(0, KC) as i:
                ch.enter(i, CW - 1 + 3)
                v.wait_ge(tile_done, i * NK + 1)
                v.wait_ge(read[1], i + 1)
                v.wait_ge(h_used, i + 1)
                nc.vector.tensor_tensor(hp[:, PAD:PAD + T], bank[0][:], sg[:], ALU.mult).then_inc(dv, 1)
                v.wait_ge(dv, i + 2)
                v.sem_inc(read[0], 1)
                o = hc[:, bass.ds(i, 1), :].rearrange("p a t -> p (a t)")
                ch(nc.vector.tensor_scalar(o, hp[:, 0:T], cwT[:, bass.ds(i, 1), 0], cols[:, 0, bass.ds(i, 1)],
                                           ALU.mult, ALU.add))
                for j in range(1, CW):
                    ins = nc.vector.scalar_tensor_tensor(o, hp[:, j:j + T], cwT[:, bass.ds(i, 1), j], o, ALU.mult, ALU.add)
                    if j < CW - 1:
                        ch(ins)
                    else:
                        ins.then_inc(h_used, 1)
                for j in range(3):
                    shift(j, bass.ds(j * KC + i, 1), 2 + j, i + 1, i * 3 + j + 1)
            ch.leave(KC)
            for j in range(3):
                shift(j, slice(3 * KC + j, 3 * KC + j + 1), j, KC + 1, 3 * KC + j + 1)
            v.wait_ge(mean_done, 1)
            for k in range(KC):
                nc.vector.tensor_tensor(hc[:, k], hc[:, k], pstat[:], ALU.subtract).then_inc(cent, 1)
            v.wait_ge(std_done, 1)
            nc.vector.reciprocal(rs[:], rs[:]).then_inc(nrm, 1)
            v.wait_ge(nrm, 1)
            v.wait_ge(sq_done, KC)
            for k in range(KC):
                nc.vector.tensor_tensor(hc[:, k], hc[:, k], rs[:], ALU.mult).then_inc(nrm, 1)
            for n in range(KC):
                v.wait_ge(cpw_done, n + 1)
                v.wait_ge(gb_slot[n % 2], 16 * (n // 2 + 1))
                if n >= 2:
                    v.wait_ge(yb_slot[n % 2], 16 * (n // 2))
                nc.vector.scalar_tensor_tensor(yo[:, n % 2], bank[3 + n % 2][:], cols[:, 3, n:n + 1], gb[:, n % 2],
                                               ALU.add, ALU.mult).then_inc(cpw_read, 1)
                v.wait_ge(cpw_read, n + 1)
                v.sem_inc(yb_done, 1)


def constants(nc, g):
    with ExitStack() as ctx:
        s = Scope(nc, ctx, "const")
        ms, done = s.sem("ms"), s.sem("done")
        block = ctx.enter_context(nc.Block())

        @block.gpsimd
        def _(pool):
            nc.gpsimd.memset(g["ident"][:], 0.0).then_inc(ms, 1)
            nc.gpsimd.memset(g["mean1024"][:], 1.0 / D).then_inc(done, 1)
            nc.gpsimd.memset(g["eps"][:, 0:1], LN_EPS).then_inc(done, 1)
            nc.gpsimd.memset(g["eps"][:, 1:2], 64e-5).then_inc(done, 1)
            pool.wait_ge(ms, 1)
            nc.gpsimd.affine_select(out=g["ident"][:], in_=g["ident"][:], compare_op=ALU.not_equal, fill=1.0, base=0,
                                    pattern=[[-1, P]], channel_multiplier=1).then_inc(done, 1)


HD = 64
C = 64
NCH = T // C
PAIRS = D // P
DS = math.exp(-0.5)
GN_EPS = 64e-5
LEVELS = 6
NU = 4


class Pair:

    def __init__(self, trip, off):
        self.trip, self.off = trip, off
        self.n = off if trip is None else trip + off

    def next(self):
        return Pair(self.trip, self.off + 1)

    def before(self):
        return Pair(self.trip, self.off - 1)


FILL = {0: {"A0": ("ZW", "ZA", "MEAN"), "B1": (("TV", 0),), "A1": (("TV", 1),), "B2": (("TQ", 0),), "A2": ("VAR", ("TQ", 1)),
            "B3": (("TK", 0),), "A3": (("TK", 1),), "B4": (("TB", 0),), "A4": (("TB", 1),)},
        1: {"A0": ("SS", "ZW", "ZA"), "B1": (("TQ", 0),), "A1": (("TQ", 1),), "B2": (("TK", 0),), "A2": (("TK", 1),),
            "B3": (("TB", 0),), "A3": (), "B4": (("TB", 1),), "A4": ()}}


def gram_steps(d, p):
    return [((which, d, X, n), p) for which in ("GB", "GK") for X in range(2) for n in range(2)]


def groups(d):
    g = [(X, n) for X in range(2) for n in range(2)]
    return g if d == 0 else g[::-1]


def fill_steps(d, p, at, first, last):
    out = []
    for f in FILL[d][at]:
        if isinstance(f, tuple):
            out.append(((f[0], d, f[1]), p))
        elif f in ("MEAN", "VAR"):
            if not first:
                out.append(((f,), p.before()))
        elif d == 0:
            out.append(((f, 1), p))
        elif not last:
            out.append(((f, 0), p.next()))
    return out


def job_steps(p, d, first, last):
    fill = lambda at: fill_steps(d, p, at, first, last)
    steps = [(("T", d, X, 0), p) for X in range(2)] + fill("A0")
    for j in range(1, LEVELS):
        steps += [(("U", d, X, j), p) for X in range(2)] + [(("V", d, X, j), p) for X in range(2)]
        if j < LEVELS - 1:
            steps += fill(f"B{j}") + [(("T", d, X, j), p) for X in range(2)] + fill(f"A{j}")
    steps += [(("MV", d, X), p) for X in range(2)]
    if d == 0:
        steps += [(("BO", 1), p), (("G", 1), p)]
    steps += [(("AC", d, X, n), p) for X, n in groups(d)]
    steps += [(("PR", d, X, n), p) for X, n in groups(d)]
    gram = [] if last else gram_steps(1 - d, p if d == 0 else p.next())
    for n in range(NCH):
        if n % NU == 0:
            steps.append((("Y", d, n // NU), p))
        if n < NCH - 1:
            steps.append((("S", d, n), p))
        steps += gram[n:n + 1]
    return steps


class BankUses:

    FIXED = {("Y", 0): 5, ("Y", 1): 7, "ZA": 7, "G": 7, "ZW": 6, "SS": 6, "BO": 6, "MEAN": 6, "VAR": 6}

    def __init__(self):
        zero = Pair(None, 0)
        steps = [(("SS", 0), zero), (("ZW", 0), zero), (("ZA", 0), zero)] + gram_steps(0, zero)
        for J in range(2 * PAIRS):
            steps += job_steps(Pair(None, J // 2), J % 2, J == 0, J == 2 * PAIRS - 1)
        last = Pair(None, PAIRS - 1)
        steps += [(("MEAN",), last), (("VAR",), last)]
        self.use, used = {}, [0] * 8
        at = {}
        turn = {"scan": 0, "rest": 0}
        for step, p in steps:
            if step not in at:
                key = ("Y", step[2]) if step[0] == "Y" else step[0]
                kind = "scan" if step[0] in ("S", "GB", "GK") else "rest"
                if key in self.FIXED:
                    at[step] = self.FIXED[key]
                else:
                    at[step] = turn[kind] % (5 if kind == "scan" else 6)
                    turn[kind] += 1
            b = at[step]
            self.use[step, p.off] = (b, used[b])
            used[b] += 1

    def __call__(self, step, p):
        b, n = self.use[step, p.off]
        if p.trip is None:
            return b, n
        each = self.use[step, p.off + 1][1] - n
        for k in range(PAIRS - 1):
            assert self.use[step, p.off + k] == (b, n + k * each), step
        return b, n + p.trip * each


def rwkv(nc, g, w0, w_up, a0, a_up, g_up, k_k, k_a, r_k, lnx_w, lnx_b):
    uses = BankUses()
    with ExitStack() as ctx:
        s = Scope(nc, ctx, "rwkv")
        inb = s.sb("inb", [P, 3, T])
        lo = s.sb("lo", [P, 3, T])
        wst = s.sb("wst", [P, 2, 2, P])
        gst = s.sb("gst", [P, P])
        NPAR = 8
        par = s.sb("par", [P, PAIRS, NPAR])
        pc = s.sb("pc", [P, NPAR])
        lnx = s.sb("lnx", [P, 2, PAIRS])
        kk, nrm = s.sb("kk", [P, T]), s.sb("nrm", [P, T])
        sq = s.sb("sq", [P, T])
        tw, ta, lw, Ls, Es = (s.sb(n, [P, T]) for n in ("tw", "ta", "lw", "Ls", "Es"))
        eE, eN, eL = (s.sb(n, [P, T]) for n in ("eE", "eN", "eL"))
        kd = s.sb("kd", [P, 2, T])
        bb = s.sb("bb", [P, T])
        bon, gbuf = s.sb("bon", [P, T]), s.sb("gbuf", [P, T])
        GC = s.sb("GC", [P, 2, NCH])
        QR = [s.sb(f"QR{d}", [P, NCH, 2, P]) for d in range(2)]
        KB = [s.sb(f"KB{d}", [P, NCH, 2, P]) for d in range(2)]
        Vbd = s.sb("Vbd", [P, NCH, P])
        Vtm = s.sb("Vtm", [P, NCH, P])
        RBs = [s.sb(f"RB{d}", [P, NCH, 3, P]) for d in range(2)]
        MKs = [s.sb(f"MK{d}", [P, NCH, 2, P]) for d in range(2)]
        Kt = s.sb("Kt", [P, NCH, P])
        W = s.sb("W", [P, NCH, 2, P])
        AC = s.sb("AC", [P, NCH, 2, P])
        PR = s.sb("PR", [P, NCH, 2, P])
        Tn, Tt, U = (s.sb(n, [P, NCH, P]) for n in ("Tn", "Tt", "U"))
        Sb = s.sb("Sb", [P, 2, P])
        yt = s.sb("yt", [P, T])
        fin = s.sb("fin", [P, 2, T])
        mlow = s.sb("mlow", [P, LEVELS, P])
        mup = s.sb("mup", [P, LEVELS, P])
        mg = s.sb("mg", [P, 2, 2, P])
        sum64 = s.sb("sum64", [P, P])
        mean64 = s.sb("mean64", [P, P])
        cmask = s.sb("cmask", [P, T])
        sq2 = s.sb("sq2", [P, T])
        fsqb = s.sb("fsqb", [P, T])
        bank = [s.ps(f"bank{i}") for i in range(8)]
        full = [s.sem(f"full{i}") for i in range(8)]
        free = [s.sem(f"free{i}") for i in range(8)]
        names = """masks params lora_in lora_ready in_ready pc_ready wst_ready gst_ready fin_ready kk_sq kk_norm kk_rn
            kk_done in_used logw scanned edone th ta_done exps bd_ready rb_ready mk_ready tt_ready t_ready u_ready
            tm_ready v_ready w_ready ac_ready pr_ready s_ready job_done rkk bo_copied g_copied bon_done cent fsq
            fstd frs fnorm faff fin_done vchain pchain achain wst_used held""".split()
        S = {n: s.sem(n) for n in names}
        block = ctx.enter_context(nc.Block())

        def rep(ap, n):
            a = ap.unsqueeze(1)
            return a.broadcast_to([P, n] + list(ap.shape[1:]))

        def wait_full(eng, step, pair):
            b, n = uses(step, pair)
            eng.wait_ge(full[b], n + 1)
            return bank[b]

        def now_read(ins, step, pair):
            ins.then_inc(free[uses(step, pair)[0]], 1)

        def order(d):
            return list(range(NCH)) if d == 0 else list(range(NCH - 1, -1, -1))

        @block.sync
        def _(sp):
            for n, vec in enumerate((w0[0, 0], w0[0, 1], a0[0, 0], a0[0, 1], k_k[0], k_a[0], k_a[0],
                                     r_k[0].rearrange("h n -> (h n)"))):
                sp.dma_start(par[:, :, n], columns(vec)).then_inc(S["params"], 16)
            for n, vec in enumerate((lnx_w[0], lnx_b[0])):
                sp.dma_start(lnx[:, n], columns(vec)).then_inc(S["params"], 16)
            for j in range(3):
                sp.dma_start(lo[:, j], g["lora"][j]).then_inc(S["lora_in"], 16)

            def load_pair(i):
                one = bass.ds(i, 1)
                for j in range(3):
                    sp.dma_start(inb[:, j], g["rkv"][j, one].rearrange("a p t -> (a p) t")).then_inc(S["in_ready"], 16)
                for d in range(2):
                    rows = slice(d * HD, (d + 1) * HD)
                    sp.dma_start(wst[rows, d, 0], w_up[0, d, :, bass.ds(i * P, P)]).then_inc(S["wst_ready"], 16)
                    sp.dma_start(wst[rows, d, 1], a_up[0, d, :, bass.ds(i * P, P)]).then_inc(S["wst_ready"], 16)
                sp.dma_start(gst[:], g_up[0, :, bass.ds(i * P, P)]).then_inc(S["gst_ready"], 16)

            def load_fin(i):
                one = bass.ds(i, 1)
                sp.dma_start(fin[:, 0], g["gate"][0, one].rearrange("a p t -> (a p) t")).then_inc(S["fin_ready"], 16)
                sp.dma_start(fin[:, 1], g["yb"][one].rearrange("a p t -> (a p) t")).then_inc(S["fin_ready"], 16)

            sp.wait_ge(S["masks"], 5)
            load_pair(0)
            load_fin(0)

            def trip(i):
                sp.wait_ge(S["in_used"], i + 1)
                sp.wait_ge(S["bon_done"], i + 1)
                sp.wait_ge(S["wst_used"], i + 1)
                load_pair(i + 1)
                sp.wait_ge(S["fin_done"], i + 2)
                load_fin(i + 1)
            with sp.Fori(0, PAIRS - 1) as i:
                trip(i)

        @block.gpsimd
        def _(pool):
            ch = Chain(pool, S["pchain"], S["held"])

            def keep(ap, base, pattern, mult, op=ALU.is_ge):
                ch(nc.gpsimd.affine_select(out=ap, in_=ap, compare_op=op, fill=0.0, base=base, pattern=pattern,
                                           channel_multiplier=mult))

            def same_block(ap, b, lo_half=0, half=None):
                size = 2 * b if half is None else b
                keep(ap, -lo_half, [[-2 * b, P // (2 * b)], [0, 2 * b]], 1)
                keep(ap, lo_half + size - 1, [[2 * b, P // (2 * b)], [0, 2 * b]], -1)

            def blocks(ap, b):
                return ap.rearrange("p (n c) -> p n c", c=2 * b)

            pool.sem_inc(S["job_done"], 1)
            ch(nc.gpsimd.memset(mlow[:], 0.0))
            ch(nc.gpsimd.memset(mup[:], 0.0))
            for j in range(LEVELS):
                b = 1 << j
                lowv, upv = blocks(mlow[:, j], b), blocks(mup[:, j], b)
                ch(nc.gpsimd.memset(lowv[:, :, 0:b], 1.0))
                ch(nc.gpsimd.memset(upv[:, :, b:2 * b], 1.0))
                same_block(lowv, b, b, 1)
                same_block(upv, b, 0, 1)
            for d in range(2):
                for n in range(2):
                    ch(nc.gpsimd.memset(mg[:, d, n], 1.0))
                    same_block(blocks(mg[:, d, n], HD // 2), HD // 2)
                    sign = 1 if d == 0 else -1
                    op = ALU.is_ge if (d == 0 and n == 1) else ALU.is_gt
                    keep(mg[:, d, n], 0, [[sign, P]], -sign, op)
            ch(nc.gpsimd.memset(sum64[:], 1.0))
            same_block(blocks(sum64[:], HD // 2), HD // 2)
            ch(nc.gpsimd.memset(mean64[:], 1.0 / HD))
            same_block(blocks(mean64[:], HD // 2), HD // 2)
            ch(nc.gpsimd.memset(cmask[:], 1.0))
            nc.gpsimd.memset(cmask[:].rearrange("p (n c) -> p n c", c=C)[:, :, 0:1], 0.0).then_inc(S["masks"], 1)
            nc.gpsimd.memset(wst[:], 0.0).then_inc(S["masks"], 1)
            for t in (QR[0], QR[1], KB[0], KB[1], Vbd):
                ins = nc.gpsimd.memset(t[:], 0.0)
                ch.mark(ins)
            ch.wait()
            pool.sem_inc(S["masks"], 3)

            def prep(i, d, q, first=False):
                v3 = lambda ap: ap.rearrange("p (n c) -> p n c", c=C)
                hold(pool, S["th"], q + 1, S["held"])
                if d == 1:
                    ch(nc.gpsimd.tensor_tensor(sq[:], inb[:, 0], kd[:, 0], ALU.mult))
                    ch(nc.gpsimd.tensor_scalar(sq[:], sq[:], pc[:, 7:8], None, ALU.mult))
                    pool.sem_inc(S["rkk"], 1)
                if not first:
                    hold(pool, S["exps"], q, S["held"])
                    hold(pool, S["scanned"], q, S["held"])
                nc.gpsimd.tensor_scalar(lw[:], tw[:], -DS / 2, -DS / 2, ALU.mult, ALU.add).then_inc(S["logw"], 1)
                ch.mark(nc.gpsimd.tensor_scalar(kd[:, d], ta[:], pc[:, 5:6], pc[:, 6:7], ALU.mult, ALU.add))
                ch(nc.gpsimd.tensor_scalar(bb[:], ta[:], 0.5, 0.5, ALU.mult, ALU.add))
                if d == 0:
                    hold(pool, S["kk_rn"], 4 * (i + 1), S["held"])
                    ch(nc.gpsimd.tensor_tensor(kk[:], kk[:], nrm[:], ALU.mult))
                ch.mark(nc.gpsimd.tensor_tensor(kd[:, d], kd[:, d], inb[:, 1], ALU.mult))
                ch(nc.gpsimd.tensor_tensor(bb[:], bb[:], kk[:], ALU.mult))
                hold(pool, S["scanned"], q + 1, S["held"])
                nc.gpsimd.tensor_tensor(Es[:], Ls[:], lw[:], ALU.subtract).then_inc(S["edone"], 1)
                if not first:
                    hold(pool, S["job_done"], q, S["held"])
                hold(pool, S["exps"], q + 1, S["held"])
                for h in range(2):
                    rows, cs = slice(h * HD, (h + 1) * HD), slice(h * C, (h + 1) * C)
                    eR = eL if d == 0 else eE
                    for dst, a, b in ((QR[d][rows, :, 0, cs], kk, eE), (KB[d][rows, :, 0, cs], None, eN),
                                      (KB[d][rows, :, 1, cs], bb, eN)):
                        src = kd[rows, d] if a is None else a[rows]
                        ch.mark(nc.gpsimd.tensor_tensor(dst, v3(src), v3(b[rows]), ALU.mult))
                    ch.mark(nc.gpsimd.tensor_tensor(QR[d][rows, :, 1, cs], v3(inb[rows, 0]), v3(eR[rows]), ALU.mult))
                    if d == 0:
                        ch.mark(nc.gpsimd.tensor_copy(Vbd[rows, :, cs], v3(inb[rows, 2])))
                ch.wait()
                pool.sem_inc(S["bd_ready"], 1)
                if d == 1:
                    pool.sem_inc(S["in_used"], 1)
                    hold(pool, S["bo_copied"], i + 1, S["held"])
                    ch(nc.gpsimd.tensor_tensor(bon[:], bon[:], inb[:, 2], ALU.mult))
                    pool.sem_inc(S["bon_done"], 1)

            prep(0, 0, 0, first=True)
            prep(0, 1, 1)
            with pool.Fori(0, PAIRS - 1) as i:
                ch.enter(i, 30)
                prep(i + 1, 0, 2 * i + 2)
                prep(i + 1, 1, 2 * i + 3)
                ch.leave(PAIRS - 1)

        @block.tensor
        def _(pe):
            def begin(step, pair):
                b, n = uses(step, pair)
                pe.wait_ge(free[b], n + 1)
                return bank[b]

            def end(ins, step, pair):
                ins.then_inc(full[uses(step, pair)[0]], 1)

            def mm(out, lhsT, rhs, start=True, stop=True):
                return nc.tensor.matmul(out, lhsT, rhs, start=start, stop=stop)

            def low_rank(p, d, which):
                pe.wait_ge(S["wst_ready"], 64 * (p.n + 1))
                w = 0 if which == "ZW" else 1
                end(mm(begin((which, d), p)[:], wst[:, d, w], lo[:, w]), (which, d), p)

            def norm_kk(p):
                pe.wait_ge(S["kk_sq"], p.n + 1)
                end(mm(begin(("SS", 0), p)[:], sum64[:], sq2[:]), ("SS", 0), p)

            def mean(p):
                pe.wait_ge(S["job_done"], 2 * p.n + 3)
                end(mm(begin(("MEAN",), p)[:], mean64[:], yt[:]), ("MEAN",), p)

            def variance(p):
                pe.wait_ge(S["fsq"], p.n + 1)
                end(mm(begin(("VAR",), p)[:], mean64[:], fsqb[:]), ("VAR",), p)

            def bonus_and_gate(p):
                pe.wait_ge(S["rkk"], p.n + 1)
                end(mm(begin(("BO", 1), p)[:], sum64[:], sq[:]), ("BO", 1), p)
                pe.wait_ge(S["gst_ready"], 16 * (p.n + 1))
                end(mm(begin(("G", 1), p)[:], gst[:], lo[:, 2]), ("G", 1), p)
                pe.wait_ge(full[7], uses(("G", 1), p)[1] + 1)
                pe.sem_inc(S["wst_used"], 1)

            def gram(step, p):
                which, d, X, n = step
                o = begin(step, p)
                for m in range(2):
                    c = NU * X + 2 * n + m
                    ins = mm(o[:, m * 256:(m + 1) * 256], KB[d][:, c, 1 if which == "GB" else 0],
                             QR[d][:, c].rearrange("p a t -> p (a t)"))
                end(ins, step, p)

            def turn(step, p):
                which, d, X = step
                src = {"TQ": lambda c: QR[d][:, c, 0], "TK": lambda c: KB[d][:, c, 0], "TB": lambda c: KB[d][:, c, 1],
                       "TV": lambda c: Vbd[:, c]}[which]
                o = begin(step, p)
                for u in range(NU):
                    ins = nc.tensor.transpose(o[:, u * P:(u + 1) * P], src(NU * X + u), g["ident"][:])
                end(ins, step, p)

            def fill(at, p, d, first, last):
                for step, q in fill_steps(d, p, at, first, last):
                    if step[0] in ("ZW", "ZA"):
                        low_rank(q, step[1], step[0])
                    elif step[0] in ("TQ", "TK", "TB", "TV"):
                        turn(step, q)
                    else:
                        {"SS": norm_kk, "MEAN": mean, "VAR": variance}[step[0]](q)

            for sem in free:
                pe.sem_inc(sem, 1)
            pe.wait_ge(S["masks"], 5)
            pe.wait_ge(S["lora_ready"], 2)
            zero = Pair(None, 0)
            norm_kk(zero)
            low_rank(zero, 0, "ZW")
            low_rank(zero, 0, "ZA")
            pe.wait_ge(S["bd_ready"], 1)
            for step, p in gram_steps(0, zero):
                gram(step, p)

            def job(p, d, first=False, last=False):
                J = 2 * p.n + d
                RB, MK = RBs[d], MKs[d]
                for j in range(LEVELS):
                    if j > 0:
                        for X in range(2):
                            pe.wait_ge(S["t_ready"], 10 * J + 2 * (j - 1) + X + 1)
                            o = begin(("U", d, X, j), p)
                            for u in range(NU):
                                c = NU * X + u
                                ins = mm(o[:, u * P:(u + 1) * P], RB[:, c, 0], Tn[:, c])
                            end(ins, ("U", d, X, j), p)
                        for X in range(2):
                            pe.wait_ge(S["u_ready"], 10 * J + 2 * (j - 1) + X + 1)
                            o = begin(("V", d, X, j), p)
                            for u in range(NU):
                                c = NU * X + u
                                ins = mm(o[:, u * P:(u + 1) * P], U[:, c], Tt[:, c])
                            end(ins, ("V", d, X, j), p)
                    if j < LEVELS - 1:
                        if j > 0:
                            fill(f"B{j}", p, d, first, last)
                        for X in range(2):
                            pe.wait_ge(S["tt_ready"], 12 * J + 2 * j + X + 1)
                            o = begin(("T", d, X, j), p)
                            for u in range(NU):
                                ins = nc.tensor.transpose(o[:, u * P:(u + 1) * P], Tt[:, NU * X + u], g["ident"][:])
                            end(ins, ("T", d, X, j), p)
                        fill(f"A{j}", p, d, first, last)
                pe.wait_ge(S["v_ready"], 2 * (p.n + 1))
                for X in range(2):
                    pe.wait_ge(S["mk_ready"], 4 * J + 2 * X + 2)
                    o = begin(("MV", d, X), p)
                    for u in range(NU):
                        c = NU * X + u
                        ins = mm(o[:, u * P:(u + 1) * P], MK[:, c, 0], Vtm[:, c])
                    end(ins, ("MV", d, X), p)
                if d == 0:
                    bonus_and_gate(p)
                for X, n in groups(d):
                    pe.wait_ge(S["w_ready"], 2 * J + X + 1)
                    pe.wait_ge(S["tt_ready"], 12 * J + 2 * (LEVELS - 1) + X + 1)
                    o = begin(("AC", d, X, n), p)
                    for m in range(2):
                        c = NU * X + 2 * n + m
                        ins = mm(o[:, m * 256:(m + 1) * 256], Tt[:, c], W[:, c].rearrange("p a t -> p (a t)"))
                    end(ins, ("AC", d, X, n), p)
                for k, (X, n) in enumerate(groups(d)):
                    pe.wait_ge(S["ac_ready"], 4 * J + k + 1)
                    o = begin(("PR", d, X, n), p)
                    for m in range(2):
                        c = NU * X + 2 * n + m
                        ins = mm(o[:, m * 256:(m + 1) * 256], AC[:, c, 0], RB[:, c, 1:3].rearrange("p a t -> p (a t)"))
                    end(ins, ("PR", d, X, n), p)
                grams = [] if last else gram_steps(1 - d, p if d == 0 else p.next())
                if grams:
                    pe.wait_ge(S["bd_ready"], J + 2)
                for n, c in enumerate(order(d)):
                    u = n % NU
                    if u == 0:
                        oy = begin(("Y", d, n // NU), p)
                    y = oy[:, u * P:(u + 1) * P]
                    if n < NCH - 1:
                        os_ = begin(("S", d, n), p)[:, 0:P]
                        mm(os_, Kt[:, c], Vtm[:, c], True, False)
                        ins = mm(os_, RB[:, c, 1], AC[:, c, 1], False, n == 0)
                        if n == 0:
                            end(ins, ("S", d, n), p)
                    mm(y, Vtm[:, c], MK[:, c, 1], True, False)
                    ins = mm(y, AC[:, c, 1], RB[:, c, 2], False, n == 0)
                    for step, q in grams[n:n + 1]:
                        gram(step, q)
                    if n > 0:
                        pe.wait_ge(S["s_ready"], 7 * J + n)
                        pe.wait_ge(S["pr_ready"], 4 * J + n // 2 + 1)
                        if n < NCH - 1:
                            end(mm(os_, PR[:, c, 0], Sb[:, n % 2], False, True), ("S", d, n), p)
                        ins = mm(y, Sb[:, n % 2], PR[:, c, 1], False, True)
                    if u == NU - 1:
                        end(ins, ("Y", d, n // NU), p)

            job(zero, 0, first=True)
            with pe.Fori(0, PAIRS - 1) as i:
                job(Pair(i, 0), 1)
                job(Pair(i, 1), 0)
            last = Pair(None, PAIRS - 1)
            job(last, 1, last=True)
            mean(last)
            variance(last)

        @block.scalar
        def _(act):
            ch = Chain(act, S["achain"])
            act.sem_inc(S["fin_done"], 1)
            act.wait_ge(S["lora_in"], 48)
            nc.scalar.activation(lo[:, 2], lo[:, 2], ACT.Sigmoid).then_inc(S["lora_ready"], 1)
            nc.scalar.activation(lo[:, 0], lo[:, 0], ACT.Tanh).then_inc(S["lora_ready"], 1)

            def four(ap, X):
                return ap[:, NU * X:NU * X + NU]

            def copied(step, p, dst, scale=1.0):
                o = wait_full(act, step, p)
                now_read(nc.scalar.activation(dst, o[:].rearrange("p (u t) -> p u t", u=NU), ACT.Copy, scale=scale), step, p)

            def signal(step, p, sem):
                b, n = uses(step, p)
                act.wait_ge(free[b], n + 2)
                act.sem_inc(S[sem], 1)

            def squares(p):
                act.wait_ge(S["in_ready"], 48 * (p.n + 1))
                act.wait_ge(S["pc_ready"], p.n + 1)
                ch.mark(nc.scalar.activation(kk[:], inb[:, 1], ACT.Copy, scale=pc[:, 4:5]))
                nc.scalar.activation(sq2[:], inb[:, 1], ACT.Square, scale=pc[:, 4:5]).then_inc(S["kk_sq"], 1)

            def norm_root(p):
                o = wait_full(act, ("SS", 0), p)
                now_read(nc.scalar.activation(nrm[:], o[:], ACT.Sqrt), ("SS", 0), p)
                ch.wait()
                signal(("SS", 0), p, "kk_norm")

            def tanhs(p, d):
                for step, dst, col in ((("ZW", d), tw, d), (("ZA", d), ta, 2 + d)):
                    o = wait_full(act, step, p)
                    now_read(nc.scalar.activation(dst[:], o[:], ACT.Tanh, scale=0.5, bias=pc[:, col:col + 1]), step, p)
                b, n = uses(("ZW", d), p)
                act.wait_ge(free[b], n + 2)
                signal(("ZA", d), p, "th")

            def exps(d, q):
                act.wait_ge(S["edone"], q + 1)
                ch.mark(nc.scalar.activation(eE[:], Es[:], ACT.Exp))
                ch.mark(nc.scalar.activation(eN[:], Ls[:], ACT.Exp, scale=-1.0))
                if d == 0:
                    ch(nc.scalar.activation(eL[:], Ls[:], ACT.Exp))
                v = Ls[:].rearrange("p (n c) -> p n c", c=C)
                end_ = C - 1 if d == 0 else 0
                ch(nc.scalar.activation(GC[:, d], v[:, :, end_], ACT.Exp))
                act.sem_inc(S["exps"], 1)

            def turned(at, p, d):
                dst = {"TQ": W[:, :, 0], "TK": Kt, "TB": RBs[d][:, :, 1], "TV": Vtm}
                for step, q in fill_steps(d, p, at, False, False):
                    if step[0] in dst:
                        copied(step, q, four(dst[step[0]], step[2]))
                        if step[0] == "TV":
                            signal(step, q, "v_ready")

            zero = Pair(None, 0)
            squares(zero)
            norm_root(zero)
            tanhs(zero, 0)
            exps(0, 0)

            def square_centred(p):
                act.wait_ge(S["cent"], p.n + 1)
                nc.scalar.activation(fsqb[:], yt[:], ACT.Square).then_inc(S["fsq"], 1)

            def deviation(p):
                o = wait_full(act, ("VAR",), p)
                now_read(nc.scalar.activation(fsqb[:], o[:], ACT.Sqrt, bias=g["eps"][:, 1:2]), ("VAR",), p)
                signal(("VAR",), p, "fstd")

            def affine(p):
                act.wait_ge(S["fnorm"], p.n + 1)
                one = bass.ds(p.n, 1)
                nc.scalar.activation(yt[:], yt[:], ACT.Identity, scale=lnx[:, 0, one], bias=lnx[:, 1, one]) \
                  .then_inc(S["faff"], 1)

            def job(p, d, first=False, last=False):
                if d == 1 and not last:
                    squares(p.next())
                for j in range(LEVELS - 1):
                    if j > 0:
                        turned(f"B{j}", p, d)
                    for X in range(2):
                        copied(("T", d, X, j), p, four(Tn, X))
                        signal(("T", d, X, j), p, "t_ready")
                    turned(f"A{j}", p, d)
                    if j == 0:
                        if d == 0:
                            tanhs(p, 1)
                        elif not last:
                            norm_root(p.next())
                            tanhs(p.next(), 0)
                    if j == 1 and d == 0 and not first:
                        square_centred(p.before())
                    if j == 4 and d == 0 and not first:
                        deviation(p.before())
                    if j == 3:
                        if d == 0:
                            exps(1, 2 * p.n + 1)
                        elif not last:
                            exps(0, 2 * p.n + 2)
                for X in range(2):
                    copied(("MV", d, X), p, four(W[:, :, 1], X), scale=-1.0)
                    signal(("MV", d, X), p, "w_ready")
                if d == 0 and not first:
                    affine(p.before())
                for X, n in groups(d):
                    cs = slice(NU * X + 2 * n, NU * X + 2 * n + 2)
                    o = wait_full(act, ("AC", d, X, n), p)
                    now_read(nc.scalar.activation(AC[:, cs].rearrange("p u a t -> p u (a t)"),
                                                  o[:].rearrange("p (u a) -> p u a", u=2), ACT.Copy), ("AC", d, X, n), p)
                    signal(("AC", d, X, n), p, "ac_ready")
                if d == 0:
                    act.wait_ge(S["fin_done"], p.n + 1)
                    for key, dst in (("BO", bon), ("G", gbuf)):
                        o = wait_full(act, (key, 1), p)
                        now_read(nc.scalar.activation(dst[:], o[:], ACT.Copy), (key, 1), p)
                    b, n = uses(("BO", 1), p)
                    act.wait_ge(free[b], n + 2)
                    signal(("G", 1), p, "bo_copied")
                for n, c in enumerate(order(d)[:-1]):
                    o = wait_full(act, ("S", d, n), p)
                    now_read(nc.scalar.activation(Sb[:, (n + 1) % 2], o[:, 0:P], ACT.Copy, scale=GC[:, d, c:c + 1]),
                             ("S", d, n), p)
                    signal(("S", d, n), p, "s_ready")

            job(zero, 0, first=True)
            with act.Fori(0, PAIRS - 1) as i:
                ch.enter(i, 8)
                job(Pair(i, 0), 1)
                job(Pair(i, 1), 0)
                ch.leave(PAIRS - 1)
            last = Pair(None, PAIRS - 1)
            job(last, 1, last=True)
            square_centred(last)
            deviation(last)
            affine(last)

        @block.vector
        def _(v):
            ch = Chain(v, S["vchain"])
            v.wait_ge(S["params"], 160)
            ch(nc.vector.tensor_scalar(par[:, :, 0:4], par[:, :, 0:4], 0.5, None, ALU.mult))
            ch(nc.vector.tensor_scalar(par[:, :, 5], par[:, :, 5], 0.5, None, ALU.mult))
            ch(nc.vector.tensor_scalar(par[:, :, 6], par[:, :, 5], -1.0, 1.0, ALU.mult, ALU.add))

            def signal(step, p, sem):
                b, n = uses(step, p)
                v.wait_ge(free[b], n + 2)
                v.sem_inc(S[sem], 1)

            def pick(p):
                nc.vector.tensor_copy(pc[:], par[:, bass.ds(p.n, 1), :].rearrange("p a n -> p (a n)")).then_inc(S["pc_ready"], 1)

            def kk_scale(p):
                v.wait_ge(S["kk_norm"], p.n + 1)
                ch(nc.vector.tensor_scalar(nrm[:], nrm[:], 1e-12, None, ALU.max))

            def kk_inverse(quarter):
                cs = slice(quarter * P, (quarter + 1) * P)
                nc.vector.reciprocal(nrm[:, cs], nrm[:, cs]).then_inc(S["kk_rn"], 1)

            def scan(d, q, first=False):
                v.wait_ge(S["logw"], q + 1)
                if not first:
                    v.wait_ge(S["exps"], q)
                r = slice(None) if d == 0 else slice(None, None, -1)
                nc.vector.tensor_tensor_scan(Ls[:, r], cmask[:], lw[:, r], 0.0, ALU.mult, ALU.add).then_inc(S["scanned"], 1)

            def gram_read(step, p):
                which, d, X, n = step
                cs = slice(NU * X + 2 * n, NU * X + 2 * n + 2)
                o = wait_full(v, step, p)
                if which == "GB":
                    for h in range(2):
                        ins = nc.vector.tensor_tensor(RBs[d][:, cs, 2 * h],
                                                      o[:].rearrange("p (u a t) -> p u a t", u=2, a=2)[:, :, h],
                                                      rep(mg[:, d, h], 2), ALU.mult)
                        if h == 0:
                            ch.mark(ins)
                    now_read(ins, step, p)
                else:
                    ins = nc.vector.tensor_tensor(MKs[d][:, cs].rearrange("p u a t -> p u (a t)"),
                                                  o[:].rearrange("p (u a) -> p u a", u=2),
                                                  rep(mg[:, d].rearrange("p a t -> p (a t)"), 2), ALU.mult)
                    now_read(ins, step, p)
                    signal(step, p, "mk_ready")

            def inverse_start(p, d):
                m1t = mup if d == 0 else mlow
                b, n = uses(("GB", d, 1, 1), p)
                v.wait_ge(free[b], n + 2)
                ch.wait()
                for X in range(2):
                    cs = slice(NU * X, NU * X + NU)
                    ch.mark(nc.vector.tensor_tensor(Tt[:, cs], RBs[d][:, cs, 0], rep(m1t[:, 0], NU), ALU.mult))
                ch.wait()
                for X in range(2):
                    cs = slice(NU * X, NU * X + NU)
                    nc.vector.tensor_tensor(Tt[:, cs], rep(g["ident"][:], NU), Tt[:, cs], ALU.subtract) \
                      .then_inc(S["tt_ready"], 1)

            def centre(p):
                o = wait_full(v, ("MEAN",), p)
                now_read(nc.vector.tensor_tensor(yt[:], yt[:], o[:], ALU.subtract), ("MEAN",), p)
                signal(("MEAN",), p, "cent")

            def normalize(p):
                v.wait_ge(S["fstd"], p.n + 1)
                ch(nc.vector.reciprocal(fsqb[:], fsqb[:]))
                nc.vector.tensor_tensor(yt[:], yt[:], fsqb[:], ALU.mult).then_inc(S["fnorm"], 1)

            def merge(p):
                v.wait_ge(S["faff"], p.n + 1)
                v.wait_ge(S["bon_done"], p.n + 1)
                ch(nc.vector.tensor_tensor(yt[:], yt[:], bon[:], ALU.add))
                ch(nc.vector.tensor_tensor(yt[:], yt[:], gbuf[:], ALU.mult))
                v.wait_ge(S["fin_ready"], 32 * (p.n + 1))
                ch(nc.vector.tensor_tensor(yt[:], yt[:], fin[:, 0], ALU.mult))
                nc.vector.tensor_tensor(g["u1T"][:, bass.ds(p.n, 1), :].rearrange("p a t -> p (a t)"), yt[:], fin[:, 1],
                                        ALU.add).then_inc(S["fin_done"], 1)
                v.wait_ge(S["fin_done"], p.n + 2)

            zero = Pair(None, 0)
            pick(zero)
            v.wait_ge(S["masks"], 5)
            kk_scale(zero)
            for quarter in range(4):
                kk_inverse(quarter)
            scan(0, 0, first=True)
            for step, p in gram_steps(0, zero):
                gram_read(step, p)
                if step[1:] == (0, 1, 1) and step[0] == "GB":
                    inverse_start(zero, 0)

            def job(p, d, first=False, last=False):
                mj = mlow if d == 0 else mup
                if d == 1 and not last:
                    v.wait_ge(S["bon_done"], p.n + 1)
                    pick(p.next())
                for j in range(1, LEVELS):
                    for X in range(2):
                        cs = slice(NU * X, NU * X + NU)
                        o = wait_full(v, ("U", d, X, j), p)
                        ins = nc.vector.tensor_tensor(U[:, cs], o[:].rearrange("p (u t) -> p u t", u=NU),
                                                      rep(mj[:, j], NU), ALU.mult)
                        now_read(ins, ("U", d, X, j), p)
                        signal(("U", d, X, j), p, "u_ready")
                    if j in (2, 3) and d == 1 and not last:
                        kk_inverse(1 if j == 2 else 3)
                    if j == 1 and d == 0 and not first:
                        centre(p.before())
                    for X in range(2):
                        cs = slice(NU * X, NU * X + NU)
                        o = wait_full(v, ("V", d, X, j), p)
                        ins = nc.vector.tensor_tensor(Tt[:, cs], Tt[:, cs], o[:].rearrange("p (u t) -> p u t", u=NU),
                                                      ALU.subtract)
                        now_read(ins, ("V", d, X, j), p)
                        signal(("V", d, X, j), p, "tt_ready")
                    if j == 1:
                        if d == 0:
                            scan(1, 2 * p.n + 1)
                        elif not last:
                            kk_scale(p.next())
                            kk_inverse(0)
                            scan(0, 2 * p.n + 2)
                    if j == 2 and d == 1 and not last:
                        kk_inverse(2)
                if d == 0 and not first:
                    normalize(p.before())
                    merge(p.before())
                for X, n in groups(d):
                    cs = slice(NU * X + 2 * n, NU * X + 2 * n + 2)
                    o = wait_full(v, ("PR", d, X, n), p)
                    o4 = o[:].rearrange("p (u a t) -> p u a t", u=2, a=2)
                    ch.mark(nc.vector.tensor_tensor(PR[:, cs, 0], rep(g["ident"][:], 2), o4[:, :, 0], ALU.subtract))
                    ins = nc.vector.tensor_tensor(PR[:, cs, 1], QR[d][:, cs, 1], o4[:, :, 1], ALU.subtract)
                    now_read(ins, ("PR", d, X, n), p)
                    ch.wait()
                    signal(("PR", d, X, n), p, "pr_ready")
                grams = [] if last else gram_steps(1 - d, p if d == 0 else p.next())
                for n in range(NCH):
                    for step, q in grams[n:n + 1]:
                        gram_read(step, q)
                        if n == 3:
                            inverse_start(q, 1 - d)
                    if n % NU < NU - 1:
                        continue
                    half = n // NU
                    o = wait_full(v, ("Y", d, half), p)
                    o4 = o[:].rearrange("p (u a) -> p u a", u=NU)
                    cs = order(d)[NU * half:NU * half + NU]
                    for h in range(2):
                        rows, fs = slice(h * HD, (h + 1) * HD), slice(h * C, (h + 1) * C)
                        y3 = yt[rows].rearrange("p (n c) -> p n c", c=C)
                        y3 = y3[:, cs[0]:cs[-1] + 1] if d == 0 else y3[:, cs[-1]:cs[0] + 1][:, ::-1]
                        src = o4[rows, :, fs]
                        ins = (nc.vector.tensor_copy(y3, src) if d == 0 else
                               nc.vector.tensor_tensor(y3, y3, src, ALU.add))
                        if h == 0:
                            ch.mark(ins)
                    now_read(ins, ("Y", d, half), p)
                    b, m = uses(("Y", d, half), p)
                    v.wait_ge(free[b], m + 2)
                ch.wait()
                v.sem_inc(S["job_done"], 1)

            job(zero, 0, first=True)
            with v.Fori(0, PAIRS - 1) as i:
                ch.enter(i, 29)
                job(Pair(i, 0), 1)
                job(Pair(i, 1), 0)
                ch.leave(PAIRS - 1)
            last = Pair(None, PAIRS - 1)
            job(last, 1, last=True)
            centre(last)
            normalize(last)
            merge(last)


E = 64
F_EXP = 256
GROUPS, PER_GROUP = 8, 8
TOP_GROUPS, TOP_K = 4, 8
ROUTED_SCALE = 2.5
ALPHA = 2.0 ** 0.25
ROWS = T + P
MAX_BLOCKS = (T * TOP_K - E) // P + E
SLOTS = 3
AHEAD = 2
TRIPS = -(-MAX_BLOCKS // SLOTS)
NBT = SLOTS * TRIPS + AHEAD
BIG = 1e30
N_CONSTS = 6 + SLOTS
NO_ROW = 65536


def row_of(vec):
    return vec.partition_broadcast(P)


def mix_and_route(nc, g, x, w_o, ln1_w, ln1_b, router_w, router_b, sh_gate, sh_up, sh_down):
    with ExitStack() as ctx:
        s = Scope(nc, ctx, "mix")
        wo = s.sb("wo", [P, KC, D])
        rows = s.sb("rows", [P, 5, D])
        xs = s.sb("x", [P, TT, D])
        u2T = s.sb("u2T", [P, KC, T])
        tmp = s.sb("tmp", [P, D])
        st = s.sb("st", [P, 2, 6])
        mv = s.sb("mv", [P, 2])
        rstd = s.sb("rstd", [P, 2 * TT])
        zrow = s.sb("zrow", [P, D])
        rw = s.sb("rw", [P, KC, E])
        rb = s.sb("rb", [P, E])
        shw = s.sb("shw", [P, KC, 2, F_EXP])
        shd = s.sb("shd", [P, 2, D])
        hT = s.sb("hT", [P, 2, T])
        hs = s.sb("hs", [P, 2, T])
        yo = s.sb("yo", [P, TT, D])
        sc = s.sb("sc", [P, TT, E])
        sel = s.sb("sel", [P, TT, E])
        m8 = s.sb("m8", [P, TT, GROUPS, 8])
        gsx = s.sb("gsx", [P, TT, 12])
        t8 = s.sb("t8", [P, TT, 8])
        gr = s.sb("gr", [P, TT, 12])
        er = s.sb("er", [P, TT, E])
        A = s.sb("A", [P, TT, E])
        wgt = s.sb("wgt", [P, TT, E])
        ws = s.sb("ws", [P, TT])
        ones = s.sb("ones", [P, P])
        before = s.sb("before", [P, P])
        upto = s.sb("upto", [P, P])
        iob = s.sb("iob", [E, NBT])
        cnt = s.sb("cnt", [E, 4])
        nb = s.sb("nb", [E, 1])
        nbr = s.sb("nbr", [E, P])
        M = s.sb("M", [E, NBT])
        ci = s.sb("ci", [E, 1])
        bank = [s.ps(f"bank{i}") for i in range(8)]
        (wo_in, x_in, rows_in, sh_in, mixed, mix_read, var1, std1, u2_ready, tp_done, tp_read, u2_out, z_ready, z_out,
         rt_in, h_done, gate_read, up_read, y_done, y_read, y_out, sh_silu, logit, score, sel_done, dve, consts, a_ready,
         pos_done, pos_read, cnt_done, nb_ready, ci_done, m_ready, eb_done, x1_out, pc, acc_sem, row1) = (s.sem(n) for n in (
             """wo_in x_in rows_in sh_in mixed mix_read var1 std1 u2_ready tp_done tp_read u2_out z_ready z_out
         rt_in h_done gate_read up_read y_done y_read y_out sh_silu logit score sel_done dve consts a_ready
         pos_done pos_read cnt_done nb_ready ci_done m_ready eb_done x1_out pc acc_sem row1""").split())
        block = ctx.enter_context(nc.Block())

        @block.sync
        def _(sp):
            sp.dma_start(wo[:], w_o[0].rearrange("(k p) n -> p k n", p=P)).then_inc(wo_in, 16)
            sp.dma_start(xs[:], x[0].rearrange("(n p) d -> p n d", p=P)).then_inc(x_in, 16)
            mod = g["mod"][0]
            for n, vec in enumerate((mod[2 * D:3 * D], ln1_w[0], ln1_b[0], mod[4 * D:5 * D], mod[3 * D:4 * D])):
                sp.dma_start(rows[:, n], row_of(vec)).then_inc(rows_in, 16)
            sp.dma_start(rw[:], router_w[0].rearrange("(k p) n -> p k n", p=P)).then_inc(rt_in, 16)
            sp.dma_start(rb[:], row_of(router_b[0])).then_inc(rt_in, 16)
            sp.dma_start(shw[:, :, 0], sh_gate[0].rearrange("(k p) n -> p k n", p=P)).then_inc(sh_in, 16)
            sp.dma_start(shw[:, :, 1], sh_up[0].rearrange("(k p) n -> p k n", p=P)).then_inc(sh_in, 16)
            sp.dma_start(shd[:], sh_down[0].rearrange("(c p) n -> p c n", p=P)).then_inc(sh_in, 16)
            sp.wait_ge(z_ready, 1)
            sp.dma_start(g["u2d"][T:ROWS], zrow[:]).then_inc(z_out, 16)
            sp.dma_start(g["acc"][T:ROWS], zrow[:]).then_inc(z_out, 16)
            for t in range(TT):
                sp.wait_ge(u2_ready, t + 1)
                sp.dma_start(g["u2d"][t * P:(t + 1) * P], xs[:, t]).then_inc(u2_out, 16)
            for t in range(TT):
                sp.wait_ge(y_read, 2 * t + 2)
                sp.dma_start(g["acc"][t * P:(t + 1) * P], yo[:, t]).then_inc(y_out, 16)
            sp.wait_ge(z_out, 32)
            sp.wait_ge(u2_out, 16 * TT)
            sp.wait_ge(y_out, 16 * TT)

        @block.gpsimd
        def _(pool):
            nc.gpsimd.memset(zrow[:], 0.0).then_inc(z_ready, 1)
            nc.gpsimd.memset(ones[:], 1.0).then_inc(pc, 1)
            nc.gpsimd.memset(before[:], 1.0).then_inc(pc, 1)
            nc.gpsimd.memset(upto[:], 1.0).then_inc(pc, 1)
            nc.gpsimd.memset(gsx[:], BIG).then_inc(pc, 1)
            pool.wait_ge(pc, 4)
            nc.gpsimd.affine_select(out=before[:], in_=before[:], compare_op=ALU.is_gt, fill=0.0, base=0,
                                    pattern=[[1, P]], channel_multiplier=-1).then_inc(consts, 1)
            nc.gpsimd.affine_select(out=upto[:], in_=upto[:], compare_op=ALU.is_ge, fill=0.0, base=0,
                                    pattern=[[1, P]], channel_multiplier=-1).then_inc(consts, 1)
            nc.gpsimd.iota(iob[:], pattern=[[1, NBT]], base=0, channel_multiplier=0,
                           allow_small_or_imprecise_dtypes=True).then_inc(consts, 1)
            nc.gpsimd.iota(g["place"][:], pattern=[[0, TT], [1, P]], base=1, channel_multiplier=0,
                           allow_small_or_imprecise_dtypes=True).then_inc(consts, 1)
            for b in range(SLOTS):
                nc.gpsimd.iota(g["rhs"][:, b, :, 0], pattern=[[P, TT]], base=1, channel_multiplier=1,
                               allow_small_or_imprecise_dtypes=True).then_inc(consts, 1)
            nc.gpsimd.iota(g["spare"][:, 0:1], pattern=[[0, 1]], base=T, channel_multiplier=1,
                           allow_small_or_imprecise_dtypes=True).then_inc(consts, 1)
            nc.gpsimd.iota(g["spare"][:, 1:2], pattern=[[0, 1]], base=-(T + 1), channel_multiplier=-1,
                           allow_small_or_imprecise_dtypes=True).then_inc(consts, 1)

        @block.tensor
        def _(pe):
            pe.wait_ge(wo_in, 16)
            for t in range(TT):
                for h in range(2):
                    for k in range(KC):
                        ins = nc.tensor.matmul(bank[2 * t + h][:], g["u1T"][:, k, t * P:(t + 1) * P],
                                               wo[:, k, h * 512:(h + 1) * 512], start=(k == 0), stop=(k == KC - 1))
                ins.then_inc(mixed, 1)
            pe.wait_ge(mix_read, 2 * TT)
            for t in range(TT):
                pe.wait_ge(u2_ready, t + 1)
                for h in range(2):
                    n = 2 * t + h
                    if n >= 2:
                        pe.wait_ge(tp_read, n - 1)
                    for k in range(4):
                        ins = nc.tensor.transpose(bank[n % 2][:, k * P:(k + 1) * P], xs[:, t, (4 * h + k) * P:(4 * h + k + 1) * P],
                                                  g["ident"][:])
                    ins.then_inc(tp_done, 1)
            pe.wait_ge(tp_read, 2 * TT)
            pe.wait_ge(rt_in, 32)
            for t in range(TT):
                for k in range(KC):
                    ins = nc.tensor.matmul(bank[2][:, t * E:(t + 1) * E], u2T[:, k, t * P:(t + 1) * P], rw[:, k],
                                           start=(k == 0), stop=(k == KC - 1))
                ins.then_inc(logit, 1)
            pe.wait_ge(sh_in, 48)
            for f in range(2):
                for w in range(2):
                    for k in range(KC):
                        ins = nc.tensor.matmul(bank[4 + 2 * f + w][:], shw[:, k, w, f * P:(f + 1) * P], u2T[:, k],
                                               start=(k == 0), stop=(k == KC - 1))
                    ins.then_inc(h_done, 1)
            pe.wait_ge(up_read, 2)
            for t in range(TT):
                for h in range(2):
                    n = 2 * t + h
                    if n >= 2:
                        pe.wait_ge(y_read, n - 1)
                    for f in range(2):
                        ins = nc.tensor.matmul(bank[n % 2][:], hT[:, f, t * P:(t + 1) * P], shd[:, f, h * 512:(h + 1) * 512],
                                               start=(f == 0), stop=(f == 1))
                    ins.then_inc(y_done, 1)
            pe.wait_ge(consts, N_CONSTS)
            pe.wait_ge(a_ready, TT)
            for t in range(TT):
                o = bank[3][:, t * E:(t + 1) * E]
                for i in range(t):
                    nc.tensor.matmul(o, ones[:], A[:, i], start=(i == 0), stop=False)
                nc.tensor.matmul(o, before[:], A[:, t], start=(t == 0), stop=True).then_inc(pos_done, 1)
            for t in range(TT):
                ins = nc.tensor.matmul(bank[2][0:E, 0:1], A[:, t], ones[:, 0:1], start=(t == 0), stop=(t == TT - 1))
            ins.then_inc(cnt_done, 1)
            pe.wait_ge(nb_ready, 1)
            nc.tensor.matmul(bank[4][0:E, 0:1], upto[0:E, 0:E], nb[:], start=True, stop=True).then_inc(ci_done, 1)
            pe.wait_ge(m_ready, 1)
            nc.tensor.matmul(bank[5][:, 0:NBT], ones[0:E], M[:], start=True, stop=True)
            nc.tensor.matmul(bank[6][:, 0:NBT], nbr[:], M[:], start=True, stop=True)
            nc.tensor.matmul(bank[7][:, 0:1], nbr[:], ones[0:E, 0:1], start=True, stop=True).then_inc(eb_done, 1)

        @block.scalar
        def _(act):
            for n in range(2 * TT):
                act.wait_ge(var1, n + 1)
                nc.scalar.activation(rstd[:, n:n + 1], mv[:, 1:2], ACT.Sqrt, bias=g["eps"][:, 0:1]).then_inc(std1, 1)
            for t in range(TT):
                act.wait_ge(logit, TT)
                nc.scalar.activation(sc[:, t], bank[2][:, t * E:(t + 1) * E], ACT.Sigmoid).then_inc(score, 1)
            for f in range(2):
                act.wait_ge(h_done, 2 * f + 1)
                nc.scalar.activation(hs[:, f], bank[4 + 2 * f][:], ACT.Silu).then_inc(sh_silu, 1)
            for n in range(2 * TT):
                act.wait_ge(y_done, n + 1)
                nc.scalar.activation(yo[:, n // 2, (n % 2) * 512:(n % 2 + 1) * 512], bank[n % 2][:], ACT.Copy) \
                   .then_inc(y_read, 1)

        @block.vector
        def _(v):
            ch = Chain(v, dve)
            v.wait_ge(rows_in, 80)
            ch.mark(nc.vector.tensor_scalar(rows[:, 0], rows[:, 0], 1.0, None, ALU.add))
            ch(nc.vector.tensor_scalar(rows[:, 3], rows[:, 3], 1.0, None, ALU.add))
            v.wait_ge(x_in, 16)

            def norm(t, src, dst, w, b, n, done):
                for h in range(2):
                    ch.mark(nc.vector.bn_stats(st[:, h], src[:, h * 512:(h + 1) * 512]))
                ch.wait()
                nc.vector.bn_aggr(mv[:], st[:]).then_inc(var1, 1)
                v.wait_ge(std1, n + 1)
                ch(nc.vector.reciprocal(rstd[:, n:n + 1], rstd[:, n:n + 1]))
                ch(nc.vector.tensor_scalar(tmp[:], src, mv[:, 0:1], rstd[:, n:n + 1], ALU.subtract, ALU.mult))
                ch(nc.vector.tensor_tensor(tmp[:], tmp[:], rows[:, w], ALU.mult))
                ins = nc.vector.tensor_tensor(dst, tmp[:], rows[:, b], ALU.add)
                if done is None:
                    ch(ins)
                else:
                    ins.then_inc(done, 1)

            for t in range(TT):
                v.wait_ge(mixed, t + 1)
                for h in range(2):
                    hs_ = slice(h * 512, (h + 1) * 512)
                    nc.vector.tensor_tensor(tmp[:, hs_], bank[2 * t + h][:], rows[:, 0, hs_], ALU.mult).then_inc(mix_read, 1)
                v.wait_ge(mix_read, 2 * t + 2)
                ch(nc.vector.scalar_tensor_tensor(tmp[:], xs[:, t], ALPHA, tmp[:], ALU.mult, ALU.add))
                ch(nc.vector.tensor_copy(xs[:, t], tmp[:]))
                norm(t, xs[:, t], g["x1"][:, t], 1, 2, 2 * t, None)
                norm(t, g["x1"][:, t], xs[:, t], 3, 4, 2 * t + 1, u2_ready)
                v.wait_ge(u2_ready, t + 1)
            for n in range(2 * TT):
                t, h = n // 2, n % 2
                v.wait_ge(tp_done, n + 1)
                nc.vector.tensor_copy(u2T[:, 4 * h:4 * h + 4, t * P:(t + 1) * P],
                                      bank[n % 2][:].rearrange("p (k t) -> p k t", k=4)).then_inc(tp_read, 1)
            v.wait_ge(rt_in, 32)
            v.wait_ge(consts, N_CONSTS)
            for t in range(TT):
                v.wait_ge(score, t + 1)
                ch(nc.vector.tensor_tensor(sel[:, t], sc[:, t], rb[:], ALU.add))
                for q in range(GROUPS):
                    ch.mark(nc.vector.max(m8[:, t, q], sel[:, t, q * PER_GROUP:(q + 1) * PER_GROUP]))
                ch.wait()
                ch(nc.vector.tensor_tensor(gsx[:, t, 4:12], m8[:, t, :, 0], m8[:, t, :, 1], ALU.add))
                ch(nc.vector.max(t8[:, t], gsx[:, t]))
                ch(nc.vector.match_replace(gr[:, t], t8[:, t], gsx[:, t], -BIG))
                ch(nc.vector.tensor_scalar(gr[:, t], gr[:, t], -BIG / 2, -BIG, ALU.is_gt, ALU.mult))
                gv = gr[:, t, 4:12].unsqueeze(2).broadcast_to([P, GROUPS, PER_GROUP])
                ch(nc.vector.tensor_tensor(sel[:, t].rearrange("p (q n) -> p q n", q=GROUPS),
                                           sel[:, t].rearrange("p (q n) -> p q n", q=GROUPS), gv, ALU.add))
                ch(nc.vector.max(t8[:, t], sel[:, t]))
                ch(nc.vector.match_replace(er[:, t], t8[:, t], sel[:, t], -3e38))
                ch(nc.vector.tensor_scalar(A[:, t], er[:, t], -2e38, None, ALU.is_lt))
                v.sem_inc(a_ready, 1)
                ch(nc.vector.tensor_tensor(wgt[:, t], sc[:, t], A[:, t], ALU.mult))
                ch(nc.vector.tensor_reduce(ws[:, t:t + 1], wgt[:, t], AX_X, ALU.add))
                ch(nc.vector.reciprocal(ws[:, t:t + 1], ws[:, t:t + 1]))
                ch(nc.vector.tensor_scalar(g["pg"][:, :, t, 1], wgt[:, t], ws[:, t:t + 1], ROUTED_SCALE, ALU.mult, ALU.mult))
                if t < 2:
                    v.wait_ge(h_done, 2 * t + 2)
                    v.wait_ge(sh_silu, t + 1)
                    nc.vector.tensor_tensor(hT[:, t], hs[:, t], bank[5 + 2 * t][:], ALU.mult).then_inc(up_read, 1)
            for t in range(TT):
                v.wait_ge(pos_done, TT)
                nc.vector.scalar_tensor_tensor(g["pg"][:, :, t, 0], bank[3][:, t * E:(t + 1) * E], 1.0, A[:, t],
                                               ALU.add, ALU.mult).then_inc(pos_read, 1)
            v.wait_ge(cnt_done, 1)
            for j in range(4):
                ch.mark(nc.vector.tensor_scalar(cnt[:, j:j + 1], bank[2][0:E, 0:1], float(P * j), None, ALU.is_gt))
            ch.wait()
            ch(nc.vector.tensor_reduce(nb[:], cnt[:], AX_X, ALU.add))
            v.sem_inc(nb_ready, 1)
            v.wait_ge(ci_done, 1)
            ch(nc.vector.tensor_copy(ci[:], bank[4][0:E, 0:1]))
            ch.mark(nc.vector.tensor_scalar(M[:], iob[:], ci[:], None, ALU.is_ge))
            ch(nc.vector.tensor_scalar(nbr[:], ones[0:E], nb[:], None, ALU.mult))
            v.sem_inc(m_ready, 1)
            v.wait_ge(eb_done, 1)
            ch.mark(nc.vector.tensor_scalar(g["table"][0:1, 0:NBT], bank[5][0:1, 0:NBT], float(E - 1), None, ALU.min))
            ch.mark(nc.vector.tensor_copy(g["table"][0:1, NBT:NBT + 1], bank[7][0:1, 0:1]))
            ch(nc.vector.tensor_copy(g["c0"][:], bank[6][:, 0:NBT]))
            ch(nc.vector.tensor_tensor(g["c0"][:], g["place"][:, 0, 0:NBT], g["c0"][:], ALU.subtract))
            ch(nc.vector.tensor_scalar(g["c0"][:], g["c0"][:], float(P), -float(P), ALU.mult, ALU.add))


def moe(nc, g, exp_gate, exp_up, exp_down):
    with ExitStack() as ctx:
        s = Scope(nc, ctx, "moe")
        wg = [s.sb(f"wg{p}", [P, KC, 2, F_EXP]) for p in range(SLOTS)]
        wd = [s.sb(f"wd{p}", [P, 2, D]) for p in range(SLOTS)]
        xg = [s.sb(f"xg{p}", [P, D]) for p in range(SLOTS)]
        xT = s.sb("xT", [P, KC, P])
        S_ = s.sb("S", [P, TT, P])
        pos = s.sb("pos", [P, TT])
        hs, hm = s.sb("hs", [P, F_EXP]), s.sb("hm", [P, F_EXP])
        hT = s.sb("hT", [P, 2, P])
        y = [s.sb(f"y{p}", [P, D]) for p in range(SLOTS)]
        val = s.sb("val", [P, 2])
        occ = s.sb("occ", [P, 1])
        row = s.sb("row", [P, 1])
        idx = [s.sb(f"idx{p}", [P, 1], I32) for p in range(SLOTS)]
        sidx = [s.sb(f"sidx{p}", [P, 1], I32) for p in range(SLOTS)]
        gcol = [s.sb(f"gcol{p}", [P, 1]) for p in range(SLOTS)]
        fetch = s.sb("fetch", [P, 1])
        pH = s.ps("pH")
        pX = [s.ps(f"pX{h}") for h in range(2)]
        pY = [s.ps(f"pY{h}") for h in range(2)]
        pT, pI = s.ps("pT"), s.ps("pI")
        wg_in = [s.sem(f"wg_in{p}") for p in range(SLOTS)]
        wu_in = [s.sem(f"wu_in{p}") for p in range(SLOTS)]
        wd_in = [s.sem(f"wd_in{p}") for p in range(SLOTS)]
        gathered = [s.sem(f"gathered{p}") for p in range(SLOTS)]
        h_done = [s.sem(f"h_done{p}") for p in range(SLOTS)]
        d_done = [s.sem(f"d_done{p}") for p in range(SLOTS)]
        (s_built, i_done, i_ready, x_zero, x_turned, x_read, silu_done, hm_done, h_turned, h_read,
         y0_read, y1_read, dch, held) = (s.sem(n) for n in (
             "s_built i_done i_ready x_zero x_turned x_read silu_done hm_done h_turned h_read "
             "y0_read y1_read dch held").split())
        y_free = [s.sem(f"y_free{p}") for p in range(SLOTS)]
        added = s.sem("added")
        block = ctx.enter_context(nc.Block())

        def blocks(eng, body):
            n_blocks = eng.value_load(g["table"][0:1, NBT:NBT + 1], min_val=1, max_val=MAX_BLOCKS)
            with eng.Fori(0, TRIPS) as i:
                with eng.If(SLOTS * i < n_blocks):
                    body(SLOTS * i, 0, i)
                    for p in range(1, SLOTS):
                        with eng.If(SLOTS * i + p < n_blocks):
                            body(SLOTS * i + p, p, i)
            return n_blocks

        def expert(eng, b):
            return bass.ds(eng.value_load(g["table"][0:1, bass.ds(b, 1)], min_val=0, max_val=E - 1), 1)

        @block.sync
        def _(sp):
            def body(b, p, i):
                e = expert(sp, b)
                sp.wait_ge(h_done[p], i + 1)
                sp.dma_start(wg[p][:, :, 0], exp_gate[0, e].rearrange("a (p k) f -> p (a k) f", p=P)).then_inc(wg_in[p], 16)
                sp.dma_start(wg[p][:, :, 1], exp_up[0, e].rearrange("a (p k) f -> p (a k) f", p=P)).then_inc(wu_in[p], 16)
                sp.wait_ge(d_done[p], 2 * i + 1)
                sp.dma_start(wd[p][:], exp_down[0, e].rearrange("a (p c) d -> p (a c) d", p=P)).then_inc(wd_in[p], 16)
            blocks(sp, body)

        @block.gpsimd
        def _(pool):
            def gather(b, q):
                hold(pool, i_ready, b + 1, held)
                pool.indirect_dma_start(out=xg[q][:], out_offset=None, in_=g["u2d"][:],
                                        in_offset=bass.IndirectOffsetOnAxis(ap=idx[q][:, 0:1], axis=0),
                                        bounds_check=ROWS - 1, oob_is_err=False).then_inc(gathered[q], 16)

            for q in range(SLOTS):
                nc.gpsimd.memset(xg[q][:], 0.0).then_inc(x_zero, 1)
            pool.wait_ge(x_zero, SLOTS)
            for q in range(AHEAD):
                gather(q, q)

            def body(b, p, i):
                hold(pool, x_turned, 2 * b + 2, held)
                gather(b + AHEAD, (p + AHEAD) % SLOTS)
                hold(pool, y0_read, b + 2, held)
                hold(pool, y1_read, b + 2, held)
                pool.indirect_dma_start(out=g["acc"][:], out_offset=bass.IndirectOffsetOnAxis(ap=sidx[p][:, 0:1], axis=0),
                                        in_=y[p][:], in_offset=None, bounds_check=ROWS - 1, compute_op=ALU.add) \
                    .then_inc(added, 16)
                hold(pool, added, 16 * (b + 1), held)
                pool.sem_inc(y_free[p], 1)
            n = blocks(pool, body)
            for q in range(SLOTS):
                pool.wait_ge(gathered[q], 16 * ((n + AHEAD + SLOTS - 1 - q) // SLOTS))

        @block.tensor
        def _(pe):
            def indices(b, q):
                pe.wait_ge(s_built, b + 1)
                for t in range(TT):
                    ins = nc.tensor.matmul(pI[:, 2 * q:2 * q + 2], S_[:, t], g["rhs"][:, q, t], start=(t == 0), stop=(t == TT - 1))
                ins.then_inc(i_done, 1)

            def turn_x(b, q, n, h, first=False):
                pe.wait_ge(gathered[q], 16 * (n + 1))
                if not first:
                    pe.wait_ge(x_read, 2 * b + h - 1)
                x3 = xg[q][:].rearrange("t (p k) -> t k p", k=KC)
                for k in range(4):
                    ins = nc.tensor.transpose(pX[h][:, k * P:(k + 1) * P], x3[:, 4 * h + k], g["ident"][:])
                ins.then_inc(x_turned, 1)

            for sem in (*h_done, *d_done, *y_free, y0_read, y1_read):
                pe.sem_inc(sem, 1)
            for q in range(AHEAD):
                indices(q, q)
            for h in range(2):
                turn_x(0, 0, 0, h, first=True)
            hm3 = hm[:].rearrange("t (p c) -> t c p", c=2)

            def body(b, p, i):
                pe.wait_ge(x_read, 2 * b + 2)
                pe.wait_ge(wg_in[p], 16 * (i + 1))
                pe.wait_ge(wu_in[p], 16 * (i + 1))
                for k in range(KC):
                    ins = nc.tensor.matmul(pH[:], xT[:, k], wg[p][:, k].rearrange("p w f -> p (w f)"),
                                           start=(k == 0), stop=(k == KC - 1))
                ins.then_inc(h_done[p], 1)
                after = (p + 1) % SLOTS, i + (p + 1) // SLOTS
                turn_x(b + 1, *after, 0)
                pe.wait_ge(hm_done, b + 1)
                for f in range(2):
                    ins = nc.tensor.transpose(pT[:, f * P:(f + 1) * P], hm3[:, f], g["ident"][:])
                ins.then_inc(h_turned, 1)
                indices(b + AHEAD, (p + AHEAD) % SLOTS)
                turn_x(b + 1, *after, 1)
                pe.wait_ge(h_read, b + 1)
                pe.wait_ge(wd_in[p], 16 * (i + 1))
                for h, used in ((0, y0_read), (1, y1_read)):
                    pe.wait_ge(used, b + 1)
                    for f in range(2):
                        ins = nc.tensor.matmul(pY[h][:], hT[:, f], wd[p][:, f, h * 512:(h + 1) * 512], start=(f == 0), stop=(f == 1))
                    ins.then_inc(d_done[p], 1)
            blocks(pe, body)

        @block.scalar
        def _(act):
            def read_x(b, h):
                act.wait_ge(x_turned, 2 * b + h + 1)
                nc.scalar.activation(xT[:, 4 * h:4 * h + 4], pX[h][:].rearrange("p (k t) -> p k t", k=4), ACT.Copy) \
                   .then_inc(x_read, 1)
            for h in range(2):
                read_x(0, h)

            def body(b, p, i):
                act.wait_ge(h_done[p], i + 2)
                nc.scalar.activation(hs[:], pH[:, 0:F_EXP], ACT.Silu).then_inc(silu_done, 1)
                read_x(b + 1, 0)
                act.wait_ge(h_turned, b + 1)
                nc.scalar.activation(hT[:], pT[:, 0:2 * P].rearrange("p (f t) -> p f t", f=2), ACT.Copy).then_inc(h_read, 1)
                read_x(b + 1, 1)
                act.wait_ge(d_done[p], 2 * i + 2)
                act.wait_ge(i_ready, b + 1)
                act.wait_ge(y_free[p], i + 1)
                nc.scalar.activation(y[p][:, 0:512], pY[0][:], ACT.Copy, scale=gcol[p][:, 0:1]).then_inc(y0_read, 1)
            blocks(act, body)

        @block.vector
        def _(v):
            ch = Chain(v, dch)

            def match(b, q):
                e = expert(v, b)
                ch.mark(nc.vector.tensor_copy(g["rhs"][:, q, :, 1], g["pg"][:, e, :, 1].rearrange("p a t -> p (a t)")))
                ch(nc.vector.tensor_scalar(pos[:], g["pg"][:, e, :, 0].rearrange("p a t -> p (a t)"),
                                           g["c0"][:, bass.ds(b, 1)], None, ALU.subtract))
                nc.vector.tensor_tensor(S_[:], g["place"][:], pos[:].unsqueeze(2).broadcast_to([P, TT, P]),
                                        ALU.is_equal).then_inc(s_built, 1)

            def rows(b, q):
                v.wait_ge(i_done, b + 1)
                ch(nc.vector.tensor_copy(val[:], pI[:, 2 * q:2 * q + 2]))
                ch.mark(nc.vector.tensor_copy(gcol[q][:], val[:, 1:2]))
                ch.mark(nc.vector.tensor_scalar(fetch[:], val[:, 0:1], 0.5, float(NO_ROW), ALU.is_lt, ALU.mult))
                ch(nc.vector.tensor_scalar(occ[:], val[:, 0:1], 1.0, None, ALU.min))
                ch.mark(nc.vector.scalar_tensor_tensor(row[:], occ[:], g["spare"][:, 1:2], val[:, 0:1], ALU.mult, ALU.add))
                nc.vector.scalar_tensor_tensor(idx[q][:], val[:, 0:1], -1.0, fetch[:], ALU.add, ALU.add).then_inc(i_ready, 1)
                ch.wait()
                ch(nc.vector.tensor_tensor(sidx[q][:], row[:], g["spare"][:, 0:1], ALU.add))

            for b in range(AHEAD):
                match(b, b)
                rows(b, b)

            def body(b, p, i):
                ch.enter(b, 8)
                q = (p + AHEAD) % SLOTS
                match(b + AHEAD, q)
                v.wait_ge(silu_done, b + 1)
                nc.vector.tensor_tensor(hm[:], hs[:], pH[:, F_EXP:2 * F_EXP], ALU.mult).then_inc(hm_done, 1)
                v.wait_ge(y_free[q], i + 1 + (p + AHEAD) // SLOTS)
                rows(b + AHEAD, q)
                v.wait_ge(d_done[p], 2 * i + 3)
                nc.vector.tensor_scalar(y[p][:, 512:D], pY[1][:], gcol[p][:, 0:1], None, ALU.mult).then_inc(y1_read, 1)
                assert ch.n - ch.start == ch.length, ch.n - ch.start
                ch.n = ch.start
            blocks(v, body)


def last_norm(nc, g, ln2_w, ln2_b, out):
    with ExitStack() as ctx:
        s = Scope(nc, ctx, "last")
        rows = s.sb("rows", [P, 3, D])
        acc = s.sb("acc", [P, TT, D])
        st = s.sb("st", [P, TT, 2, 6])
        mv = s.sb("mv", [P, TT, 2])
        rstd = s.sb("rstd", [P, TT])
        rows_in, acc_in, var_done, std_done, out_ready, stored, dve = (s.sem(n) for n in (
            "rows_in acc_in var_done std_done out_ready stored dve").split())
        acc_in = [s.sem(f"acc_in{t}") for t in range(TT)]
        block = ctx.enter_context(nc.Block())

        @block.sync
        def _(sp):
            for n, vec in enumerate((g["mod"][0][5 * D:6 * D], ln2_w[0], ln2_b[0])):
                sp.dma_start(rows[:, n], row_of(vec)).then_inc(rows_in, 16)
            for t in range(TT):
                sp.dma_start(acc[:, t], g["acc"][t * P:(t + 1) * P]).then_inc(acc_in[t], 16)
            for t in range(TT):
                sp.wait_ge(out_ready, t + 1)
                sp.dma_start(out[0, t * P:(t + 1) * P], acc[:, t]).then_inc(stored, 16)
            sp.wait_ge(stored, 16 * TT)

        @block.scalar
        def _(act):
            for t in range(TT):
                act.wait_ge(var_done, t + 1)
                nc.scalar.activation(rstd[:, t:t + 1], mv[:, t, 1:2], ACT.Sqrt, bias=g["eps"][:, 0:1]).then_inc(std_done, 1)

        @block.vector
        def _(v):
            ch = Chain(v, dve)
            v.wait_ge(rows_in, 48)
            ch(nc.vector.tensor_scalar(rows[:, 0], rows[:, 0], 1.0, None, ALU.add))
            for t in range(TT):
                v.wait_ge(acc_in[t], 16)
                ch(nc.vector.tensor_tensor(acc[:, t], acc[:, t], rows[:, 0], ALU.mult))
                ch(nc.vector.scalar_tensor_tensor(acc[:, t], g["x1"][:, t], ALPHA, acc[:, t], ALU.mult, ALU.add))
                for h in range(2):
                    ch.mark(nc.vector.bn_stats(st[:, t, h], acc[:, t, h * 512:(h + 1) * 512]))
                ch.wait()
                nc.vector.bn_aggr(mv[:, t], st[:, t]).then_inc(var_done, 1)
                v.wait_ge(std_done, t + 1)
                ch(nc.vector.reciprocal(rstd[:, t:t + 1], rstd[:, t:t + 1]))
                ch(nc.vector.tensor_scalar(acc[:, t], acc[:, t], mv[:, t, 0:1], rstd[:, t:t + 1], ALU.subtract, ALU.mult))
                ch(nc.vector.tensor_tensor(acc[:, t], acc[:, t], rows[:, 1], ALU.mult))
                nc.vector.tensor_tensor(acc[:, t], acc[:, t], rows[:, 2], ALU.add).then_inc(out_ready, 1)


_INS = """x c ada_w ada_b w_in shift_mu w0 w_up a0 a_up g_up k_k k_a r_k lnx_w lnx_b conv_w conv_b cnorm_w
cnorm_b cpw_w cpw_b gate_b w_o ln1_w ln1_b router_w router_b exp_gate exp_up exp_down sh_gate sh_up sh_down
ln2_w ln2_b""".split()


def hybrid_encoder_layer(nc, a, out):
    with ExitStack() as ctx:
        ctx.enter_context(nc.allow_non_contiguous_dma("columns of parameters"))

        def sb(name, shape, dt=F32):
            return ctx.enter_context(nc.sbuf_tensor(name, shape, dt))

        g = {
            "u1T": sb("u1T", [P, KC, T]),
            "ident": sb("ident", [P, P]),
            "mean1024": sb("mean1024", [P, P]),
            "eps": sb("eps", [P, 2]),
        }
        for name, shape in (("mod", (1, MODS * D)), ("rkv", (3, KC, P, T)), ("lora", (3, P, T)), ("gate", (2, KC, P, T)),
                            ("yb", (KC, P, T)), ("u2d", (ROWS, D)), ("acc", (ROWS, D))):
            g[name] = nc.dram_tensor(f"scratch_{name}", shape, F32, kind="Internal").ap()
        constants(nc, g)
        modulation_and_norm(nc, g, a["x"], a["c"], a["ada_w"], a["ada_b"])
        projections_and_conv(nc, g, *[a[n] for n in (
            "w_in", "shift_mu", "conv_w", "conv_b", "cnorm_w", "cnorm_b", "cpw_w", "cpw_b", "gate_b")])
        rwkv(nc, g, *[a[n] for n in ("w0", "w_up", "a0", "a_up", "g_up", "k_k", "k_a", "r_k", "lnx_w", "lnx_b")])
        g["x1"] = sb("x1", [P, TT, D])
        g["pg"] = sb("pg", [P, E, TT, 2])
        g["place"] = sb("place", [P, TT, P])
        g["rhs"] = sb("rhs", [P, SLOTS, TT, 2])
        g["spare"] = sb("spare", [P, 2])
        g["table"] = sb("table", [1, NBT + 2], I32)
        g["c0"] = sb("c0", [P, NBT])
        mix_and_route(nc, g, *[a[n] for n in ("x", "w_o", "ln1_w", "ln1_b", "router_w", "router_b",
                                              "sh_gate", "sh_up", "sh_down")])
        moe(nc, g, a["exp_gate"], a["exp_up"], a["exp_down"])
        last_norm(nc, g, a["ln2_w"], a["ln2_b"], out)


def kernel(**inputs):
    import numpy as _np
    import concourse.bacc as _bacc
    from concourse.bass_utils import run_bass_kernel_spmd as _run

    nc = _bacc.Bacc("TRN2", target_bir_lowering=False, num_devices=1)
    arrays, args = {}, {}
    for name in _INS:
        arr = _np.ascontiguousarray(inputs[name])
        arrays[f"in_{name}"] = arr
        args[name] = nc.dram_tensor(f"in_{name}", arr.shape, mybir.dt.from_np(arr.dtype), kind="ExternalInput").ap()
    out = nc.dram_tensor("out", (1, T, D), F32, kind="ExternalOutput").ap()
    hybrid_encoder_layer(nc, args, out)
    r = _run(nc, [arrays], core_ids=[0])
    return r.results[0]["out"]
```

```python
from contextlib import ExitStack
import math
import concourse.bass as bass
from concourse import mybir

F32 = mybir.dt.float32
I32 = mybir.dt.int32
F32R = mybir.dt.float32r
ALU = mybir.AluOpType
ACT = mybir.ActivationFunctionType
AX_X = mybir.AxisListType.X

P = 128
T = 512
D = 1024
KC = D // P
TT = T // P
CW = 31
PAD = CW // 2
LN_EPS = 1e-5
RW_COLS = 3 * D + 4 * 64 + 128
MODS = 6


def hold(pool, sem, value, held):
    pool.wait_ge(sem, value)
    pool.sem_inc(held, 1)


class Chain:

    def __init__(self, eng, sem, held=None):
        self.eng, self.sem, self.n, self.trip, self.held = eng, sem, 0, 0, held

    def enter(self, trip, length):
        self.trip, self.length, self.start = trip * length, length, self.n

    def leave(self, trips):
        assert self.n - self.start == self.length, (self.n - self.start, self.length)
        self.n, self.trip = self.start + self.length * trips, 0

    def mark(self, ins):
        ins.then_inc(self.sem, 1)
        self.n += 1

    def wait(self, but=0):
        if self.held is None:
            self.eng.wait_ge(self.sem, self.trip + self.n - but)
        else:
            hold(self.eng, self.sem, self.trip + self.n, self.held)

    def __call__(self, ins):
        self.mark(ins)
        self.wait()


class Scope:

    def __init__(self, nc, ctx, stage):
        self.nc, self.ctx, self.stage, self.sems = nc, ctx, stage, []
        ctx.callback(self.close)

    def close(self):
        self.nc.clear_and_free_semaphores(self.sems)
        self.nc.all_engine_barrier()

    def sb(self, name, shape, dt=F32):
        return self.ctx.enter_context(self.nc.sbuf_tensor(f"{self.stage}_{name}", list(shape), dt))

    def ps(self, name, shape=(P, 512)):
        return self.ctx.enter_context(self.nc.psum_tensor(f"{self.stage}_{name}", list(shape), F32))

    def sem(self, name):
        self.sems.append(self.nc.alloc_semaphore(f"{self.stage}_{name}"))
        return self.sems[-1]


HD = 64
C = 64
LEVELS = 6
MASKS = {"mlow": (LEVELS, P), "mup": (LEVELS, P), "mg": (2, 2, P), "sum64": (P,), "mean64": (P,), "cmask": (T,)}


def scan_masks(nc, g, ch):
    mlow, mup, mg, sum64, mean64, cmask = (g[n] for n in MASKS)

    def keep(ap, base, pattern, mult, op=ALU.is_ge):
        ch(nc.gpsimd.affine_select(out=ap, in_=ap, compare_op=op, fill=0.0, base=base, pattern=pattern,
                                   channel_multiplier=mult))

    def same_block(ap, b, lo_half=0, half=None):
        size = 2 * b if half is None else b
        keep(ap, -lo_half, [[-2 * b, P // (2 * b)], [0, 2 * b]], 1)
        keep(ap, lo_half + size - 1, [[2 * b, P // (2 * b)], [0, 2 * b]], -1)

    def blocks(ap, b):
        return ap.rearrange("p (n c) -> p n c", c=2 * b)

    ch(nc.gpsimd.memset(mlow[:], 0.0))
    ch(nc.gpsimd.memset(mup[:], 0.0))
    for j in range(LEVELS):
        b = 1 << j
        lowv, upv = blocks(mlow[:, j], b), blocks(mup[:, j], b)
        ch(nc.gpsimd.memset(lowv[:, :, 0:b], 1.0))
        ch(nc.gpsimd.memset(upv[:, :, b:2 * b], 1.0))
        same_block(lowv, b, b, 1)
        same_block(upv, b, 0, 1)
    for d in range(2):
        for n in range(2):
            ch(nc.gpsimd.memset(mg[:, d, n], 1.0))
            same_block(blocks(mg[:, d, n], HD // 2), HD // 2)
            sign = 1 if d == 0 else -1
            keep(mg[:, d, n], 0, [[sign, P]], -sign, ALU.is_ge if (d == 0 and n == 1) else ALU.is_gt)
    for m, value in ((sum64, 1.0), (mean64, 1.0 / HD)):
        ch(nc.gpsimd.memset(m[:], value))
        same_block(blocks(m[:], HD // 2), HD // 2)
    ch(nc.gpsimd.memset(cmask[:], 1.0))
    ch(nc.gpsimd.memset(cmask[:].rearrange("p (n c) -> p n c", c=C)[:, :, 0:1], 0.0))


def columns(vec, n=KC):
    return vec.rearrange("(k p) -> p k", p=P)


def modulation_and_norm(nc, g, x, c, ada_w, ada_b):
    with ExitStack() as ctx:
        s = Scope(nc, ctx, "mod")
        GROUP = 512
        NG = 2 * D // GROUP
        aw = s.sb("aw", [P, NG, KC, GROUP])
        xs = s.sb("x", [P, TT, D])
        xn = s.sb("xn", [P, TT, D])
        ccol = s.sb("ccol", [P, KC])
        bias, row = s.sb("bias", [1, 2 * D]), s.sb("row", [1, 2 * D])
        mod = s.sb("mod", [P, 2, KC])
        stats = s.sb("stats", [P, TT, 2, 6])
        mv = s.sb("mv", [P, TT, 2])
        std = s.sb("std", [P, TT])
        rstd = s.sb("rstd", [P, TT])
        acc = [s.ps(f"acc{i}") for i in range(NG)]
        tp = [s.ps(f"tp{i}") for i in range(4)]
        row_done, row_out, mod_in = s.sem("row_done"), s.sem("row_out"), s.sem("mod_in")
        x_in, c_in, b_in = s.sem("x_in"), s.sem("c_in"), s.sem("b_in")
        aw_in = [s.sem(f"aw_in{i}") for i in range(NG)]
        silu_done, mod_done, var_done, std_done, xn_done, tp_done, tp_used, dve, masks = (s.sem(n) for n in (
            "silu_done mod_done var_done std_done xn_done tp_done tp_used dve masks".split()))
        block = ctx.enter_context(nc.Block())

        @block.sync
        def _(sp):
            sp.dma_start(ccol[:], columns(c[0])).then_inc(c_in, 16)
            sp.dma_start(xs[:], x[0].rearrange("(n p) d -> p n d", p=P)).then_inc(x_in, 16)
            for n in range(NG):
                sp.dma_start(aw[:, n], ada_w[0, :, n * GROUP:(n + 1) * GROUP].rearrange("(k p) n -> p k n", p=P)) \
                  .then_inc(aw_in[n], 16)
            sp.dma_start(bias[:], ada_b[:, 0:2 * D]).then_inc(b_in, 16)
            sp.wait_ge(row_done, NG)
            sp.dma_start(g["mod"][:, 0:2 * D], row[:]).then_inc(row_out, 16)
            sp.wait_ge(row_out, 16)
            for n in range(2):
                sp.dma_start(mod[:, n], columns(g["mod"][0, n * D:(n + 1) * D])).then_inc(mod_in, 16)

        @block.gpsimd
        def _(pool):
            scan_masks(nc, g, Chain(pool, masks))

        @block.scalar
        def _(act):
            act.wait_ge(c_in, 16)
            nc.scalar.activation(g["csil"][:], ccol[:], ACT.Silu).then_inc(silu_done, 1)
            act.wait_ge(var_done, TT)
            nc.scalar.activation(std[:], mv[:, :, 1], ACT.Sqrt, bias=g["eps"][:, 0:1]).then_inc(std_done, 1)

        @block.tensor
        def _(pe):
            def turn(k):
                for t in range(TT):
                    ins = nc.tensor.transpose(tp[k % 4][:, t * P:(t + 1) * P], xn[:, t, k * P:(k + 1) * P], g["ident"][:])
                ins.then_inc(tp_done, 1)
            pe.wait_ge(silu_done, 1)
            for n in range(NG):
                pe.wait_ge(aw_in[n], 16)
                for k in range(KC):
                    ins = nc.tensor.matmul(acc[n][0:1, :], g["csil"][:, k:k + 1], aw[:, n, k], start=(k == 0), stop=(k == KC - 1))
                ins.then_inc(mod_done, 1)
            pe.wait_ge(xn_done, TT)
            for k in range(KC):
                if k >= 4:
                    pe.wait_ge(tp_used, k - 3)
                turn(k)

        @block.vector
        def _(v):
            ch = Chain(v, dve)
            v.wait_ge(x_in, 16)
            for t in range(TT):
                for h in range(2):
                    ch.mark(nc.vector.bn_stats(stats[:, t, h, :], xs[:, t, h * 512:(h + 1) * 512]))
            ch.wait()
            for t in range(TT):
                nc.vector.bn_aggr(mv[:, t, :], stats[:, t, :, :]).then_inc(var_done, 1)
            v.wait_ge(std_done, 1)
            ch(nc.vector.reciprocal(rstd[:], std[:]))
            for t in range(TT):
                nc.vector.tensor_scalar(xn[:, t, :], xs[:, t, :], mv[:, t, 0:1], rstd[:, t:t + 1],
                                        ALU.subtract, ALU.mult).then_inc(xn_done, 1)
            v.wait_ge(b_in, 16)
            for n in range(NG):
                v.wait_ge(mod_done, n + 1)
                cs = slice(n * GROUP, (n + 1) * GROUP)
                nc.vector.tensor_tensor(row[:, cs], acc[n][0:1, :], bias[:, cs], ALU.add).then_inc(row_done, 1)
            v.wait_ge(mod_in, 32)
            ch(nc.vector.tensor_scalar(mod[:, 1], mod[:, 1], 1.0, None, ALU.add))
            for k in range(KC):
                v.wait_ge(tp_done, k + 1)
                nc.vector.tensor_scalar(g["u1T"][:, k, :], tp[k % 4][:], mod[:, 1, k:k + 1], mod[:, 0, k:k + 1],
                                        ALU.mult, ALU.add).then_inc(tp_used, 1)


RW_TILES = RW_COLS // P
TILE0 = {"ha": RW_TILES, "hb": RW_TILES + KC, "r": 0, "k": KC, "v": 2 * KC,
         "ga": RW_TILES + 2 * KC, "gb": RW_TILES + 3 * KC}
KINDS = list(TILE0)


def projections_and_conv(nc, g, ada_w, ada_b, w_in, shift_mu, conv_w, conv_b, cnorm_w, cnorm_b, cpw_w, cpw_b, gate_b):
    with ExitStack() as ctx:
        s = Scope(nc, ctx, "proj")
        NK = len(KINDS)
        w = s.sb("w", [P, NK, KC, P])
        w_hi, w_lo = (s.sb(n, [P, NK, KC, P], F32R) for n in ("w_hi", "w_lo"))
        u_hi, u_lo = (s.sb(n, [P, KC, T], F32R) for n in ("u_hi", "u_lo"))
        mu = s.sb("mu", [P, 3, RW_TILES])
        cwT = s.sb("cwT", [P, KC, CW])
        cols = s.sb("cols", [P, 6, KC])
        sg = s.sb("sg", [P, T])
        hp = s.sb("hp", [P, T + 2 * PAD])
        hc = s.sb("hc", [P, KC, T])
        MG = 4 * D // KC
        aw = s.sb("aw", [P, KC, MG])
        bias, row = s.sb("bias", [1, MG]), s.sb("row", [1, MG])
        aw_in, bias_in, mod_done, mod_read, mod_out = (s.sem(n) for n in "aw_in bias_in mod_done mod_read mod_out".split())
        st = s.sb("st", [P, 5, T])
        sq = s.sb("sq", [P, 2, T])
        rs = s.sb("rs", [P, T])
        gb = s.sb("gb", [P, 2, T])
        yo = sq
        bank = [s.ps(f"bank{i}") for i in range(NK)]
        pstat = s.ps("pstat")
        w_in_sem = [s.sem(f"w{k}") for k in KINDS]
        params, mu_done, h_used, base_done, hp_done = (s.sem(n) for n in (
            "params", "mu_done", "h_used", "base_done", "hp_done"))
        held = s.sem("held")
        u_high, u_split, w_high, w_split, h_high, h_split, c_high, c_split = (s.sem(n) for n in (
            "u_high u_split w_high w_split h_high h_split c_high c_split").split())
        tile_done = s.sem("tile_done")
        read = [s.sem(f"read_{k}") for k in KINDS]
        shifted = [s.sem(f"shifted{j}") for j in range(3)]
        gated = [s.sem(f"gated{j}") for j in range(2)]
        stored = [s.sem(f"stored{j}") for j in range(5)]
        mean_done, cent, sq_done, sq_used, var_done, std_done, nrm, silu, cpw_done, cpw_read, yb_done, gb_in, yb_out = (
            s.sem(n) for n in ("mean_done", "cent", "sq_done", "sq_used", "var_done", "std_done", "nrm", "silu",
                               "cpw_done", "cpw_read", "yb_done", "gb_in", "yb_out"))
        wc_in = [s.sem(f"wc_in{j}") for j in range(2)]
        yb_slot = [s.sem(f"yb_slot{j}") for j in range(2)]
        gb_slot = [s.sem(f"gb_slot{j}") for j in range(2)]
        w_v = w_in[0].rearrange("(k p) n -> p k n", p=P)
        cpw_v = cpw_w[0].rearrange("(k p) n -> p k n", p=P)
        block = ctx.enter_context(nc.Block())

        @block.sync
        def _(sp):
            def store(i):
                one = bass.ds(i, 1)
                for j in range(3):
                    sp.wait_ge(shifted[j], i + 1)
                    sp.dma_start(g["rkv"][j, one].rearrange("a p t -> (a p) t"), st[:, j]).then_inc(stored[j], 16)
                for j in range(2):
                    sp.wait_ge(gated[j], i + 1)
                    sp.dma_start(g["gate"][j, one].rearrange("a p t -> (a p) t"), st[:, 3 + j]).then_inc(stored[3 + j], 16)

            for j in range(NK):
                sp.dma_start(w[:, j], w_v[:, :, TILE0[KINDS[j]] * P:(TILE0[KINDS[j]] + 1) * P]).then_inc(w_in_sem[j], 16)
            for n in range(2):
                sp.dma_start(mu[:, n], shift_mu[0, n].rearrange("(k p) -> p k", p=P)).then_inc(params, 16)
            for n, vec in enumerate((conv_b[0], cnorm_w[0], cnorm_b[0], cpw_b[0], gate_b[0, 0], gate_b[0, 1])):
                sp.dma_start(cols[:, n], columns(vec)).then_inc(params, 16)
            for k in range(KC):
                sp.dma_start(cwT[:, k], conv_w[0, :, k * P:(k + 1) * P].rearrange("j p -> p j")).then_inc(params, 16)

            def mod_columns(i):
                return bass.ds(2 * D + i * MG, MG)

            def load_mod(i):
                sp.dma_start(aw[:], ada_w[0, :, mod_columns(i)].rearrange("(k p) n -> p k n", p=P)).then_inc(aw_in, 16)
                sp.dma_start(bias[:], ada_b[:, mod_columns(i)]).then_inc(bias_in, 16)

            def store_mod(i):
                sp.wait_ge(mod_read, i + 2)
                sp.dma_start(g["mod"][:, mod_columns(i)], row[:]).then_inc(mod_out, 16)
            load_mod(0)

            def load(i):
                for j in range(NK):
                    sp.wait_ge(w_split, (i - 1) * NK + j + 1)
                    sp.dma_start(w[:, j], w_v[:, :, bass.ds((TILE0[KINDS[j]] + i) * P, P)]).then_inc(w_in_sem[j], 16)
            load(1)
            store_mod(0)
            load_mod(1)
            with sp.Fori(2, KC) as i:
                load(i)
                store(i - 2)
                store_mod(i - 1)
                load_mod(i)
            for j in range(3):
                sp.wait_ge(w_split, (KC - 1) * NK + j + 1)
                sp.dma_start(w[:, j], w_v[:, :, (3 * KC + j) * P:(3 * KC + j + 1) * P]).then_inc(w_in_sem[j], 16)
            store(KC - 2)
            store(KC - 1)
            for j in range(3):
                sp.wait_ge(shifted[j], KC + 1)
                sp.dma_start(g["lora"][j], st[:, j]).then_inc(stored[j], 16)
            store_mod(KC - 1)
            for n in range(KC):
                if n < 2:
                    sp.wait_ge(w_split, KC * NK)
                else:
                    sp.wait_ge(c_split, n - 1)
                sp.dma_start(w[:, 3 + n % 2], cpw_v[:, :, n * P:(n + 1) * P]).then_inc(wc_in[n % 2], 16)
            sp.wait_ge(mod_out, 16 * (KC + 1))

        @block.gpsimd
        def _(pool):
            def low_part(j, n):
                hold(pool, w_high, n + 1, held)
                nc.gpsimd.tensor_tensor(w_lo[:, j], w[:, j], w_hi[:, j].bitcast(F32), ALU.subtract).then_inc(w_split, 1)

            for j in range(NK):
                low_part(j, j)
            with pool.Fori(1, KC) as i:
                for j in range(NK):
                    low_part(j, i * NK + j)
            for j in range(3):
                low_part(j, KC * NK + j)
            pool.wait_ge(stored[4], 16 * (KC + 1))
            for n in range(KC):
                if n >= 2:
                    pool.wait_ge(yb_done, n - 1)
                pool.dma_start(gb[:, n % 2], g["gate"][1, n]).then_inc(gb_slot[n % 2], 16)
                pool.wait_ge(yb_done, n + 1)
                pool.dma_start(g["yb"][n], yo[:, n % 2]).then_inc(yb_slot[n % 2], 16)
            for j in range(3):
                pool.wait_ge(stored[j], 16 * (KC + 2))
            pool.wait_ge(stored[3], 16 * (KC + 1))
            for j in range(2):
                pool.wait_ge(yb_slot[j], 16 * KC // 2)

        @block.tensor
        def _(pe):
            def product(o, j, k):
                for n, (a, b) in enumerate(((w_hi, u_hi), (w_lo, u_hi), (w_hi, u_lo))):
                    ins = nc.tensor.matmul(o[:], a[:, j, k], b[:, k], start=(k == 0 and n == 0),
                                           stop=(k == KC - 1 and n == 2))
                return ins

            def project(j, trip, free):
                pe.wait_ge(w_split, trip * NK + j + 1)
                if free is not None:
                    pe.wait_ge(read[j], free)
                for k in range(KC):
                    if free is None and j == 0:
                        pe.wait_ge(u_split, k + 1)
                    ins = product(bank[j], j, k)
                ins.then_inc(tile_done, 1)
            def modulate(i):
                pe.wait_ge(mod_read, i + 1)
                pe.wait_ge(aw_in, 16 * (i + 1))
                for k in range(KC):
                    ins = nc.tensor.matmul(pstat[0:1, :], g["csil"][:, k:k + 1], aw[:, k], start=(k == 0), stop=(k == KC - 1))
                ins.then_inc(mod_done, 1)

            for j in range(NK):
                project(j, 0, None)
            modulate(0)
            with pe.Fori(1, KC) as i:
                for j in range(NK):
                    project(j, i, i)
                modulate(i)
            for j in range(3):
                project(j, KC, KC)
            pe.wait_ge(mod_read, KC + 1)
            pe.wait_ge(h_used, KC + 1)
            for k in range(KC):
                ins = nc.tensor.matmul(pstat[:], g["mean1024"][:], hc[:, k], start=(k == 0), stop=(k == KC - 1))
            ins.then_inc(mean_done, 1)
            pe.wait_ge(cent, KC)
            for k in range(KC):
                pe.wait_ge(sq_done, k + 1)
                nc.tensor.matmul(pstat[:], g["mean1024"][:], sq[:, k % 2], start=(k == 0), stop=(k == KC - 1)) \
                  .then_inc(sq_used, 1)
            for n in range(KC):
                pe.wait_ge(c_split, n + 1)
                if n < 2:
                    pe.wait_ge(read[3 + n], KC)
                if n >= 2:
                    pe.wait_ge(cpw_read, n - 1)
                for k in range(KC):
                    if n == 0:
                        pe.wait_ge(h_split, k + 1)
                    ins = product(bank[3 + n % 2], 3 + n % 2, k)
                ins.then_inc(cpw_done, 1)

        @block.scalar
        def _(act):
            def high_part(j, trip):
                act.wait_ge(w_in_sem[j], 16 * (trip + 1))
                nc.scalar.activation(w_hi[:, j], w[:, j], ACT.Copy).then_inc(w_high, 1)

            for k in range(KC):
                nc.scalar.activation(u_hi[:, k], g["u1T"][:, k], ACT.Copy).then_inc(u_high, 1)
                if k == 0:
                    high_part(0, 0)
            for j in range(1, NK):
                high_part(j, 0)
            act.sem_inc(hp_done, 1)
            for sem in (*stored, mod_out):
                act.sem_inc(sem, 16)
            act.wait_ge(params, 16 * (2 + 6 + KC))
            act.wait_ge(mu_done, 2)
            def trip(i, ahead):
                def finished(j):
                    act.wait_ge(tile_done, i * NK + j + 1)

                def split_next(j):
                    if j < ahead:
                        high_part(j, i + 1)
                finished(0)
                split_next(0)
                finished(1)
                act.wait_ge(hp_done, i + 1)
                nc.scalar.activation(sg[:], bank[1][:], ACT.Sigmoid).then_inc(read[1], 1)
                split_next(1)
                for j in range(3):
                    finished(2 + j)
                    act.wait_ge(stored[j], 16 * (i + 1))
                    nc.scalar.activation(st[:, j], bank[2 + j][:], ACT.Copy, scale=mu[:, 2, bass.ds(j * KC + i, 1)]) \
                      .then_inc(base_done, 1)
                    split_next(2 + j)
                for j in range(2):
                    finished(5 + j)
                    act.wait_ge(stored[3 + j], 16 * (i + 1))
                    nc.scalar.activation(st[:, 3 + j], bank[5 + j][:], ACT.Sigmoid, bias=cols[:, 4 + j, bass.ds(i, 1)]) \
                      .then_inc(gated[j], 1)
                    act.wait_ge(gated[j], i + 1)
                    nc.scalar.sem_inc(read[5 + j], 1)
                    split_next(5 + j)
            with act.Fori(0, KC - 1) as i:
                trip(i, NK)
            trip(KC - 1, 3)
            for j in range(3):
                act.wait_ge(tile_done, KC * NK + j + 1)
                act.wait_ge(stored[j], 16 * (KC + 1))
                nc.scalar.activation(st[:, j], bank[j][:], ACT.Copy, scale=mu[:, 2, 3 * KC + j:3 * KC + j + 1]) \
                  .then_inc(base_done, 1)
            def conv_high(n):
                act.wait_ge(wc_in[n % 2], 16 * (n // 2 + 1))
                if n >= 2:
                    act.wait_ge(cpw_done, n - 1)
                nc.scalar.activation(w_hi[:, 3 + n % 2], w[:, 3 + n % 2], ACT.Copy).then_inc(c_high, 1)

            for n in range(2):
                conv_high(n)
            for k in range(KC):
                act.wait_ge(cent, k + 1)
                if k >= 2:
                    act.wait_ge(sq_used, k - 1)
                nc.scalar.activation(sq[:, k % 2], hc[:, k], ACT.Square).then_inc(sq_done, 1)
            act.wait_ge(sq_used, KC)
            nc.scalar.activation(rs[:], pstat[:], ACT.Sqrt, bias=g["eps"][:, 0:1]).then_inc(std_done, 1)
            for k in range(KC):
                act.wait_ge(nrm, k + 2)
                nc.scalar.activation(hc[:, k], hc[:, k], ACT.Silu, scale=cols[:, 1, k:k + 1], bias=cols[:, 2, k:k + 1]) \
                  .then_inc(silu, 1)
                act.wait_ge(silu, k + 1)
                nc.scalar.activation(u_hi[:, k], hc[:, k], ACT.Copy).then_inc(h_high, 1)
            for n in range(2, KC):
                conv_high(n)

        @block.vector
        def _(v):
            v.sem_inc(h_used, 1)
            v.sem_inc(mod_read, 1)
            for k in range(KC):
                v.wait_ge(u_high, k + 1)
                nc.vector.tensor_tensor(u_lo[:, k], g["u1T"][:, k], u_hi[:, k].bitcast(F32), ALU.subtract).then_inc(u_split, 1)
            nc.vector.memset(hp[:, 0:PAD], 0.0)
            nc.vector.memset(hp[:, PAD + T:], 0.0)
            v.wait_ge(params, 16 * (2 + 6 + KC))
            nc.vector.tensor_tensor(mu[:, 2], mu[:, 0], mu[:, 1], ALU.add).then_inc(mu_done, 1)
            v.wait_ge(mu_done, 1)
            nc.vector.tensor_scalar(mu[:, 2], mu[:, 2], -1.0, 1.0, ALU.mult, ALU.add).then_inc(mu_done, 1)

            conv = s.sem("conv")
            ch = Chain(v, conv)

            def shift(j, tile, b, done, n_base):
                v.wait_ge(base_done, n_base)
                ch(nc.vector.scalar_tensor_tensor(st[:, j, 1:T], bank[b][:, 0:T - 1], mu[:, 0, tile], st[:, j, 1:T],
                                                  ALU.mult, ALU.add))
                nc.vector.scalar_tensor_tensor(st[:, j, 0:T - 1], bank[b][:, 1:T], mu[:, 1, tile], st[:, j, 0:T - 1],
                                               ALU.mult, ALU.add).then_inc(shifted[j], 1)
                v.wait_ge(shifted[j], done)
                v.sem_inc(read[b], 1)

            with v.Fori(0, KC) as i:
                ch.enter(i, 2 * CW - 1 + 3)
                v.wait_ge(tile_done, i * NK + 1)
                v.wait_ge(read[1], i + 1)
                v.wait_ge(h_used, i + 1)
                nc.vector.tensor_tensor(hp[:, PAD:PAD + T], bank[0][:], sg[:], ALU.mult).then_inc(hp_done, 1)
                v.wait_ge(hp_done, i + 2)
                v.sem_inc(read[0], 1)
                o = hc[:, bass.ds(i, 1), :].rearrange("p a t -> p (a t)")
                for j in range(CW):
                    for h in range(2):
                        half = slice(h * T // 2, (h + 1) * T // 2)
                        src = hp[:, j + h * T // 2:j + (h + 1) * T // 2]
                        if j == 0:
                            ins = nc.vector.tensor_scalar(o[:, half], src, cwT[:, bass.ds(i, 1), 0], cols[:, 0, bass.ds(i, 1)],
                                                          ALU.mult, ALU.add)
                        else:
                            ch.wait(1)
                            ins = nc.vector.scalar_tensor_tensor(o[:, half], src, cwT[:, bass.ds(i, 1), j], o[:, half],
                                                                 ALU.mult, ALU.add)
                        if j < CW - 1 or h == 0:
                            ch.mark(ins)
                ins.then_inc(h_used, 1)
                ch.wait()
                for j in range(3):
                    shift(j, bass.ds(j * KC + i, 1), 2 + j, i + 1, i * 3 + j + 1)
                v.wait_ge(mod_done, i + 1)
                v.wait_ge(bias_in, 16 * (i + 1))
                v.wait_ge(mod_out, 16 * (i + 1))
                nc.vector.tensor_tensor(row[:], pstat[0:1, :], bias[:], ALU.add).then_inc(mod_read, 1)
            ch.leave(KC)
            for j in range(3):
                shift(j, slice(3 * KC + j, 3 * KC + j + 1), j, KC + 1, 3 * KC + j + 1)
            v.wait_ge(mean_done, 1)
            for k in range(KC):
                nc.vector.tensor_tensor(hc[:, k], hc[:, k], pstat[:], ALU.subtract).then_inc(cent, 1)
            v.wait_ge(std_done, 1)
            nc.vector.reciprocal(rs[:], rs[:]).then_inc(nrm, 1)
            v.wait_ge(nrm, 1)
            v.wait_ge(sq_done, KC)
            for k in range(KC):
                nc.vector.tensor_tensor(hc[:, k], hc[:, k], rs[:], ALU.mult).then_inc(nrm, 1)
            def conv_low(n):
                v.wait_ge(c_high, n + 1)
                nc.vector.tensor_tensor(w_lo[:, 3 + n % 2], w[:, 3 + n % 2], w_hi[:, 3 + n % 2].bitcast(F32), ALU.subtract) \
                  .then_inc(c_split, 1)

            for n in range(2):
                conv_low(n)
            for k in range(KC):
                v.wait_ge(h_high, k + 1)
                nc.vector.tensor_tensor(u_lo[:, k], hc[:, k], u_hi[:, k].bitcast(F32), ALU.subtract).then_inc(h_split, 1)
            for n in range(KC):
                v.wait_ge(cpw_done, n + 1)
                v.wait_ge(gb_slot[n % 2], 16 * (n // 2 + 1))
                if n >= 2:
                    v.wait_ge(yb_slot[n % 2], 16 * (n // 2))
                nc.vector.scalar_tensor_tensor(yo[:, n % 2], bank[3 + n % 2][:], cols[:, 3, n:n + 1], gb[:, n % 2],
                                               ALU.add, ALU.mult).then_inc(cpw_read, 1)
                v.wait_ge(cpw_read, n + 1)
                v.sem_inc(yb_done, 1)
                if n + 2 < KC:
                    conv_low(n + 2)


def constants(nc, g):
    with ExitStack() as ctx:
        s = Scope(nc, ctx, "const")
        ms, done = s.sem("ms"), s.sem("done")
        block = ctx.enter_context(nc.Block())

        @block.gpsimd
        def _(pool):
            nc.gpsimd.memset(g["ident"][:], 0.0).then_inc(ms, 1)
            nc.gpsimd.memset(g["mean1024"][:], 1.0 / D).then_inc(done, 1)
            nc.gpsimd.memset(g["eps"][:, 0:1], LN_EPS).then_inc(done, 1)
            nc.gpsimd.memset(g["eps"][:, 1:2], 64e-5).then_inc(done, 1)
            pool.wait_ge(ms, 1)
            nc.gpsimd.affine_select(out=g["ident"][:], in_=g["ident"][:], compare_op=ALU.not_equal, fill=1.0, base=0,
                                    pattern=[[-1, P]], channel_multiplier=1).then_inc(done, 1)


NCH = T // C
PAIRS = D // P
DS = math.exp(-0.5)
GN_EPS = 64e-5
NU = 4


class Pair:

    def __init__(self, trip, off):
        self.trip, self.off = trip, off
        self.n = off if trip is None else trip + off

    def next(self):
        return Pair(self.trip, self.off + 1)

    def before(self):
        return Pair(self.trip, self.off - 1)


FILL = {0: {"A0": ("ZW", "ZA", "MEAN"), "B1": (("TV", 0),), "A1": (("TV", 1),), "B2": (("TQ", 0),), "A2": ("VAR", ("TQ", 1)),
            "B3": (("TK", 0),), "A3": (("TK", 1),), "B4": (("TB", 0),), "A4": (("TB", 1),), "B5": (("MV", 0), ("MV", 1))},
        1: {"A0": (("TQ", 0), ("TQ", 1)), "B1": ("SS",), "A1": ("ZW", "ZA"), "B2": (("TK", 0),), "A2": (("TK", 1),),
            "B3": (), "A3": (("TB", 0),), "B4": (), "A4": (("TB", 1),), "B5": (("MV", 0), ("MV", 1))}}


def gram_steps(d, p):
    return [((which, d, X), p) for which in ("GB", "GK") for X in range(2)]


def groups(d):
    g = [(X, n) for X in range(2) for n in range(2)]
    return g if d == 0 else g[::-1]


def fill_steps(d, p, at, first, last):
    out = []
    for f in FILL[d][at]:
        if isinstance(f, tuple):
            out.append(((f[0], d, f[1]), p))
        elif f in ("MEAN", "VAR"):
            if not first:
                out.append(((f,), p.before()))
        elif d == 0:
            out.append(((f, 1), p))
        elif not last:
            out.append(((f, 0), p.next()))
    return out


def job_steps(p, d, first, last):
    fill = lambda at: fill_steps(d, p, at, first, last)
    steps = [(("T", d, X, 0), p) for X in range(2)] + fill("A0")
    for j in range(1, LEVELS):
        steps += [(("U", d, X, j), p) for X in range(2)] + [(("V", d, X, j), p) for X in range(2)]
        steps += fill(f"B{j}")
        if j < LEVELS - 1:
            steps += [(("T", d, X, j), p) for X in range(2)] + fill(f"A{j}")
    if d == 0:
        steps += [(("BO", 1), p), (("G", 1), p)]
    steps += [(("AC", d, X, n), p) for X, n in groups(d)]
    steps += [(("PR", d, X, n), p) for X, n in groups(d)]
    gram = [] if last else gram_steps(1 - d, p if d == 0 else p.next())
    for n in range(NCH):
        if n % NU == 0:
            steps.append((("Y", d, n // NU), p))
        if n < NCH - 1:
            steps.append((("S", d, n), p))
        if n % 2 == 1:
            steps += gram[n // 2:n // 2 + 1]
    return steps


class BankUses:

    OUTPUT = {0: 6, 1: 7}

    def __init__(self):
        zero = Pair(None, 0)
        steps = [(("SS", 0), zero), (("ZW", 0), zero), (("ZA", 0), zero)] + gram_steps(0, zero)
        for J in range(2 * PAIRS):
            steps += job_steps(Pair(None, J // 2), J % 2, J == 0, J == 2 * PAIRS - 1)
        last = Pair(None, PAIRS - 1)
        steps += [(("MEAN",), last), (("VAR",), last)]
        self.use, used = {}, [0] * 8
        at, when = {}, [0] * 8
        mid = Pair(None, 1)
        for now, (step, _) in enumerate(job_steps(mid, 0, False, False) + job_steps(mid, 1, False, False), 1):
            if step[0] == "Y":
                b = self.OUTPUT[step[2]]
            else:
                b = min(range(6 if step[0] in ("S", "GB", "GK", "AC", "PR") else 8), key=lambda b: when[b])
            at[step], when[b] = b, now
        for step, p in steps:
            b = at[step]
            self.use[step, p.off] = (b, used[b])
            used[b] += 1

    def __call__(self, step, p):
        b, n = self.use[step, p.off]
        if p.trip is None:
            return b, n
        each = self.use[step, p.off + 1][1] - n
        for k in range(PAIRS - 1):
            assert self.use[step, p.off + k] == (b, n + k * each), step
        return b, n + p.trip * each


def rwkv(nc, g, w0, w_up, a0, a_up, g_up, k_k, k_a, r_k, lnx_w, lnx_b):
    uses = BankUses()
    with ExitStack() as ctx:
        s = Scope(nc, ctx, "rwkv")
        inb = s.sb("inb", [P, 3, T])
        lo = s.sb("lo", [P, 3, T])
        wst = s.sb("wst", [P, 2, 2, P])
        gst = s.sb("gst", [P, P])
        NPAR = 8
        par = s.sb("par", [P, PAIRS, NPAR])
        pc = s.sb("pc", [P, NPAR])
        lnx = s.sb("lnx", [P, 2, PAIRS])
        kk, nrm = s.sb("kk", [P, T]), s.sb("nrm", [P, T])
        sq = s.sb("sq", [P, T])
        tw, ta, lw, Ls, Es = (s.sb(n, [P, T]) for n in ("tw", "ta", "lw", "Ls", "Es"))
        eE, eN, eL = (s.sb(n, [P, T]) for n in ("eE", "eN", "eL"))
        kd = s.sb("kd", [P, 2, T])
        bb = s.sb("bb", [P, T])
        bon, gbuf = s.sb("bon", [P, T]), s.sb("gbuf", [P, T])
        GC = s.sb("GC", [P, 2, NCH])
        QR = [s.sb(f"QR{d}", [P, NCH, 2, C]) for d in range(2)]
        Qb = [s.sb(f"Qb{d}", [P, NCH, P]) for d in range(2)]
        KB = [s.sb(f"KB{d}", [P, NCH, 2, P]) for d in range(2)]
        Vbd = s.sb("Vbd", [P, NCH, P])
        Vtm = s.sb("Vtm", [P, NCH, P])
        RBs = [s.sb(f"RB{d}", [P, NCH, 3, P]) for d in range(2)]
        MKs = [s.sb(f"MK{d}", [P, NCH, 2, P]) for d in range(2)]
        Kt = s.sb("Kt", [P, NCH, P])
        W = s.sb("W", [P, NCH, 2, P])
        AC = s.sb("AC", [P, NCH, 2, P])
        PR = s.sb("PR", [P, NCH, 2, P])
        Tn, Tt, U = (s.sb(n, [P, NCH, P]) for n in ("Tn", "Tt", "U"))
        Sb = s.sb("Sb", [P, 2, P])
        yt = s.sb("yt", [P, T])
        fin = s.sb("fin", [P, 2, T])
        mlow, mup, mg, sum64, mean64, cmask = (g[n] for n in MASKS)
        sq2 = s.sb("sq2", [P, T])
        fsqb = s.sb("fsqb", [P, T])
        bank = [s.ps(f"bank{i}") for i in range(8)]
        full = [s.sem(f"full{i}") for i in range(8)]
        free = [s.sem(f"free{i}") for i in range(8)]
        names = """zeroed params lora_in lora_ready in_ready pc_ready wst_ready gst_ready fin_ready kk_sq kk_norm kk_rn
            in_used logw scanned edone th exps bd_ready mk_ready tt_ready t_ready u_ready v_ready w_ready
            ac_ready pr_ready s_ready job_done rkk bo_copied bon_done cent fsq fstd fnorm faff fin_done vchain
            pchain achain wst_used held""".split()
        S = {n: s.sem(n) for n in names}
        block = ctx.enter_context(nc.Block())

        def rep(ap, n):
            a = ap.unsqueeze(1)
            return a.broadcast_to([P, n] + list(ap.shape[1:]))

        def wait_full(eng, step, pair):
            b, n = uses(step, pair)
            eng.wait_ge(full[b], n + 1)
            return bank[b]

        def now_read(ins, step, pair):
            ins.then_inc(free[uses(step, pair)[0]], 1)

        def order(d):
            return list(range(NCH)) if d == 0 else list(range(NCH - 1, -1, -1))

        @block.sync
        def _(sp):
            for n, vec in enumerate((w0[0, 0], w0[0, 1], a0[0, 0], a0[0, 1], k_k[0], k_a[0], k_a[0],
                                     r_k[0].rearrange("h n -> (h n)"))):
                sp.dma_start(par[:, :, n], columns(vec)).then_inc(S["params"], 16)
            for n, vec in enumerate((lnx_w[0], lnx_b[0])):
                sp.dma_start(lnx[:, n], columns(vec)).then_inc(S["params"], 16)
            for j in range(3):
                sp.dma_start(lo[:, j], g["lora"][j]).then_inc(S["lora_in"], 16)

            def load_pair(i):
                one = bass.ds(i, 1)
                for j in range(3):
                    sp.dma_start(inb[:, j], g["rkv"][j, one].rearrange("a p t -> (a p) t")).then_inc(S["in_ready"], 16)
                for d in range(2):
                    rows = slice(d * HD, (d + 1) * HD)
                    sp.dma_start(wst[rows, d, 0], w_up[0, d, :, bass.ds(i * P, P)]).then_inc(S["wst_ready"], 16)
                    sp.dma_start(wst[rows, d, 1], a_up[0, d, :, bass.ds(i * P, P)]).then_inc(S["wst_ready"], 16)
                sp.dma_start(gst[:], g_up[0, :, bass.ds(i * P, P)]).then_inc(S["gst_ready"], 16)

            def load_fin(i):
                one = bass.ds(i, 1)
                sp.dma_start(fin[:, 0], g["gate"][0, one].rearrange("a p t -> (a p) t")).then_inc(S["fin_ready"], 16)
                sp.dma_start(fin[:, 1], g["yb"][one].rearrange("a p t -> (a p) t")).then_inc(S["fin_ready"], 16)

            sp.wait_ge(S["zeroed"], 1)
            load_pair(0)
            load_fin(0)

            def trip(i):
                sp.wait_ge(S["in_used"], i + 1)
                sp.wait_ge(S["bon_done"], i + 1)
                sp.wait_ge(S["wst_used"], i + 1)
                load_pair(i + 1)
                sp.wait_ge(S["fin_done"], i + 2)
                load_fin(i + 1)
            with sp.Fori(0, PAIRS - 1) as i:
                trip(i)

        @block.gpsimd
        def _(pool):
            ch = Chain(pool, S["pchain"], S["held"])

            pool.sem_inc(S["job_done"], 1)
            def prep(i, d, q, first=False, zeroed=None):
                v3 = lambda ap: ap.rearrange("p (n c) -> p n c", c=C)
                hold(pool, S["th"], q + 1, S["held"])
                if d == 1:
                    ch(nc.gpsimd.tensor_tensor(sq[:], inb[:, 0], kd[:, 0], ALU.mult))
                    ch(nc.gpsimd.tensor_scalar(sq[:], sq[:], pc[:, 7:8], None, ALU.mult))
                    pool.sem_inc(S["rkk"], 1)
                if not first:
                    hold(pool, S["exps"], q, S["held"])
                    hold(pool, S["scanned"], q, S["held"])
                nc.gpsimd.tensor_scalar(lw[:], tw[:], -DS / 2, -DS / 2, ALU.mult, ALU.add).then_inc(S["logw"], 1)
                ch.mark(nc.gpsimd.tensor_scalar(kd[:, d], ta[:], pc[:, 5:6], pc[:, 6:7], ALU.mult, ALU.add))
                ch(nc.gpsimd.tensor_scalar(bb[:], ta[:], 0.5, 0.5, ALU.mult, ALU.add))
                ch.mark(nc.gpsimd.tensor_tensor(kd[:, d], kd[:, d], inb[:, 1], ALU.mult))
                hold(pool, S["scanned"], q + 1, S["held"])
                nc.gpsimd.tensor_tensor(Es[:], Ls[:], lw[:], ALU.subtract).then_inc(S["edone"], 1)
                if d == 0:
                    hold(pool, S["kk_rn"], 4 * (i + 1), S["held"])
                    ch(nc.gpsimd.tensor_tensor(kk[:], kk[:], nrm[:], ALU.mult))
                ch(nc.gpsimd.tensor_tensor(bb[:], bb[:], kk[:], ALU.mult))
                if not first:
                    hold(pool, S["job_done"], q, S["held"])
                hold(pool, S["exps"], q + 1, S["held"])
                if zeroed is not None:
                    pool.wait_ge(S["zeroed"], zeroed)
                ch.mark(nc.gpsimd.tensor_tensor(QR[d][:, :, 0], v3(kk[:]), v3(eE[:]), ALU.mult))
                ch.mark(nc.gpsimd.tensor_tensor(QR[d][:, :, 1], v3(inb[:, 0]), v3((eL if d == 0 else eE)[:]), ALU.mult))
                ch.wait()
                for h in range(2):
                    rows, cs = slice(h * HD, (h + 1) * HD), slice(h * C, (h + 1) * C)
                    for dst, a, b in ((Qb[d][rows, :, cs], kk, eE), (KB[d][rows, :, 0, cs], None, eN),
                                      (KB[d][rows, :, 1, cs], bb, eN)):
                        src = kd[rows, d] if a is None else a[rows]
                        ch.mark(nc.gpsimd.tensor_tensor(dst, v3(src), v3(b[rows]), ALU.mult))
                    if d == 0:
                        ch.mark(nc.gpsimd.tensor_copy(Vbd[rows, :, cs], v3(inb[rows, 2])))
                ch.wait()
                pool.sem_inc(S["bd_ready"], 1)
                if d == 1:
                    pool.sem_inc(S["in_used"], 1)
                    hold(pool, S["bo_copied"], i + 1, S["held"])
                    ch(nc.gpsimd.tensor_tensor(bon[:], bon[:], inb[:, 2], ALU.mult))
                    pool.sem_inc(S["bon_done"], 1)

            prep(0, 0, 0, first=True, zeroed=4)
            prep(0, 1, 1, zeroed=5)
            with pool.Fori(0, PAIRS - 1) as i:
                ch.enter(i, 30)
                prep(i + 1, 0, 2 * i + 2)
                prep(i + 1, 1, 2 * i + 3)
                ch.leave(PAIRS - 1)

        @block.tensor
        def _(pe):
            def begin(step, pair):
                b, n = uses(step, pair)
                pe.wait_ge(free[b], n + 1)
                return bank[b]

            def end(ins, step, pair):
                ins.then_inc(full[uses(step, pair)[0]], 1)

            def mm(out, lhsT, rhs, start=True, stop=True):
                return nc.tensor.matmul(out, lhsT, rhs, start=start, stop=stop)

            def low_rank(p, d, which):
                pe.wait_ge(S["wst_ready"], 64 * (p.n + 1))
                w = 0 if which == "ZW" else 1
                end(mm(begin((which, d), p)[:], wst[:, d, w], lo[:, w]), (which, d), p)

            def norm_kk(p):
                pe.wait_ge(S["kk_sq"], p.n + 1)
                end(mm(begin(("SS", 0), p)[:], sum64[:], sq2[:]), ("SS", 0), p)

            def mean(p):
                pe.wait_ge(S["job_done"], 2 * p.n + 3)
                end(mm(begin(("MEAN",), p)[:], mean64[:], yt[:]), ("MEAN",), p)

            def variance(p):
                pe.wait_ge(S["fsq"], p.n + 1)
                end(mm(begin(("VAR",), p)[:], mean64[:], fsqb[:]), ("VAR",), p)

            def bonus_and_gate(p):
                pe.wait_ge(S["rkk"], p.n + 1)
                end(mm(begin(("BO", 1), p)[:], sum64[:], sq[:]), ("BO", 1), p)
                pe.wait_ge(S["gst_ready"], 16 * (p.n + 1))
                end(mm(begin(("G", 1), p)[:], gst[:], lo[:, 2]), ("G", 1), p)
                b, n = uses(("G", 1), p)
                pe.wait_ge(full[b], n + 1)
                pe.sem_inc(S["wst_used"], 1)

            def gram(step, p):
                which, d, X = step
                o = begin(step, p)
                for u in range(NU):
                    c = NU * X + u
                    ins = mm(o[:, u * P:(u + 1) * P], KB[d][:, c, 1 if which == "GB" else 0],
                             QR[d][:, c].rearrange("p a t -> p (a t)"))
                end(ins, step, p)

            def turn(step, p):
                which, d, X = step
                src = {"TQ": lambda c: Qb[d][:, c], "TK": lambda c: KB[d][:, c, 0], "TB": lambda c: KB[d][:, c, 1],
                       "TV": lambda c: Vbd[:, c]}[which]
                o = begin(step, p)
                for u in range(NU):
                    ins = nc.tensor.transpose(o[:, u * P:(u + 1) * P], src(NU * X + u), g["ident"][:])
                end(ins, step, p)

            def values(step, p):
                _, d, X = step
                pe.wait_ge(S["v_ready"], 2 * (p.n + 1))
                pe.wait_ge(S["mk_ready"], 2 * (2 * p.n + d) + X + 1)
                o = begin(step, p)
                for u in range(NU):
                    c = NU * X + u
                    ins = mm(o[:, u * P:(u + 1) * P], MKs[d][:, c, 0], Vtm[:, c])
                end(ins, step, p)

            def fill(at, p, d, first, last):
                for step, q in fill_steps(d, p, at, first, last):
                    if step[0] in ("ZW", "ZA"):
                        low_rank(q, step[1], step[0])
                    elif step[0] in ("TQ", "TK", "TB", "TV"):
                        turn(step, q)
                    elif step[0] == "MV":
                        values(step, q)
                    else:
                        {"SS": norm_kk, "MEAN": mean, "VAR": variance}[step[0]](q)

            for sem in free:
                pe.sem_inc(sem, 1)
            pe.wait_ge(S["lora_ready"], 2)
            zero = Pair(None, 0)
            norm_kk(zero)
            low_rank(zero, 0, "ZW")
            low_rank(zero, 0, "ZA")
            pe.wait_ge(S["bd_ready"], 1)
            for step, p in gram_steps(0, zero):
                gram(step, p)

            def job(p, d, first=False, last=False):
                J = 2 * p.n + d
                RB, MK = RBs[d], MKs[d]
                for j in range(LEVELS):
                    if j > 0:
                        for X in range(2):
                            pe.wait_ge(S["t_ready"], 10 * J + 2 * (j - 1) + X + 1)
                            o = begin(("U", d, X, j), p)
                            for u in range(NU):
                                c = NU * X + u
                                ins = mm(o[:, u * P:(u + 1) * P], RB[:, c, 0], Tn[:, c])
                            end(ins, ("U", d, X, j), p)
                        for X in range(2):
                            pe.wait_ge(S["u_ready"], 10 * J + 2 * (j - 1) + X + 1)
                            o = begin(("V", d, X, j), p)
                            for u in range(NU):
                                c = NU * X + u
                                ins = mm(o[:, u * P:(u + 1) * P], U[:, c], Tt[:, c])
                            end(ins, ("V", d, X, j), p)
                    if j > 0:
                        fill(f"B{j}", p, d, first, last)
                    if j < LEVELS - 1:
                        for X in range(2):
                            pe.wait_ge(S["tt_ready"], 12 * J + 2 * j + X + 1)
                            o = begin(("T", d, X, j), p)
                            for u in range(NU):
                                ins = nc.tensor.transpose(o[:, u * P:(u + 1) * P], Tt[:, NU * X + u], g["ident"][:])
                            end(ins, ("T", d, X, j), p)
                        fill(f"A{j}", p, d, first, last)
                if d == 0:
                    bonus_and_gate(p)
                for X, n in groups(d):
                    pe.wait_ge(S["w_ready"], 2 * J + X + 1)
                    pe.wait_ge(S["tt_ready"], 12 * J + 2 * (LEVELS - 1) + X + 1)
                    o = begin(("AC", d, X, n), p)
                    for m in range(2):
                        c = NU * X + 2 * n + m
                        ins = mm(o[:, m * 256:(m + 1) * 256], Tt[:, c], W[:, c].rearrange("p a t -> p (a t)"))
                    end(ins, ("AC", d, X, n), p)
                for k, (X, n) in enumerate(groups(d)):
                    pe.wait_ge(S["ac_ready"], 4 * J + k + 1)
                    o = begin(("PR", d, X, n), p)
                    for m in range(2):
                        c = NU * X + 2 * n + m
                        ins = mm(o[:, m * 256:(m + 1) * 256], AC[:, c, 0], RB[:, c, 1:3].rearrange("p a t -> p (a t)"))
                    end(ins, ("PR", d, X, n), p)
                grams = [] if last else gram_steps(1 - d, p if d == 0 else p.next())
                for n, c in enumerate(order(d)):
                    u = n % NU
                    if u == 0:
                        oy = begin(("Y", d, n // NU), p)
                    y = oy[:, u * P:(u + 1) * P]
                    if n < NCH - 1:
                        os_ = begin(("S", d, n), p)[:, 0:P]
                        mm(os_, Kt[:, c], Vtm[:, c], True, False)
                        ins = mm(os_, RB[:, c, 1], AC[:, c, 1], False, n == 0)
                        if n == 0:
                            end(ins, ("S", d, n), p)
                    mm(y, Vtm[:, c], MK[:, c, 1], True, False)
                    ins = mm(y, AC[:, c, 1], RB[:, c, 2], False, n == 0)
                    if n % 2 == 1:
                        for step, q in grams[n // 2:n // 2 + 1]:
                            pe.wait_ge(S["bd_ready"], J + 2)
                            gram(step, q)
                    if n > 0:
                        pe.wait_ge(S["s_ready"], 7 * J + n)
                        pe.wait_ge(S["pr_ready"], 4 * J + n // 2 + 1)
                        if n < NCH - 1:
                            end(mm(os_, PR[:, c, 0], Sb[:, n % 2], False, True), ("S", d, n), p)
                        ins = mm(y, Sb[:, n % 2], PR[:, c, 1], False, True)
                    if u == NU - 1:
                        end(ins, ("Y", d, n // NU), p)

            job(zero, 0, first=True)
            with pe.Fori(0, PAIRS - 1) as i:
                job(Pair(i, 0), 1)
                job(Pair(i, 1), 0)
            last = Pair(None, PAIRS - 1)
            job(last, 1, last=True)
            mean(last)
            variance(last)

        @block.scalar
        def _(act):
            ch = Chain(act, S["achain"])
            act.sem_inc(S["fin_done"], 1)
            act.wait_ge(S["lora_in"], 48)
            nc.scalar.activation(lo[:, 2], lo[:, 2], ACT.Sigmoid).then_inc(S["lora_ready"], 1)
            nc.scalar.activation(lo[:, 0], lo[:, 0], ACT.Tanh).then_inc(S["lora_ready"], 1)

            def four(ap, X):
                return ap[:, NU * X:NU * X + NU]

            def copied(step, p, dst, scale=1.0):
                o = wait_full(act, step, p)
                now_read(nc.scalar.activation(dst, o[:].rearrange("p (u t) -> p u t", u=NU), ACT.Copy, scale=scale), step, p)

            def signal(step, p, sem):
                b, n = uses(step, p)
                act.wait_ge(free[b], n + 2)
                act.sem_inc(S[sem], 1)

            def squares(p):
                act.wait_ge(S["in_ready"], 48 * (p.n + 1))
                act.wait_ge(S["pc_ready"], p.n + 1)
                ch.mark(nc.scalar.activation(kk[:], inb[:, 1], ACT.Copy, scale=pc[:, 4:5]))
                nc.scalar.activation(sq2[:], inb[:, 1], ACT.Square, scale=pc[:, 4:5]).then_inc(S["kk_sq"], 1)

            def norm_root(p):
                o = wait_full(act, ("SS", 0), p)
                now_read(nc.scalar.activation(nrm[:], o[:], ACT.Sqrt), ("SS", 0), p)
                ch.wait()
                signal(("SS", 0), p, "kk_norm")

            def tanhs(p, d):
                for step, dst, col in ((("ZW", d), tw, d), (("ZA", d), ta, 2 + d)):
                    o = wait_full(act, step, p)
                    now_read(nc.scalar.activation(dst[:], o[:], ACT.Tanh, scale=0.5, bias=pc[:, col:col + 1]), step, p)
                b, n = uses(("ZW", d), p)
                act.wait_ge(free[b], n + 2)
                signal(("ZA", d), p, "th")

            def exps(d, q, part):
                if part == 0:
                    act.wait_ge(S["edone"], q + 1)
                    ch.mark(nc.scalar.activation(eE[:], Es[:], ACT.Exp))
                    ch.mark(nc.scalar.activation(eN[:], Ls[:], ACT.Exp, scale=-1.0))
                    return
                if d == 0:
                    ch.mark(nc.scalar.activation(eL[:], Ls[:], ACT.Exp))
                v = Ls[:].rearrange("p (n c) -> p n c", c=C)
                end_ = C - 1 if d == 0 else 0
                ch(nc.scalar.activation(GC[:, d], v[:, :, end_], ACT.Exp))
                act.sem_inc(S["exps"], 1)

            def turned(at, p, d):
                dst = {"TQ": W[:, :, 0], "TK": Kt, "TB": RBs[d][:, :, 1], "TV": Vtm}
                for step, q in fill_steps(d, p, at, False, False):
                    if step[0] in dst:
                        copied(step, q, four(dst[step[0]], step[2]))
                        if step[0] == "TV":
                            signal(step, q, "v_ready")

            zero = Pair(None, 0)
            squares(zero)
            norm_root(zero)
            tanhs(zero, 0)
            exps(0, 0, 0)
            exps(0, 0, 1)

            def square_centred(p):
                act.wait_ge(S["cent"], p.n + 1)
                nc.scalar.activation(fsqb[:], yt[:], ACT.Square).then_inc(S["fsq"], 1)

            def deviation(p):
                o = wait_full(act, ("VAR",), p)
                now_read(nc.scalar.activation(fsqb[:], o[:], ACT.Sqrt, bias=g["eps"][:, 1:2]), ("VAR",), p)
                signal(("VAR",), p, "fstd")

            def affine(p):
                act.wait_ge(S["fnorm"], p.n + 1)
                one = bass.ds(p.n, 1)
                nc.scalar.activation(yt[:], yt[:], ACT.Identity, scale=lnx[:, 0, one], bias=lnx[:, 1, one]) \
                  .then_inc(S["faff"], 1)

            def job(p, d, first=False, last=False):
                for j in range(LEVELS - 1):
                    if j > 0:
                        turned(f"B{j}", p, d)
                    for X in range(2):
                        copied(("T", d, X, j), p, four(Tn, X))
                        signal(("T", d, X, j), p, "t_ready")
                    turned(f"A{j}", p, d)
                    if j == 0:
                        if d == 0:
                            tanhs(p, 1)
                        elif not last:
                            squares(p.next())
                    if j == 1 and d == 1 and not last:
                        norm_root(p.next())
                        tanhs(p.next(), 0)
                    if j == 1 and d == 0 and not first:
                        square_centred(p.before())
                    if j in (3, 4):
                        if d == 0:
                            exps(1, 2 * p.n + 1, j - 3)
                        elif not last:
                            exps(0, 2 * p.n + 2, j - 3)
                    if j == 2 and d == 0 and not first:
                        deviation(p.before())
                for X in range(2):
                    copied(("MV", d, X), p, four(W[:, :, 1], X), scale=-1.0)
                    signal(("MV", d, X), p, "w_ready")
                if d == 0 and not first:
                    affine(p.before())
                for X, n in groups(d):
                    cs = slice(NU * X + 2 * n, NU * X + 2 * n + 2)
                    o = wait_full(act, ("AC", d, X, n), p)
                    now_read(nc.scalar.activation(AC[:, cs].rearrange("p u a t -> p u (a t)"),
                                                  o[:].rearrange("p (u a) -> p u a", u=2), ACT.Copy), ("AC", d, X, n), p)
                    signal(("AC", d, X, n), p, "ac_ready")
                if d == 0:
                    act.wait_ge(S["fin_done"], p.n + 1)
                    for key, dst in (("BO", bon), ("G", gbuf)):
                        o = wait_full(act, (key, 1), p)
                        now_read(nc.scalar.activation(dst[:], o[:], ACT.Copy), (key, 1), p)
                    b, n = uses(("BO", 1), p)
                    act.wait_ge(free[b], n + 2)
                    signal(("G", 1), p, "bo_copied")
                for n, c in enumerate(order(d)[:-1]):
                    o = wait_full(act, ("S", d, n), p)
                    now_read(nc.scalar.activation(Sb[:, (n + 1) % 2], o[:, 0:P], ACT.Copy, scale=GC[:, d, c:c + 1]),
                             ("S", d, n), p)
                    signal(("S", d, n), p, "s_ready")

            job(zero, 0, first=True)
            with act.Fori(0, PAIRS - 1) as i:
                ch.enter(i, 8)
                job(Pair(i, 0), 1)
                job(Pair(i, 1), 0)
                ch.leave(PAIRS - 1)
            last = Pair(None, PAIRS - 1)
            job(last, 1, last=True)
            square_centred(last)
            deviation(last)
            affine(last)

        @block.vector
        def _(v):
            ch = Chain(v, S["vchain"])
            nc.vector.memset(wst[:], 0.0).then_inc(S["zeroed"], 1)
            v.wait_ge(S["params"], 160)
            ch(nc.vector.tensor_scalar(par[:, :, 0:4], par[:, :, 0:4], 0.5, None, ALU.mult))
            ch(nc.vector.tensor_scalar(par[:, :, 5], par[:, :, 5], 0.5, None, ALU.mult))
            ch(nc.vector.tensor_scalar(par[:, :, 6], par[:, :, 5], -1.0, 1.0, ALU.mult, ALU.add))

            def signal(step, p, sem):
                b, n = uses(step, p)
                v.wait_ge(free[b], n + 2)
                v.sem_inc(S[sem], 1)

            def pick(p):
                nc.vector.tensor_copy(pc[:], par[:, bass.ds(p.n, 1), :].rearrange("p a n -> p (a n)")).then_inc(S["pc_ready"], 1)

            def kk_scale(p):
                v.wait_ge(S["kk_norm"], p.n + 1)
                ch(nc.vector.tensor_scalar(nrm[:], nrm[:], 1e-12, None, ALU.max))

            def kk_inverse(quarter):
                cs = slice(quarter * P, (quarter + 1) * P)
                nc.vector.reciprocal(nrm[:, cs], nrm[:, cs]).then_inc(S["kk_rn"], 1)

            def scan(d, q, first=False):
                v.wait_ge(S["logw"], q + 1)
                if not first:
                    v.wait_ge(S["exps"], q)
                r = slice(None) if d == 0 else slice(None, None, -1)
                nc.vector.tensor_tensor_scan(Ls[:, r], cmask[:], lw[:, r], 0.0, ALU.mult, ALU.add).then_inc(S["scanned"], 1)

            def gram_read(step, p):
                which, d, X = step
                cs = slice(NU * X, NU * X + NU)
                o4 = wait_full(v, step, p)[:].rearrange("p (u a t) -> p u a t", u=NU, a=2)
                dst = RBs[d][:, cs, 0:3:2] if which == "GB" else MKs[d][:, cs]
                for h in range(2):
                    rows, fs = slice(h * HD, (h + 1) * HD), slice(h * C, (h + 1) * C)
                    ins = nc.vector.tensor_tensor(dst[rows, :, :, fs], o4[rows], 
                                                  mg[rows, d, :, fs].unsqueeze(1).broadcast_to([HD, NU, 2, C]), ALU.mult)
                    if h == 0:
                        ch.mark(ins)
                now_read(ins, step, p)
                if which == "GK":
                    ch.wait()
                    signal(step, p, "mk_ready")

            def inverse_start(p, d):
                m1t = mup if d == 0 else mlow
                b, n = uses(("GB", d, 1), p)
                v.wait_ge(free[b], n + 2)
                ch.wait()
                for X in range(2):
                    cs = slice(NU * X, NU * X + NU)
                    ch.mark(nc.vector.tensor_tensor(Tt[:, cs], RBs[d][:, cs, 0], rep(m1t[:, 0], NU), ALU.mult))
                ch.wait()
                for X in range(2):
                    cs = slice(NU * X, NU * X + NU)
                    nc.vector.tensor_tensor(Tt[:, cs], rep(g["ident"][:], NU), Tt[:, cs], ALU.subtract) \
                      .then_inc(S["tt_ready"], 1)

            def centre(p):
                o = wait_full(v, ("MEAN",), p)
                now_read(nc.vector.tensor_tensor(yt[:], yt[:], o[:], ALU.subtract), ("MEAN",), p)
                signal(("MEAN",), p, "cent")

            def inverse_deviation(p, quarter):
                v.wait_ge(S["fstd"], p.n + 1)
                cs = slice(quarter * P, (quarter + 1) * P)
                ch.mark(nc.vector.reciprocal(fsqb[:, cs], fsqb[:, cs]))

            def normalize(p):
                ch.wait()
                nc.vector.tensor_tensor(yt[:], yt[:], fsqb[:], ALU.mult).then_inc(S["fnorm"], 1)

            def merge(p):
                v.wait_ge(S["faff"], p.n + 1)
                v.wait_ge(S["bon_done"], p.n + 1)
                ch(nc.vector.tensor_tensor(yt[:], yt[:], bon[:], ALU.add))
                ch(nc.vector.tensor_tensor(yt[:], yt[:], gbuf[:], ALU.mult))
                v.wait_ge(S["fin_ready"], 32 * (p.n + 1))
                ch(nc.vector.tensor_tensor(yt[:], yt[:], fin[:, 0], ALU.mult))
                nc.vector.tensor_tensor(g["u1T"][:, bass.ds(p.n, 1), :].rearrange("p a t -> p (a t)"), yt[:], fin[:, 1],
                                        ALU.add).then_inc(S["fin_done"], 1)
                v.wait_ge(S["fin_done"], p.n + 2)

            zero = Pair(None, 0)
            pick(zero)
            for t in (Qb[0], KB[0]):
                nc.vector.memset(t[:], 0.0).then_inc(S["zeroed"], 1)
            kk_scale(zero)
            for quarter in range(4):
                kk_inverse(quarter)
            scan(0, 0, first=True)
            nc.vector.memset(Vbd[:], 0.0).then_inc(S["zeroed"], 1)
            for t in (Qb[1][:], KB[1][:], *(RB[:, :, 0:3:2] for RB in RBs), *(MK[:] for MK in MKs), PR[:, :, 1]):
                ch.mark(nc.vector.memset(t, 0.0))
            ch.wait()
            v.sem_inc(S["zeroed"], 1)
            for step, p in gram_steps(0, zero):
                gram_read(step, p)
                if step == ("GB", 0, 1):
                    inverse_start(zero, 0)

            def job(p, d, first=False, last=False):
                mj = mlow if d == 0 else mup
                if d == 1 and not last:
                    v.wait_ge(S["bon_done"], p.n + 1)
                    pick(p.next())
                for j in range(1, LEVELS):
                    for X in range(2):
                        cs = slice(NU * X, NU * X + NU)
                        o = wait_full(v, ("U", d, X, j), p)
                        ins = nc.vector.tensor_tensor(U[:, cs], o[:].rearrange("p (u t) -> p u t", u=NU),
                                                      rep(mj[:, j], NU), ALU.mult)
                        now_read(ins, ("U", d, X, j), p)
                        signal(("U", d, X, j), p, "u_ready")
                    if j in (3, 4) and d == 1 and not last:
                        kk_inverse(1 if j == 3 else 3)
                    if j == 1 and d == 0 and not first:
                        centre(p.before())
                    if j in (3, 4) and d == 0 and not first:
                        inverse_deviation(p.before(), 0 if j == 3 else 2)
                    for X in range(2):
                        cs = slice(NU * X, NU * X + NU)
                        o = wait_full(v, ("V", d, X, j), p)
                        ins = nc.vector.tensor_tensor(Tt[:, cs], Tt[:, cs], o[:].rearrange("p (u t) -> p u t", u=NU),
                                                      ALU.subtract)
                        now_read(ins, ("V", d, X, j), p)
                        signal(("V", d, X, j), p, "tt_ready")
                    if j == 1 and d == 0:
                        scan(1, 2 * p.n + 1)
                    if j in (3, 4) and d == 0 and not first:
                        inverse_deviation(p.before(), 1 if j == 3 else 3)
                        if j == 4:
                            normalize(p.before())
                    if j == 2 and d == 1 and not last:
                        kk_scale(p.next())
                        kk_inverse(0)
                        scan(0, 2 * p.n + 2)
                    if j == 3 and d == 1 and not last:
                        kk_inverse(2)
                if d == 0 and not first:
                    merge(p.before())
                for X, n in groups(d):
                    cs = slice(NU * X + 2 * n, NU * X + 2 * n + 2)
                    o = wait_full(v, ("PR", d, X, n), p)
                    o4 = o[:].rearrange("p (u a t) -> p u a t", u=2, a=2)
                    ch.mark(nc.vector.tensor_tensor(PR[:, cs, 0], rep(g["ident"][:], 2), o4[:, :, 0], ALU.subtract))
                    for h in range(2):
                        rows, fs = slice(h * HD, (h + 1) * HD), slice(h * C, (h + 1) * C)
                        ins = nc.vector.tensor_tensor(PR[rows, cs, 1, fs], QR[d][rows, cs, 1], o4[rows, :, 1, fs], ALU.subtract)
                        if h == 0:
                            ch.mark(ins)
                    now_read(ins, ("PR", d, X, n), p)
                    ch.wait()
                    signal(("PR", d, X, n), p, "pr_ready")
                grams = [] if last else gram_steps(1 - d, p if d == 0 else p.next())
                for n in range(NCH):
                    if n % 2 == 1:
                        for step, q in grams[n // 2:n // 2 + 1]:
                            gram_read(step, q)
                            if n == 3:
                                inverse_start(q, 1 - d)
                    if n % NU < NU - 1:
                        continue
                    half = n // NU
                    o = wait_full(v, ("Y", d, half), p)
                    o4 = o[:].rearrange("p (u a) -> p u a", u=NU)
                    cs = order(d)[NU * half:NU * half + NU]
                    for h in range(2):
                        rows, fs = slice(h * HD, (h + 1) * HD), slice(h * C, (h + 1) * C)
                        y3 = yt[rows].rearrange("p (n c) -> p n c", c=C)
                        y3 = y3[:, cs[0]:cs[-1] + 1] if d == 0 else y3[:, cs[-1]:cs[0] + 1][:, ::-1]
                        src = o4[rows, :, fs]
                        ins = (nc.vector.tensor_copy(y3, src) if d == 0 else
                               nc.vector.tensor_tensor(y3, y3, src, ALU.add))
                        if h == 0:
                            ch.mark(ins)
                    now_read(ins, ("Y", d, half), p)
                    b, m = uses(("Y", d, half), p)
                    v.wait_ge(free[b], m + 2)
                ch.wait()
                v.sem_inc(S["job_done"], 1)

            job(zero, 0, first=True)
            with v.Fori(0, PAIRS - 1) as i:
                ch.enter(i, 40)
                job(Pair(i, 0), 1)
                job(Pair(i, 1), 0)
                ch.leave(PAIRS - 1)
            last = Pair(None, PAIRS - 1)
            job(last, 1, last=True)
            centre(last)
            for quarter in range(4):
                inverse_deviation(last, quarter)
            normalize(last)
            merge(last)


E = 64
F_EXP = 256
GROUPS, PER_GROUP = 8, 8
TOP_GROUPS, TOP_K = 4, 8
ROUTED_SCALE = 2.5
ALPHA = 2.0 ** 0.25
ROWS = T + P
MAX_BLOCKS = (T * TOP_K - E) // P + E
SLOTS = 3
AHEAD = 2
TRIPS = -(-MAX_BLOCKS // SLOTS)
NBT = SLOTS * TRIPS + AHEAD
BIG = 1e30
N_CONSTS = 6 + SLOTS
NO_ROW = 65536


def row_of(vec):
    return vec.partition_broadcast(P)


def mix_and_route(nc, g, x, w_o, ln1_w, ln1_b, router_w, router_b, sh_gate, sh_up, sh_down):
    with ExitStack() as ctx:
        s = Scope(nc, ctx, "mix")
        wo = s.sb("wo", [P, KC, D])
        rows = s.sb("rows", [P, 5, D])
        xs = s.sb("x", [P, TT, D])
        u2T = s.sb("u2T", [P, KC, T])
        tmp = s.sb("tmp", [P, D])
        u2n = s.sb("u2n", [P, 2, D])
        st = s.sb("st", [P, 2, 6])
        mv = s.sb("mv", [P, 2])
        rstd = s.sb("rstd", [P, 2 * TT])
        zrow = s.sb("zrow", [P, D])
        rw = s.sb("rw", [P, KC, E])
        rb = s.sb("rb", [P, E])
        shw = s.sb("shw", [P, KC, 2, F_EXP])
        shd = s.sb("shd", [P, 2, D])
        hT = s.sb("hT", [P, 2, T])
        hs = s.sb("hs", [P, 2, T])
        yo = s.sb("yo", [P, TT, D])
        sc = s.sb("sc", [P, TT, E])
        sel = s.sb("sel", [P, TT, E])
        m8 = s.sb("m8", [P, TT, GROUPS, 8])
        gsx = s.sb("gsx", [P, TT, 12])
        t8 = s.sb("t8", [P, TT, 8])
        gr = s.sb("gr", [P, TT, 12])
        er = s.sb("er", [P, TT, E])
        A = s.sb("A", [P, TT, E])
        wgt = s.sb("wgt", [P, TT, E])
        ws = s.sb("ws", [P, TT])
        ones = s.sb("ones", [P, P])
        before = s.sb("before", [P, P])
        upto = s.sb("upto", [P, P])
        iob = s.sb("iob", [E, NBT])
        cnt = s.sb("cnt", [E, 4])
        nb = s.sb("nb", [E, 1])
        nbr = s.sb("nbr", [E, P])
        M = s.sb("M", [E, NBT])
        ci = s.sb("ci", [E, 1])
        bank = [s.ps(f"bank{i}") for i in range(8)]
        (u2_normed, scaled, x_in, rows_in, sh_in, mixed, mix_read, var1, std1, u2_ready, tp_done, tp_read, u2_out, z_ready, z_out,
         rt_in, h_done, gate_read, up_read, y_done, y_read, y_out, sh_silu, logit, score, sel_done, dve, consts, a_ready,
         pos_done, pos_read, cnt_done, nb_ready, ci_done, m_ready, eb_done, pc) = (s.sem(n) for n in (
             """u2_normed scaled x_in rows_in sh_in mixed mix_read var1 std1 u2_ready tp_done tp_read u2_out z_ready z_out
         rt_in h_done gate_read up_read y_done y_read y_out sh_silu logit score sel_done dve consts a_ready
         pos_done pos_read cnt_done nb_ready ci_done m_ready eb_done pc""").split())
        wo_in = [s.sem(f"wo_in{k}") for k in range(KC)]
        block = ctx.enter_context(nc.Block())

        @block.sync
        def _(sp):
            for k in range(KC):
                sp.dma_start(wo[:, k], w_o[0, k * P:(k + 1) * P]).then_inc(wo_in[k], 16)
            sp.dma_start(xs[:], x[0].rearrange("(n p) d -> p n d", p=P)).then_inc(x_in, 16)
            mod = g["mod"][0]
            for n, vec in enumerate((mod[2 * D:3 * D], ln1_w[0], ln1_b[0], mod[4 * D:5 * D], mod[3 * D:4 * D])):
                sp.dma_start(rows[:, n], row_of(vec)).then_inc(rows_in, 16)
            sp.dma_start(rw[:], router_w[0].rearrange("(k p) n -> p k n", p=P)).then_inc(rt_in, 16)
            sp.dma_start(rb[:], row_of(router_b[0])).then_inc(rt_in, 16)
            sp.dma_start(shw[:, :, 0], sh_gate[0].rearrange("(k p) n -> p k n", p=P)).then_inc(sh_in, 16)
            sp.dma_start(shw[:, :, 1], sh_up[0].rearrange("(k p) n -> p k n", p=P)).then_inc(sh_in, 16)
            sp.dma_start(shd[:], sh_down[0].rearrange("(c p) n -> p c n", p=P)).then_inc(sh_in, 16)
            sp.wait_ge(z_ready, 1)
            sp.dma_start(g["u2d"][T:ROWS], zrow[:]).then_inc(z_out, 16)
            sp.dma_start(g["acc"][T:ROWS], zrow[:]).then_inc(z_out, 16)
            for t in range(TT):
                sp.wait_ge(u2_ready, t + 1)
                sp.dma_start(g["u2d"][t * P:(t + 1) * P], xs[:, t]).then_inc(u2_out, 16)
            for t in range(TT):
                sp.wait_ge(y_read, 2 * t + 2)
                sp.dma_start(g["acc"][t * P:(t + 1) * P], yo[:, t]).then_inc(y_out, 16)
            sp.wait_ge(z_out, 32)
            sp.wait_ge(u2_out, 16 * TT)
            sp.wait_ge(y_out, 16 * TT)

        @block.gpsimd
        def _(pool):
            nc.gpsimd.memset(zrow[:], 0.0).then_inc(z_ready, 1)
            nc.gpsimd.memset(ones[:], 1.0).then_inc(pc, 1)
            nc.gpsimd.memset(before[:], 1.0).then_inc(pc, 1)
            nc.gpsimd.memset(upto[:], 1.0).then_inc(pc, 1)
            nc.gpsimd.memset(gsx[:], BIG).then_inc(pc, 1)
            pool.wait_ge(pc, 4)
            nc.gpsimd.affine_select(out=before[:], in_=before[:], compare_op=ALU.is_gt, fill=0.0, base=0,
                                    pattern=[[1, P]], channel_multiplier=-1).then_inc(consts, 1)
            nc.gpsimd.affine_select(out=upto[:], in_=upto[:], compare_op=ALU.is_ge, fill=0.0, base=0,
                                    pattern=[[1, P]], channel_multiplier=-1).then_inc(consts, 1)
            nc.gpsimd.iota(iob[:], pattern=[[1, NBT]], base=0, channel_multiplier=0,
                           allow_small_or_imprecise_dtypes=True).then_inc(consts, 1)
            nc.gpsimd.iota(g["place"][:], pattern=[[0, TT], [1, P]], base=1, channel_multiplier=0,
                           allow_small_or_imprecise_dtypes=True).then_inc(consts, 1)
            for b in range(SLOTS):
                nc.gpsimd.iota(g["rhs"][:, b, :, 0], pattern=[[P, TT]], base=1, channel_multiplier=1,
                               allow_small_or_imprecise_dtypes=True).then_inc(consts, 1)
            nc.gpsimd.iota(g["spare"][:, 0:1], pattern=[[0, 1]], base=T, channel_multiplier=1,
                           allow_small_or_imprecise_dtypes=True).then_inc(consts, 1)
            nc.gpsimd.iota(g["spare"][:, 1:2], pattern=[[0, 1]], base=-(T + 1), channel_multiplier=-1,
                           allow_small_or_imprecise_dtypes=True).then_inc(consts, 1)
            for t in range(TT):
                pool.wait_ge(u2_normed, t + 1)
                nc.gpsimd.tensor_tensor(xs[:, t], u2n[:, t % 2], rows[:, 3], ALU.mult).then_inc(scaled, 1)
                pool.wait_ge(scaled, t + 1)
                nc.gpsimd.tensor_tensor(xs[:, t], xs[:, t], rows[:, 4], ALU.add).then_inc(u2_ready, 1)

        @block.tensor
        def _(pe):
            for t in range(TT):
                for k in range(KC):
                    if t == 0:
                        pe.wait_ge(wo_in[k], 16)
                    for h in range(2):
                        ins = nc.tensor.matmul(bank[2 * t + h][:], g["u1T"][:, k, t * P:(t + 1) * P],
                                               wo[:, k, h * 512:(h + 1) * 512], start=(k == 0), stop=(k == KC - 1))
                ins.then_inc(mixed, 1)
            pe.wait_ge(mix_read, 2 * TT)
            for t in range(TT):
                pe.wait_ge(u2_ready, t + 1)
                for h in range(2):
                    n = 2 * t + h
                    if n >= 2:
                        pe.wait_ge(tp_read, n - 1)
                    for k in range(4):
                        ins = nc.tensor.transpose(bank[n % 2][:, k * P:(k + 1) * P], xs[:, t, (4 * h + k) * P:(4 * h + k + 1) * P],
                                                  g["ident"][:])
                    ins.then_inc(tp_done, 1)
            pe.wait_ge(tp_read, 2 * TT)
            pe.wait_ge(rt_in, 32)
            for t in range(TT):
                for k in range(KC):
                    ins = nc.tensor.matmul(bank[2][:, t * E:(t + 1) * E], u2T[:, k, t * P:(t + 1) * P], rw[:, k],
                                           start=(k == 0), stop=(k == KC - 1))
                ins.then_inc(logit, 1)
            pe.wait_ge(sh_in, 48)
            for f in range(2):
                for w in range(2):
                    for k in range(KC):
                        ins = nc.tensor.matmul(bank[4 + 2 * f + w][:], shw[:, k, w, f * P:(f + 1) * P], u2T[:, k],
                                               start=(k == 0), stop=(k == KC - 1))
                    ins.then_inc(h_done, 1)
            pe.wait_ge(up_read, 2)
            for t in range(TT):
                for h in range(2):
                    n = 2 * t + h
                    if n >= 2:
                        pe.wait_ge(y_read, n - 1)
                    for f in range(2):
                        ins = nc.tensor.matmul(bank[n % 2][:], hT[:, f, t * P:(t + 1) * P], shd[:, f, h * 512:(h + 1) * 512],
                                               start=(f == 0), stop=(f == 1))
                    ins.then_inc(y_done, 1)
            pe.wait_ge(consts, N_CONSTS)
            pe.wait_ge(a_ready, TT)
            for t in range(TT):
                o = bank[3][:, t * E:(t + 1) * E]
                for i in range(t):
                    nc.tensor.matmul(o, ones[:], A[:, i], start=(i == 0), stop=False)
                nc.tensor.matmul(o, before[:], A[:, t], start=(t == 0), stop=True).then_inc(pos_done, 1)
            for t in range(TT):
                ins = nc.tensor.matmul(bank[2][0:E, 0:1], A[:, t], ones[:, 0:1], start=(t == 0), stop=(t == TT - 1))
            ins.then_inc(cnt_done, 1)
            pe.wait_ge(nb_ready, 1)
            nc.tensor.matmul(bank[4][0:E, 0:1], upto[0:E, 0:E], nb[:], start=True, stop=True).then_inc(ci_done, 1)
            pe.wait_ge(m_ready, 1)
            nc.tensor.matmul(bank[5][:, 0:NBT], ones[0:E], M[:], start=True, stop=True)
            nc.tensor.matmul(bank[6][:, 0:NBT], nbr[:], M[:], start=True, stop=True)
            nc.tensor.matmul(bank[7][:, 0:1], nbr[:], ones[0:E, 0:1], start=True, stop=True).then_inc(eb_done, 1)

        @block.scalar
        def _(act):
            for n in range(2 * TT):
                act.wait_ge(var1, n + 1)
                nc.scalar.activation(rstd[:, n:n + 1], mv[:, 1:2], ACT.Sqrt, bias=g["eps"][:, 0:1]).then_inc(std1, 1)
            for t in range(TT):
                act.wait_ge(logit, TT)
                nc.scalar.activation(sc[:, t], bank[2][:, t * E:(t + 1) * E], ACT.Sigmoid).then_inc(score, 1)
            for f in range(2):
                act.wait_ge(h_done, 2 * f + 1)
                nc.scalar.activation(hs[:, f], bank[4 + 2 * f][:], ACT.Silu).then_inc(sh_silu, 1)
            for n in range(2 * TT):
                act.wait_ge(y_done, n + 1)
                nc.scalar.activation(yo[:, n // 2, (n % 2) * 512:(n % 2 + 1) * 512], bank[n % 2][:], ACT.Copy) \
                   .then_inc(y_read, 1)

        @block.vector
        def _(v):
            ch = Chain(v, dve)
            v.wait_ge(rows_in, 80)
            ch.mark(nc.vector.tensor_scalar(rows[:, 0], rows[:, 0], 1.0, None, ALU.add))
            ch(nc.vector.tensor_scalar(rows[:, 3], rows[:, 3], 1.0, None, ALU.add))
            v.wait_ge(x_in, 16)

            def norm(src, dst, n):
                for h in range(2):
                    ch.mark(nc.vector.bn_stats(st[:, h], src[:, h * 512:(h + 1) * 512]))
                ch.wait()
                nc.vector.bn_aggr(mv[:], st[:]).then_inc(var1, 1)
                v.wait_ge(std1, n + 1)
                ch(nc.vector.reciprocal(rstd[:, n:n + 1], rstd[:, n:n + 1]))
                return nc.vector.tensor_scalar(dst, src, mv[:, 0:1], rstd[:, n:n + 1], ALU.subtract, ALU.mult)

            for t in range(TT):
                v.wait_ge(mixed, t + 1)
                for h in range(2):
                    hs_ = slice(h * 512, (h + 1) * 512)
                    nc.vector.tensor_tensor(tmp[:, hs_], bank[2 * t + h][:], rows[:, 0, hs_], ALU.mult).then_inc(mix_read, 1)
                v.wait_ge(mix_read, 2 * t + 2)
                ch(nc.vector.scalar_tensor_tensor(xs[:, t], xs[:, t], ALPHA, tmp[:], ALU.mult, ALU.add))
                ch(norm(xs[:, t], tmp[:], 2 * t))
                ch(nc.vector.tensor_tensor(tmp[:], tmp[:], rows[:, 1], ALU.mult))
                ch(nc.vector.tensor_tensor(g["x1"][:, t], tmp[:], rows[:, 2], ALU.add))
                if t >= 2:
                    v.wait_ge(u2_ready, t - 1)
                norm(g["x1"][:, t], u2n[:, t % 2], 2 * t + 1).then_inc(u2_normed, 1)
            for n in range(2 * TT):
                t, h = n // 2, n % 2
                v.wait_ge(tp_done, n + 1)
                nc.vector.tensor_copy(u2T[:, 4 * h:4 * h + 4, t * P:(t + 1) * P],
                                      bank[n % 2][:].rearrange("p (k t) -> p k t", k=4)).then_inc(tp_read, 1)
            v.wait_ge(rt_in, 32)
            v.wait_ge(consts, N_CONSTS)
            for t in range(TT):
                v.wait_ge(score, t + 1)
                ch(nc.vector.tensor_tensor(sel[:, t], sc[:, t], rb[:], ALU.add))
                for q in range(GROUPS):
                    ch.mark(nc.vector.max(m8[:, t, q], sel[:, t, q * PER_GROUP:(q + 1) * PER_GROUP]))
                ch.wait()
                ch(nc.vector.tensor_tensor(gsx[:, t, 4:12], m8[:, t, :, 0], m8[:, t, :, 1], ALU.add))
                ch(nc.vector.max(t8[:, t], gsx[:, t]))
                ch(nc.vector.match_replace(gr[:, t], t8[:, t], gsx[:, t], -BIG))
                ch(nc.vector.tensor_scalar(gr[:, t], gr[:, t], -BIG / 2, -BIG, ALU.is_gt, ALU.mult))
                gv = gr[:, t, 4:12].unsqueeze(2).broadcast_to([P, GROUPS, PER_GROUP])
                ch(nc.vector.tensor_tensor(sel[:, t].rearrange("p (q n) -> p q n", q=GROUPS),
                                           sel[:, t].rearrange("p (q n) -> p q n", q=GROUPS), gv, ALU.add))
                ch(nc.vector.max(t8[:, t], sel[:, t]))
                ch(nc.vector.match_replace(er[:, t], t8[:, t], sel[:, t], -3e38))
                ch(nc.vector.tensor_scalar(A[:, t], er[:, t], -2e38, None, ALU.is_lt))
                v.sem_inc(a_ready, 1)
                ch(nc.vector.tensor_tensor(wgt[:, t], sc[:, t], A[:, t], ALU.mult))
                ch(nc.vector.tensor_reduce(ws[:, t:t + 1], wgt[:, t], AX_X, ALU.add))
                ch(nc.vector.reciprocal(ws[:, t:t + 1], ws[:, t:t + 1]))
                ch(nc.vector.tensor_scalar(g["pg"][:, :, t, 1], wgt[:, t], ws[:, t:t + 1], ROUTED_SCALE, ALU.mult, ALU.mult))
                if t < 2:
                    v.wait_ge(h_done, 2 * t + 2)
                    v.wait_ge(sh_silu, t + 1)
                    nc.vector.tensor_tensor(hT[:, t], hs[:, t], bank[5 + 2 * t][:], ALU.mult).then_inc(up_read, 1)
            for t in range(TT):
                v.wait_ge(pos_done, TT)
                nc.vector.scalar_tensor_tensor(g["pg"][:, :, t, 0], bank[3][:, t * E:(t + 1) * E], 1.0, A[:, t],
                                               ALU.add, ALU.mult).then_inc(pos_read, 1)
            v.wait_ge(cnt_done, 1)
            for j in range(4):
                ch.mark(nc.vector.tensor_scalar(cnt[:, j:j + 1], bank[2][0:E, 0:1], float(P * j), None, ALU.is_gt))
            ch.wait()
            ch(nc.vector.tensor_reduce(nb[:], cnt[:], AX_X, ALU.add))
            v.sem_inc(nb_ready, 1)
            v.wait_ge(ci_done, 1)
            ch(nc.vector.tensor_copy(ci[:], bank[4][0:E, 0:1]))
            ch.mark(nc.vector.tensor_scalar(M[:], iob[:], ci[:], None, ALU.is_ge))
            ch(nc.vector.tensor_scalar(nbr[:], ones[0:E], nb[:], None, ALU.mult))
            v.sem_inc(m_ready, 1)
            v.wait_ge(eb_done, 1)
            ch.mark(nc.vector.tensor_scalar(g["table"][0:1, 0:NBT], bank[5][0:1, 0:NBT], float(E - 1), None, ALU.min))
            ch.mark(nc.vector.tensor_copy(g["table"][0:1, NBT:NBT + 1], bank[7][0:1, 0:1]))
            ch(nc.vector.tensor_copy(g["c0"][:], bank[6][:, 0:NBT]))
            ch(nc.vector.tensor_tensor(g["c0"][:], g["place"][:, 0, 0:NBT], g["c0"][:], ALU.subtract))
            ch(nc.vector.tensor_scalar(g["c0"][:], g["c0"][:], float(P), -float(P), ALU.mult, ALU.add))


def moe(nc, g, exp_gate, exp_up, exp_down, ln2_w, ln2_b):
    with ExitStack() as ctx:
        s = Scope(nc, ctx, "moe")
        wg = [s.sb(f"wg{p}", [P, KC, 2, F_EXP]) for p in range(SLOTS)]
        wd = [s.sb(f"wd{p}", [P, 2, D]) for p in range(SLOTS)]
        xg = [s.sb(f"xg{p}", [P, D]) for p in range(SLOTS)]
        xT = s.sb("xT", [P, KC, P])
        S_ = s.sb("S", [P, TT, P])
        pos = s.sb("pos", [P, TT])
        hs, hm = s.sb("hs", [P, F_EXP]), s.sb("hm", [P, F_EXP])
        hT = s.sb("hT", [P, 2, P])
        y = [s.sb(f"y{p}", [P, D]) for p in range(SLOTS)]
        val = s.sb("val", [P, 2])
        occ = s.sb("occ", [P, 1])
        row = s.sb("row", [P, 1])
        idx = [s.sb(f"idx{p}", [P, 1], I32) for p in range(SLOTS)]
        sidx = [s.sb(f"sidx{p}", [P, 1], I32) for p in range(SLOTS)]
        gcol = [s.sb(f"gcol{p}", [P, 1]) for p in range(SLOTS)]
        fetch = s.sb("fetch", [P, 1])
        pH = s.ps("pH")
        pX = [s.ps(f"pX{h}") for h in range(2)]
        pY = [s.ps(f"pY{h}") for h in range(2)]
        pT, pI = s.ps("pT"), s.ps("pI")
        wg_in = [s.sem(f"wg_in{p}") for p in range(SLOTS)]
        wu_in = [s.sem(f"wu_in{p}") for p in range(SLOTS)]
        wd_in = [s.sem(f"wd_in{p}") for p in range(SLOTS)]
        gathered = [s.sem(f"gathered{p}") for p in range(SLOTS)]
        h_done = [s.sem(f"h_done{p}") for p in range(SLOTS)]
        d_done = [s.sem(f"d_done{p}") for p in range(SLOTS)]
        (s_built, i_done, i_ready, x_zero, x_turned, x_read, silu_done, hm_done, h_turned, h_read,
         y0_read, y1_read, dch, held) = (s.sem(n) for n in (
             "s_built i_done i_ready x_zero x_turned x_read silu_done hm_done h_turned h_read "
             "y0_read y1_read dch held").split())
        y_free = [s.sem(f"y_free{p}") for p in range(SLOTS)]
        added = s.sem("added")
        rows_in = s.sem("rows_in")
        block = ctx.enter_context(nc.Block())

        def blocks(eng, body):
            n_blocks = eng.value_load(g["table"][0:1, NBT:NBT + 1], min_val=1, max_val=MAX_BLOCKS)
            with eng.Fori(0, TRIPS) as i:
                with eng.If(SLOTS * i < n_blocks):
                    body(SLOTS * i, 0, i)
                    for p in range(1, SLOTS):
                        with eng.If(SLOTS * i + p < n_blocks):
                            body(SLOTS * i + p, p, i)
            return n_blocks

        def expert(eng, b):
            return bass.ds(eng.value_load(g["table"][0:1, bass.ds(b, 1)], min_val=0, max_val=E - 1), 1)

        @block.sync
        def _(sp):
            def body(b, p, i):
                e = expert(sp, b)
                if p > 0:
                    sp.wait_ge(i_ready, AHEAD)
                sp.wait_ge(h_done[p], i + 1)
                sp.dma_start(wg[p][:, :, 0], exp_gate[0, e].rearrange("a (p k) f -> p (a k) f", p=P)).then_inc(wg_in[p], 16)
                sp.dma_start(wg[p][:, :, 1], exp_up[0, e].rearrange("a (p k) f -> p (a k) f", p=P)).then_inc(wu_in[p], 16)
                sp.wait_ge(d_done[p], 2 * i + 1)
                sp.dma_start(wd[p][:], exp_down[0, e].rearrange("a (p c) d -> p (a c) d", p=P)).then_inc(wd_in[p], 16)
            for n, vec in enumerate((g["mod"][0][5 * D:6 * D], ln2_w[0], ln2_b[0])):
                sp.dma_start(g["last_rows"][:, n], row_of(vec)).then_inc(rows_in, 16)
            blocks(sp, body)
            sp.wait_ge(rows_in, 48)

        @block.gpsimd
        def _(pool):
            def gather(b, q):
                hold(pool, i_ready, b + 1, held)
                pool.indirect_dma_start(out=xg[q][:], out_offset=None, in_=g["u2d"][:],
                                        in_offset=bass.IndirectOffsetOnAxis(ap=idx[q][:, 0:1], axis=0),
                                        bounds_check=ROWS - 1, oob_is_err=False).then_inc(gathered[q], 16)

            for q in range(SLOTS):
                nc.gpsimd.memset(xg[q][:], 0.0).then_inc(x_zero, 1)
            pool.wait_ge(x_zero, SLOTS)
            for q in range(AHEAD):
                gather(q, q)

            def body(b, p, i):
                hold(pool, x_turned, 2 * b + 2, held)
                gather(b + AHEAD, (p + AHEAD) % SLOTS)
                hold(pool, y0_read, b + 2, held)
                hold(pool, y1_read, b + 2, held)
                pool.indirect_dma_start(out=g["acc"][:], out_offset=bass.IndirectOffsetOnAxis(ap=sidx[p][:, 0:1], axis=0),
                                        in_=y[p][:], in_offset=None, bounds_check=ROWS - 1, compute_op=ALU.add) \
                    .then_inc(added, 16)
                hold(pool, added, 16 * (b + 1), held)
                pool.sem_inc(y_free[p], 1)
            n = blocks(pool, body)
            for q in range(SLOTS):
                pool.wait_ge(gathered[q], 16 * ((n + AHEAD + SLOTS - 1 - q) // SLOTS))

        @block.tensor
        def _(pe):
            def indices(b, q):
                pe.wait_ge(s_built, b + 1)
                for t in range(TT):
                    ins = nc.tensor.matmul(pI[:, 2 * q:2 * q + 2], S_[:, t], g["rhs"][:, q, t], start=(t == 0), stop=(t == TT - 1))
                ins.then_inc(i_done, 1)

            def turn_x(b, q, n, h, first=False):
                pe.wait_ge(gathered[q], 16 * (n + 1))
                if not first:
                    pe.wait_ge(x_read, 2 * b + h - 1)
                x3 = xg[q][:].rearrange("t (p k) -> t k p", k=KC)
                for k in range(4):
                    ins = nc.tensor.transpose(pX[h][:, k * P:(k + 1) * P], x3[:, 4 * h + k], g["ident"][:])
                ins.then_inc(x_turned, 1)

            for sem in (*h_done, *d_done, *y_free, y0_read, y1_read):
                pe.sem_inc(sem, 1)
            for q in range(AHEAD):
                indices(q, q)
            for h in range(2):
                turn_x(0, 0, 0, h, first=True)
            hm3 = hm[:].rearrange("t (p c) -> t c p", c=2)

            def body(b, p, i):
                pe.wait_ge(x_read, 2 * b + 2)
                pe.wait_ge(wg_in[p], 16 * (i + 1))
                pe.wait_ge(wu_in[p], 16 * (i + 1))
                for k in range(KC):
                    ins = nc.tensor.matmul(pH[:], xT[:, k], wg[p][:, k].rearrange("p w f -> p (w f)"),
                                           start=(k == 0), stop=(k == KC - 1))
                ins.then_inc(h_done[p], 1)
                after = (p + 1) % SLOTS, i + (p + 1) // SLOTS
                turn_x(b + 1, *after, 0)
                turn_x(b + 1, *after, 1)
                pe.wait_ge(hm_done, b + 1)
                for f in range(2):
                    ins = nc.tensor.transpose(pT[:, f * P:(f + 1) * P], hm3[:, f], g["ident"][:])
                ins.then_inc(h_turned, 1)
                indices(b + AHEAD, (p + AHEAD) % SLOTS)
                pe.wait_ge(h_read, b + 1)
                pe.wait_ge(wd_in[p], 16 * (i + 1))
                for h, used in ((0, y0_read), (1, y1_read)):
                    pe.wait_ge(used, b + 1)
                    for f in range(2):
                        ins = nc.tensor.matmul(pY[h][:], hT[:, f], wd[p][:, f, h * 512:(h + 1) * 512], start=(f == 0), stop=(f == 1))
                    ins.then_inc(d_done[p], 1)
            blocks(pe, body)

        @block.scalar
        def _(act):
            def read_x(b, h):
                act.wait_ge(x_turned, 2 * b + h + 1)
                nc.scalar.activation(xT[:, 4 * h:4 * h + 4], pX[h][:].rearrange("p (k t) -> p k t", k=4), ACT.Copy) \
                   .then_inc(x_read, 1)
            for h in range(2):
                read_x(0, h)

            def body(b, p, i):
                act.wait_ge(h_done[p], i + 2)
                nc.scalar.activation(hs[:], pH[:, 0:F_EXP], ACT.Silu).then_inc(silu_done, 1)
                read_x(b + 1, 0)
                read_x(b + 1, 1)
                act.wait_ge(h_turned, b + 1)
                nc.scalar.activation(hT[:], pT[:, 0:2 * P].rearrange("p (f t) -> p f t", f=2), ACT.Copy).then_inc(h_read, 1)
                act.wait_ge(d_done[p], 2 * i + 2)
                act.wait_ge(i_ready, b + 1)
                act.wait_ge(y_free[p], i + 1)
                nc.scalar.activation(y[p][:, 0:512], pY[0][:], ACT.Copy, scale=gcol[p][:, 0:1]).then_inc(y0_read, 1)
            blocks(act, body)

        @block.vector
        def _(v):
            ch = Chain(v, dch)

            def match(b, q):
                e = expert(v, b)
                ch.mark(nc.vector.tensor_copy(g["rhs"][:, q, :, 1], g["pg"][:, e, :, 1].rearrange("p a t -> p (a t)")))
                ch(nc.vector.tensor_scalar(pos[:], g["pg"][:, e, :, 0].rearrange("p a t -> p (a t)"),
                                           g["c0"][:, bass.ds(b, 1)], None, ALU.subtract))
                nc.vector.tensor_tensor(S_[:], g["place"][:], pos[:].unsqueeze(2).broadcast_to([P, TT, P]),
                                        ALU.is_equal).then_inc(s_built, 1)

            def rows(b, q):
                v.wait_ge(i_done, b + 1)
                ch(nc.vector.tensor_copy(val[:], pI[:, 2 * q:2 * q + 2]))
                ch.mark(nc.vector.tensor_copy(gcol[q][:], val[:, 1:2]))
                ch.mark(nc.vector.tensor_scalar(fetch[:], val[:, 0:1], 0.5, float(NO_ROW), ALU.is_lt, ALU.mult))
                ch(nc.vector.tensor_scalar(occ[:], val[:, 0:1], 1.0, None, ALU.min))
                ch.mark(nc.vector.scalar_tensor_tensor(row[:], occ[:], g["spare"][:, 1:2], val[:, 0:1], ALU.mult, ALU.add))
                nc.vector.scalar_tensor_tensor(idx[q][:], val[:, 0:1], -1.0, fetch[:], ALU.add, ALU.add).then_inc(i_ready, 1)
                ch.wait()
                ch(nc.vector.tensor_tensor(sidx[q][:], row[:], g["spare"][:, 0:1], ALU.add))

            for b in range(AHEAD):
                match(b, b)
                rows(b, b)

            def body(b, p, i):
                ch.enter(b, 8)
                q = (p + AHEAD) % SLOTS
                match(b + AHEAD, q)
                v.wait_ge(silu_done, b + 1)
                nc.vector.tensor_tensor(hm[:], hs[:], pH[:, F_EXP:2 * F_EXP], ALU.mult).then_inc(hm_done, 1)
                v.wait_ge(y_free[q], i + 1 + (p + AHEAD) // SLOTS)
                rows(b + AHEAD, q)
                v.wait_ge(d_done[p], 2 * i + 3)
                nc.vector.tensor_scalar(y[p][:, 512:D], pY[1][:], gcol[p][:, 0:1], None, ALU.mult).then_inc(y1_read, 1)
                assert ch.n - ch.start == ch.length, ch.n - ch.start
                ch.n = ch.start
            blocks(v, body)
            v.wait_ge(rows_in, 48)
            nc.vector.tensor_scalar(g["last_rows"][:, 0], g["last_rows"][:, 0], 1.0, None, ALU.add)


def last_norm(nc, g, out):
    with ExitStack() as ctx:
        s = Scope(nc, ctx, "last")
        rows = g["last_rows"]
        acc = s.sb("acc", [P, TT, D])
        st = s.sb("st", [P, TT, 2, 6])
        mv = s.sb("mv", [P, TT, 2])
        rstd = s.sb("rstd", [P, TT])
        normed, scaled, last_ready, var_done, std_done, out_ready, stored, dve = (s.sem(n) for n in (
            "normed scaled last_ready var_done std_done out_ready stored dve").split())
        acc_in = [s.sem(f"acc_in{t}") for t in range(TT)]
        block = ctx.enter_context(nc.Block())

        @block.sync
        def _(sp):
            for t in range(TT):
                sp.dma_start(acc[:, t], g["acc"][t * P:(t + 1) * P]).then_inc(acc_in[t], 16)
            for t in range(TT):
                if t < TT - 1:
                    sp.wait_ge(out_ready, t + 1)
                else:
                    sp.wait_ge(last_ready, 1)
                sp.dma_start(out[0, t * P:(t + 1) * P], acc[:, t]).then_inc(stored, 16)
            sp.wait_ge(stored, 16 * TT)

        @block.scalar
        def _(act):
            for t in range(TT):
                act.wait_ge(var_done, t + 1)
                nc.scalar.activation(rstd[:, t:t + 1], mv[:, t, 1:2], ACT.Sqrt, bias=g["eps"][:, 0:1]).then_inc(std_done, 1)

        @block.vector
        def _(v):
            ch = Chain(v, dve)
            for t in range(TT):
                v.wait_ge(acc_in[t], 16)
                ch(nc.vector.tensor_tensor(acc[:, t], acc[:, t], rows[:, 0], ALU.mult))
                ch(nc.vector.scalar_tensor_tensor(acc[:, t], g["x1"][:, t], ALPHA, acc[:, t], ALU.mult, ALU.add))
                for h in range(2):
                    ch.mark(nc.vector.bn_stats(st[:, t, h], acc[:, t, h * 512:(h + 1) * 512]))
                ch.wait()
                nc.vector.bn_aggr(mv[:, t], st[:, t]).then_inc(var_done, 1)
                v.wait_ge(std_done, t + 1)
                ch(nc.vector.reciprocal(rstd[:, t:t + 1], rstd[:, t:t + 1]))
                nc.vector.tensor_scalar(acc[:, t], acc[:, t], mv[:, t, 0:1], rstd[:, t:t + 1], ALU.subtract, ALU.mult) \
                  .then_inc(normed, 1)
            v.wait_ge(normed, TT)
            t = TT - 1
            ch(nc.vector.tensor_tensor(acc[:, t], acc[:, t], rows[:, 1], ALU.mult))
            nc.vector.tensor_tensor(acc[:, t], acc[:, t], rows[:, 2], ALU.add).then_inc(last_ready, 1)

        @block.gpsimd
        def _(pool):
            for t in range(TT - 1):
                pool.wait_ge(normed, t + 1)
                nc.gpsimd.tensor_tensor(acc[:, t], acc[:, t], rows[:, 1], ALU.mult).then_inc(scaled, 1)
                pool.wait_ge(scaled, t + 1)
                nc.gpsimd.tensor_tensor(acc[:, t], acc[:, t], rows[:, 2], ALU.add).then_inc(out_ready, 1)


_INS = """x c ada_w ada_b w_in shift_mu w0 w_up a0 a_up g_up k_k k_a r_k lnx_w lnx_b conv_w conv_b cnorm_w
cnorm_b cpw_w cpw_b gate_b w_o ln1_w ln1_b router_w router_b exp_gate exp_up exp_down sh_gate sh_up sh_down
ln2_w ln2_b""".split()


def hybrid_encoder_layer(nc, a, out):
    with ExitStack() as ctx:
        ctx.enter_context(nc.allow_non_contiguous_dma("columns of parameters"))

        def sb(name, shape, dt=F32):
            return ctx.enter_context(nc.sbuf_tensor(name, shape, dt))

        g = {
            "u1T": sb("u1T", [P, KC, T]),
            "ident": sb("ident", [P, P]),
            "mean1024": sb("mean1024", [P, P]),
            "eps": sb("eps", [P, 2]),
            "csil": sb("csil", [P, KC]),
        }
        for name, shape in (("mod", (1, MODS * D)), ("rkv", (3, KC, P, T)), ("lora", (3, P, T)), ("gate", (2, KC, P, T)),
                            ("yb", (KC, P, T)), ("u2d", (ROWS, D)), ("acc", (ROWS, D))):
            g[name] = nc.dram_tensor(f"scratch_{name}", shape, F32, kind="Internal").ap()
        with ExitStack() as until_scan:
            for name, shape in MASKS.items():
                g[name] = until_scan.enter_context(nc.sbuf_tensor(name, [P, *shape], F32))
            constants(nc, g)
            modulation_and_norm(nc, g, a["x"], a["c"], a["ada_w"], a["ada_b"])
            projections_and_conv(nc, g, *[a[n] for n in (
                "ada_w", "ada_b", "w_in", "shift_mu", "conv_w", "conv_b", "cnorm_w", "cnorm_b", "cpw_w", "cpw_b", "gate_b")])
            rwkv(nc, g, *[a[n] for n in ("w0", "w_up", "a0", "a_up", "g_up", "k_k", "k_a", "r_k", "lnx_w", "lnx_b")])
        g["x1"] = sb("x1", [P, TT, D])
        g["pg"] = sb("pg", [P, E, TT, 2])
        g["place"] = sb("place", [P, TT, P])
        g["rhs"] = sb("rhs", [P, SLOTS, TT, 2])
        g["spare"] = sb("spare", [P, 2])
        g["table"] = sb("table", [1, NBT + 2], I32)
        g["c0"] = sb("c0", [P, NBT])
        mix_and_route(nc, g, *[a[n] for n in ("x", "w_o", "ln1_w", "ln1_b", "router_w", "router_b",
                                              "sh_gate", "sh_up", "sh_down")])
        g["last_rows"] = sb("last_rows", [P, 3, D])
        moe(nc, g, *[a[n] for n in ("exp_gate", "exp_up", "exp_down", "ln2_w", "ln2_b")])
        last_norm(nc, g, out)


def kernel(**inputs):
    import numpy as _np
    import concourse.bacc as _bacc
    from concourse.bass_utils import run_bass_kernel_spmd as _run

    nc = _bacc.Bacc("TRN2", target_bir_lowering=False, num_devices=1)
    arrays, args = {}, {}
    for name in _INS:
        arr = _np.ascontiguousarray(inputs[name])
        arrays[f"in_{name}"] = arr
        args[name] = nc.dram_tensor(f"in_{name}", arr.shape, mybir.dt.from_np(arr.dtype), kind="ExternalInput").ap()
    out = nc.dram_tensor("out", (1, T, D), F32, kind="ExternalOutput").ap()
    hybrid_encoder_layer(nc, args, out)
    r = _run(nc, [arrays], core_ids=[0])
    return r.results[0]["out"]
```
